# Optimizing a Trainium2 kernel written in Bass

```python
import math
import jax, jax.numpy as jnp
from jax import lax
import numpy as np

D_MODEL = 1024
BATCH = 1
SEQ = 256
DEPTH = 1

ATT_HEADS = 8
HEAD_DIM = 64
ATT_WIDTH = ATT_HEADS * HEAD_DIM
MOBA_BLOCK = 256
MOBA_TOPK = 3
MOBA_QCHUNK = 32
REL_BUCKETS = 32
REL_MAX_DIST = 128
SSM_WIDTH = D_MODEL // 2
SSM_GROUP = 16
SSM_GROUPS = SSM_WIDTH // SSM_GROUP
SSM_STATE = 64
DT_MIN = 1e-3
DT_MAX = 1e-1
N_BRANCH = 2
IN_WIDTH = 3 * ATT_WIDTH + SSM_WIDTH + N_BRANCH * D_MODEL
N_EXPERTS = 32
TOP_K = 4
D_FF = D_MODEL
SWIGLU_ALPHA = 1.702
SWIGLU_LIMIT = 7.0
MOE_BLOCK = 256
RMS_EPS = 1e-6
N_MOD = 6

kernel_name = "hybrid_s5_moba_moe_adaln_block"

def rms_norm(x, g):
    xf = x.astype(jnp.float32)
    y = xf * lax.rsqrt(jnp.mean(xf * xf, axis=-1, keepdims=True) + RMS_EPS)
    return (y * g.astype(jnp.float32)).astype(x.dtype)

def rel_bucket(dist):
    n = jnp.maximum(dist, 0)
    max_exact = REL_BUCKETS // 2
    nf = jnp.maximum(n, 1).astype(jnp.float32)
    large = max_exact + (jnp.log(nf / max_exact) / math.log(REL_MAX_DIST / max_exact)
                         * (REL_BUCKETS - max_exact)).astype(jnp.int32)
    large = jnp.minimum(large, REL_BUCKETS - 1)
    return jnp.where(n < max_exact, n, large)

def s5_ssm(u, a_re, a_im, log_dt, b_re, b_im, c_re, c_im, d_skip):
    bsz, s, _ = u.shape
    f32 = jnp.float32
    uf = u.astype(f32).reshape(bsz, s, SSM_GROUPS, SSM_GROUP)
    lam_re = jnp.minimum(a_re.astype(f32), -1e-4)
    lam_im = a_im.astype(f32)
    dt = jnp.exp(log_dt.astype(f32))[:, None]
    mag = jnp.exp(lam_re * dt)
    lb_re = mag * jnp.cos(lam_im * dt)
    lb_im = mag * jnp.sin(lam_im * dt)
    n_re = lb_re - 1.0
    n_im = lb_im
    den = lam_re * lam_re + lam_im * lam_im
    z_re = ((n_re * lam_re + n_im * lam_im) / den)[..., None]
    z_im = ((n_im * lam_re - n_re * lam_im) / den)[..., None]
    br = b_re.astype(f32)
    bi = b_im.astype(f32)
    bb_re = z_re * br - z_im * bi
    bb_im = z_re * bi + z_im * br
    bu_re = jnp.einsum('bsgc,gpc->bsgp', uf, bb_re)
    bu_im = jnp.einsum('bsgc,gpc->bsgp', uf, bb_im)
    a_re_s = jnp.broadcast_to(lb_re, (1, s, SSM_GROUPS, SSM_STATE))
    a_im_s = jnp.broadcast_to(lb_im, (1, s, SSM_GROUPS, SSM_STATE))

    def combine(e1, e2):
        ar1, ai1, br1, bi1 = e1
        ar2, ai2, br2, bi2 = e2
        return (ar2 * ar1 - ai2 * ai1,
                ar2 * ai1 + ai2 * ar1,
                ar2 * br1 - ai2 * bi1 + br2,
                ar2 * bi1 + ai2 * br1 + bi2)

    _, _, x_re, x_im = lax.associative_scan(combine, (a_re_s, a_im_s, bu_re, bu_im), axis=1)
    y = (jnp.einsum('bsgp,gcp->bsgc', x_re, c_re.astype(f32))
         - jnp.einsum('bsgp,gcp->bsgc', x_im, c_im.astype(f32)))
    y = y.reshape(bsz, s, SSM_WIDTH) + d_skip.astype(f32) * uf.reshape(bsz, s, SSM_WIDTH)
    return y.astype(u.dtype)

def moba_attention(q, k, v, rel_bias):
    bsz, s, h, hd = q.shape
    f32 = jnp.float32
    nb = -(-s // MOBA_BLOCK)
    sp = nb * MOBA_BLOCK
    pad = ((0, 0), (0, sp - s), (0, 0), (0, 0))
    qh = jnp.pad(q, pad).transpose(0, 2, 1, 3) * (hd ** -0.5)
    kb = jnp.pad(k, pad).transpose(0, 2, 1, 3).reshape(bsz, h, nb, MOBA_BLOCK, hd)
    vb = jnp.pad(v, pad).transpose(0, 2, 1, 3).reshape(bsz, h, nb, MOBA_BLOCK, hd)
    k_mean = jnp.mean(kb.astype(f32), axis=3)
    gate = jnp.einsum('bhsd,bhnd->bhsn', qh.astype(f32), k_mean)
    q_blk = jnp.arange(sp) // MOBA_BLOCK
    gate = jnp.where(jnp.arange(nb)[None, :] < q_blk[:, None], gate, -jnp.inf)
    n_sel = min(MOBA_TOPK, nb)
    _, sel = lax.top_k(gate, n_sel)
    n_chunks = sp // MOBA_QCHUNK
    q_c = qh.reshape(bsz, h, n_chunks, MOBA_QCHUNK, hd).transpose(2, 0, 1, 3, 4)
    sel_c = sel.reshape(bsz, h, n_chunks, MOBA_QCHUNK, n_sel).transpose(2, 0, 1, 3, 4)
    b_ix = jnp.arange(bsz)[:, None, None, None]
    h_ix = jnp.arange(h)[None, :, None, None]
    h_ix5 = jnp.arange(h)[None, :, None, None, None]
    offs = jnp.arange(MOBA_BLOCK)

    def chunk(args):
        ci, qc, sc = args
        q_pos = ci * MOBA_QCHUNK + jnp.arange(MOBA_QCHUNK)
        own = (ci * MOBA_QCHUNK) // MOBA_BLOCK
        k_sel = kb[b_ix, h_ix, sc]
        v_sel = vb[b_ix, h_ix, sc]
        s_sel = jnp.einsum('bhqd,bhqnjd->bhqnj', qc, k_sel).astype(f32)
        kpos = sc[..., None] * MOBA_BLOCK + offs
        bias_sel = rel_bias[rel_bucket(q_pos[:, None, None] - kpos), h_ix5]
        s_sel = jnp.where((sc < own)[..., None], s_sel + bias_sel, -jnp.inf)
        k_own = lax.dynamic_index_in_dim(kb, own, axis=2, keepdims=False)
        v_own = lax.dynamic_index_in_dim(vb, own, axis=2, keepdims=False)
        kpos_own = own * MOBA_BLOCK + offs
        bias_own = rel_bias[rel_bucket(q_pos[:, None] - kpos_own[None, :])].transpose(2, 0, 1)
        s_own = jnp.einsum('bhqd,bhjd->bhqj', qc, k_own).astype(f32) + bias_own
        s_own = jnp.where(kpos_own[None, :] <= q_pos[:, None], s_own, -jnp.inf)
        logits = jnp.concatenate(
            [s_sel.reshape(bsz, h, MOBA_QCHUNK, n_sel * MOBA_BLOCK), s_own], axis=-1)
        p = jax.nn.softmax(logits, axis=-1)
        p_sel = p[..., :n_sel * MOBA_BLOCK].reshape(bsz, h, MOBA_QCHUNK, n_sel, MOBA_BLOCK)
        p_own = p[..., n_sel * MOBA_BLOCK:]
        out = (jnp.einsum('bhqnj,bhqnjd->bhqd', p_sel.astype(v_sel.dtype), v_sel)
               + jnp.einsum('bhqj,bhjd->bhqd', p_own.astype(v_own.dtype), v_own))
        return out

    out = lax.map(chunk, (jnp.arange(n_chunks), q_c, sel_c))
    out = out.transpose(1, 0, 3, 2, 4).reshape(bsz, sp, h, hd)
    return out[:, :s]

def hybrid_mixer(h, rel_bias, w_in, a_re, a_im, log_dt, b_re, b_im, c_re, c_im, d_skip,
                 w_glu, w_ssm_out, w_att_out, w_out):
    bsz, s, d = h.shape
    proj = h @ w_in
    q, k, v, u, g_att, g_ssm = jnp.split(
        proj, [ATT_WIDTH, 2 * ATT_WIDTH, 3 * ATT_WIDTH, 3 * ATT_WIDTH + SSM_WIDTH,
               3 * ATT_WIDTH + SSM_WIDTH + D_MODEL], axis=-1)
    heads = (bsz, s, ATT_HEADS, HEAD_DIM)
    att = moba_attention(q.reshape(heads), k.reshape(heads), v.reshape(heads), rel_bias)
    att = att.reshape(bsz, s, ATT_WIDTH) @ w_att_out
    y = jax.nn.gelu(s5_ssm(u, a_re, a_im, log_dt, b_re, b_im, c_re, c_im, d_skip))
    glu_v, glu_g = jnp.split(y @ w_glu, 2, axis=-1)
    ssm = (glu_v * jax.nn.sigmoid(glu_g)) @ w_ssm_out
    merged = jax.nn.sigmoid(g_att) * att + jax.nn.sigmoid(g_ssm) * ssm
    return merged @ w_out

def moe_ffn(h, w_router, b_router, w1, b1, w2, b2):
    bsz, s, d = h.shape
    t = bsz * s
    xt = h.reshape(t, d)
    logits = (xt @ w_router + b_router).astype(jnp.float32)
    top_val, top_idx = lax.top_k(logits, TOP_K)
    gates = jax.nn.softmax(top_val, axis=-1)
    tk = t * TOP_K
    e_flat = top_idx.reshape(tk)
    tok_flat = jnp.arange(tk, dtype=jnp.int32) // TOP_K
    w_flat = gates.reshape(tk)
    order = jnp.argsort(e_flat)
    e_sorted = e_flat[order]
    tok_sorted = tok_flat[order]
    w_sorted = w_flat[order]
    counts = jnp.bincount(e_flat, length=N_EXPERTS)
    starts = jnp.cumsum(counts) - counts
    padded = (counts + MOE_BLOCK - 1) // MOE_BLOCK * MOE_BLOCK
    pad_ends = jnp.cumsum(padded)
    pad_starts = pad_ends - padded
    dest = pad_starts[e_sorted] + (jnp.arange(tk) - starts[e_sorted])
    n_blocks = tk // MOE_BLOCK + N_EXPERTS
    p_rows = n_blocks * MOE_BLOCK
    buf_tok = jnp.zeros((p_rows,), jnp.int32).at[dest].set(tok_sorted)
    buf_w = jnp.zeros((p_rows,), jnp.float32).at[dest].set(w_sorted)
    block_e = jnp.minimum(
        jnp.searchsorted(pad_ends, jnp.arange(n_blocks) * MOE_BLOCK, side='right'), N_EXPERTS - 1)
    xb = xt[buf_tok].reshape(n_blocks, MOE_BLOCK, d)

    def expert_block(args):
        xblk, e = args
        gu = xblk @ w1[e] + b1[e]
        g, up = gu[:, :D_FF], gu[:, D_FF:]
        g = jnp.minimum(g, SWIGLU_LIMIT)
        up = jnp.clip(up, -SWIGLU_LIMIT, SWIGLU_LIMIT)
        act = (up + 1.0) * g * jax.nn.sigmoid(SWIGLU_ALPHA * g)
        return act @ w2[e] + b2[e]

    yb = lax.map(expert_block, (xb, block_e)).reshape(p_rows, d)
    out = jnp.zeros((t, d), yb.dtype).at[buf_tok].add(yb * buf_w[:, None].astype(yb.dtype))
    return out.reshape(bsz, s, d)

def setup_inputs(seed: int = 0) -> dict:
    key = jax.random.key(seed)
    ks = iter(jax.random.split(key, 32))
    f32 = jnp.float32
    L, D, G, P, C = DEPTH, D_MODEL, SSM_GROUPS, SSM_STATE, SSM_GROUP

    def nrm(shape, scale):
        return jax.random.normal(next(ks), shape, f32) * scale

    return {
        "x": nrm((BATCH, SEQ, D), 1.0),
        "c": nrm((BATCH, D), 1.0),
        "rel_bias": nrm((REL_BUCKETS, ATT_HEADS), 0.5),
        "w_ada": nrm((L, D, N_MOD * D), 0.5 * D ** -0.5),
        "b_ada": nrm((L, N_MOD * D), 0.02),
        "g_pre_mix": 1.0 + nrm((L, D), 0.05),
        "g_post_mix": 1.0 + nrm((L, D), 0.05),
        "g_pre_ffn": 1.0 + nrm((L, D), 0.05),
        "g_post_ffn": 1.0 + nrm((L, D), 0.05),
        "w_in": nrm((L, D, IN_WIDTH), D ** -0.5),
        "ssm_a_re": -0.5 + nrm((L, G, P), 0.01),
        "ssm_a_im": math.pi * jnp.arange(P, dtype=f32)[None, None, :] + nrm((L, G, P), 0.01),
        "ssm_log_dt": jax.random.uniform(next(ks), (L, G), f32,
                                         minval=math.log(DT_MIN), maxval=math.log(DT_MAX)),
        "ssm_b_re": nrm((L, G, P, C), (2 * C) ** -0.5),
        "ssm_b_im": nrm((L, G, P, C), (2 * C) ** -0.5),
        "ssm_c_re": nrm((L, G, C, P), (2 * P) ** -0.5 * 4.0),
        "ssm_c_im": nrm((L, G, C, P), (2 * P) ** -0.5 * 4.0),
        "ssm_d": nrm((L, SSM_WIDTH), 1.0),
        "w_glu": nrm((L, SSM_WIDTH, 2 * SSM_WIDTH), SSM_WIDTH ** -0.5),
        "w_ssm_out": nrm((L, SSM_WIDTH, D), SSM_WIDTH ** -0.5),
        "w_att_out": nrm((L, ATT_WIDTH, D), ATT_WIDTH ** -0.5),
        "w_out": nrm((L, D, D), D ** -0.5),
        "w_router": nrm((L, D, N_EXPERTS), D ** -0.5),
        "b_router": nrm((L, N_EXPERTS), 0.01),
        "w_exp_in": nrm((L, N_EXPERTS, D, 2 * D_FF), D ** -0.5),
        "b_exp_in": nrm((L, N_EXPERTS, 2 * D_FF), 0.01),
        "w_exp_out": nrm((L, N_EXPERTS, D_FF, D), D_FF ** -0.5),
        "b_exp_out": nrm((L, N_EXPERTS, D), 0.01),
    }

def reference(x, c, rel_bias, w_ada, b_ada, g_pre_mix, g_post_mix, g_pre_ffn, g_post_ffn,
              w_in, ssm_a_re, ssm_a_im, ssm_log_dt, ssm_b_re, ssm_b_im, ssm_c_re, ssm_c_im,
              ssm_d, w_glu, w_ssm_out, w_att_out, w_out, w_router, b_router,
              w_exp_in, b_exp_in, w_exp_out, b_exp_out):
    cond = jax.nn.silu(c)
    for l in range(DEPTH):
        mod = cond @ w_ada[l] + b_ada[l]
        sh1, sc1, gt1, sh2, sc2, gt2 = [m[:, None, :] for m in jnp.split(mod, N_MOD, axis=-1)]
        h = rms_norm(x, g_pre_mix[l]) * (1.0 + sc1) + sh1
        y = hybrid_mixer(h, rel_bias, w_in[l], ssm_a_re[l], ssm_a_im[l], ssm_log_dt[l],
                         ssm_b_re[l], ssm_b_im[l], ssm_c_re[l], ssm_c_im[l], ssm_d[l],
                         w_glu[l], w_ssm_out[l], w_att_out[l], w_out[l])
        x = x + gt1 * rms_norm(y, g_post_mix[l])
        h = rms_norm(x, g_pre_ffn[l]) * (1.0 + sc2) + sh2
        y = moe_ffn(h, w_router[l], b_router[l], w_exp_in[l], b_exp_in[l],
                    w_exp_out[l], b_exp_out[l])
        x = x + gt2 * rms_norm(y, g_post_ffn[l])
    return x


_drawn_inputs = setup_inputs


def setup_inputs(seed=0):
    import zlib

    import numpy as np

    out = dict(_drawn_inputs(seed))
    spreads = {}
    factors = {'g_post_ffn': 4.236,
     'ssm_a_re': 6.972,
     'b_router': 4.014,
     'b_exp_in': 8.0,
     'b_exp_out': 8.0}
    for name, (base, spread) in spreads.items():
        noise = np.random.default_rng([zlib.crc32(name.encode()), seed]).standard_normal(out[name].shape)
        drawn = base * np.exp(spread * noise) if base else spread * noise
        out[name] = __import__('jax').numpy.asarray(drawn.astype(out[name].dtype))
    for name, factor in factors.items():
        out[name] = (out[name] * factor).astype(out[name].dtype)
    return out
```

```python
from contextlib import ExitStack
import math

import numpy as np

import concourse.bass as bass
from concourse import mybir

F32 = mybir.dt.float32
I32 = mybir.dt.int32
U32 = mybir.dt.uint32
ALU = mybir.AluOpType
ACT = mybir.ActivationFunctionType
AX = mybir.AxisListType.X

P = 128
D = 1024
T = 256
TT = T // P
KD = D // P
HEADS, HD = 8, 64
AW = HEADS * HD
SW = D // 2
KS = SW // P
GROUPS, GC, GP = 32, 16, 64
ST = GROUPS * GP // P
BUCKETS, MAX_DIST = 32, 128
NE, TOPK, FF = 32, 4, 1024
CAP = P
LIMIT, ALPHA = 7.0, 1.702
EPS = 1e-6
MASKED = -1.0e30
NOWHERE = 1000.0
GELU_C = math.sqrt(2.0 / math.pi)
ROUND = 12582912.0

C_ID, C_ONE, C_TRI, C_IOTA = 0, P, 2 * P, 3 * P
C_EVEN = 4 * P
C_ODD = C_EVEN + 1
C_HOT = C_ODD + 1
N_HOT = 2 * T - 1
C_N = C_HOT + N_HOT

MIX = (["sh1a", "sh1b", "sc1a", "sc1b", "u", "q", "k", "v", "ga0", "ga1",
        "gt1a", "gt1b", "sh2a", "sh2b", "sc2a", "sc2b", "gs0", "gs1", "glu", "ao", "so",
        "gt2a", "gt2b", "wo0", "wo1"])
ADA = ["sh1a", "sh1b", "sc1a", "sc1b", "gt1a", "gt1b", "sh2a", "sh2b", "sc2a", "sc2b", "gt2a", "gt2b"]
G_USERS = [n for n in ADA if n[:2] != "sh"]
ADA_COL = {n: 512 * (2 * ["sh1", "sc1", "gt1", "sh2", "sc2", "gt2"].index(n[:3]) + (n[3] == "b")) for n in ADA}
MIX_SLOTS = 4
SLOTS = 6
PW = 4096

FILLS = []
for name in MIX:
    if name in ADA:
        FILLS.append((name, 0, "dve"))
    elif name in ("glu", "ao"):
        FILLS += [(name, b, "act") for b in range(4)]
    elif name == "so":
        FILLS += [(name, b, "dve") for b in range(4)]
    else:
        FILLS += [(name, b, "act") for b in range(2)]
FILL = {(name, b): f for f, (name, b, _) in enumerate(FILLS)}


def used_up(n):
    return 1 + max(f for f, (name, _, _) in enumerate(FILLS) if name == MIX[n])


def emptied(f):
    who = FILLS[f][2]
    return who, sum(x[2] == who for x in FILLS[:f + 1])


def constants():
    c = np.zeros((P, C_N), np.float32)
    c[:, C_ID:C_ID + P] = np.eye(P)
    c[:, C_ONE:C_ONE + P] = 1.0
    c[:, C_TRI:C_TRI + P] = np.triu(np.ones((P, P)), 1)
    c[:, C_IOTA:C_IOTA + P] = np.arange(P)[None, :]
    exact = BUCKETS // 2
    for j in range(N_HOT):
        dist = T - 1 - j
        if dist < 0:
            c[BUCKETS, C_HOT + j] = 1.0
            continue
        large = exact + int(np.float32(np.log(np.float32(max(dist, 1)) / np.float32(exact)))
                            / np.float32(math.log(MAX_DIST / exact)) * np.float32(BUCKETS - exact))
        c[dist if dist < exact else min(large, BUCKETS - 1), C_HOT + j] = 1.0
    even = (np.arange(P) // GC) % 2 == 0
    c[:, C_EVEN] = even
    c[:, C_ODD] = ~even
    return c


class Steps:

    def __init__(self, eng, sem):
        self.eng, self.sem, self.n, self.at = eng, sem, 0, 0

    def do(self, ins):
        ins.then_inc(self.sem, 1)
        self.n += 1

    def settle(self):
        self.eng.wait_ge(self.sem, self.at + self.n)


def build(nc, x, c, rel_bias, w_ada, b_ada, g_pre_mix, g_post_mix, g_pre_ffn, g_post_ffn, w_in,
          ssm_a_re, ssm_a_im, ssm_log_dt, ssm_b_re, ssm_b_im, ssm_c_re, ssm_c_im, ssm_d, w_glu,
          w_ssm_out, w_att_out, w_out, w_router, b_router, w_exp_in, b_exp_in, w_exp_out, b_exp_out,
          const, bias_line, bias_rows, out):
    ctx = ExitStack()
    with ctx:
        def sb(name, shape, dt=F32):
            return ctx.enter_context(nc.sbuf_tensor(name, shape, dt))

        def sem(name):
            return ctx.enter_context(nc.semaphore(name))

        ring = sb("ring", [P, SLOTS, PW])
        cst = sb("cst", [P, C_HOT])
        xs = sb("xs", [P, TT, D])
        hT = sb("hT", [P, KD, T])
        row_a = sb("row_a", [P, D])
        row_b = sb("row_b", [P, D])
        row_g = sb("row_g", [P, D])
        small = sb("small", [P, 640])
        work = sb("work", [P, 19712])
        flag = sb("flag", [P, 1], I32)
        idx = sb("idx", [P, TT, 8], U32)
        psum = ctx.enter_context(nc.psum_tensor("psum", [P, 8, 512], F32))
        bank = [psum[:, i, :] for i in range(8)]
        bu_re, bu_im = psum[:, 0:2, 0:T], psum[:, 0:2, T:2 * T]

        at = [0]

        def carve(n, where=None):
            start = at[0] if where is None else where
            if where is None:
                at[0] += n
                assert at[0] <= 19712
            return work[:, start:start + n]

        ident = cst[:, C_ID:C_ID + P]
        ones = cst[:, C_ONE:C_ONE + P]
        tri = cst[:, C_TRI:C_TRI + P]
        iota = cst[:, C_IOTA:C_IOTA + P]

        uT = carve(1024).rearrange("p (j t) -> p j t", j=KS)
        qk_flat = carve(2048)
        qT = qk_flat[:, 0:1024].rearrange("p (j t) -> p j t", j=4)
        kT = qk_flat[:, 1024:2048].rearrange("p (j t) -> p j t", j=4)
        gs_t = qk_flat.rearrange("p (j t) -> p j t", j=KD)
        vv = carve(1024).rearrange("p (a n) -> p a n", a=TT)
        attT = carve(1024).rearrange("p (j t) -> p j t", j=4)
        ta_flat = carve(2048)
        ga_t = ta_flat.rearrange("p (j t) -> p j t", j=KD)
        ao_flat = carve(2048)
        aoT = ao_flat.rearrange("p (j t) -> p j t", j=KD)
        ssm_flat = carve(3584)
        zr, zi, tp = (ssm_flat[:, 512 * n:512 * n + 512] for n in range(3))
        xre = [ssm_flat[:, 1536 + 1024 * n:2048 + 1024 * n] for n in range(2)]
        xim = [ssm_flat[:, 2048 + 1024 * n:2560 + 1024 * n] for n in range(2)]
        attn_flat = carve(2304)
        bias_m = [attn_flat[:, 384 * n:384 * n + 384] for n in range(2)]
        lg_m = [attn_flat[:, 768 + 384 * n:1152 + 384 * n] for n in range(2)]
        pt_m = [attn_flat[:, 1536 + 384 * n:1920 + 384 * n] for n in range(2)]
        btct = carve(2048)
        BT = btct[:, 0:1024].rearrange("p (r j s) -> p r j s", r=2, j=4)
        CT = btct[:, 1024:2048].rearrange("p (r j s) -> p r j s", r=2, j=4)
        row_g2 = btct[:, 0:1024]
        bada = carve(1024).rearrange("p (b n) -> p b n", b=2)
        grow = carve(512)
        cond_b = carve(1024).rearrange("p (k m) -> p k m", k=KD)
        b_in = qk_flat[:, 0:512].rearrange("p (r s c) -> p r s c", r=2, s=ST)
        b_bar = qk_flat[:, 512:1536].rearrange("p (r s c) -> p r s c", r=2, s=ST)
        b_tmp = qk_flat[:, 1536:1792].rearrange("p (s c) -> p s c", s=ST)
        b_tmp2 = qk_flat[:, 1792:2048].rearrange("p (s c) -> p s c", s=ST)
        c_in = ssm_flat[:, 0:512].rearrange("p (r j s) -> p r j s", r=2, j=4)
        c_pad = ssm_flat[:, 512:1536].rearrange("p (r j s) -> p r j s", r=2, j=4)
        tab_c = ring[:, 4, :].rearrange("p (s t) -> p s t", s=ST)
        tab_s = ring[:, 5, :].rearrange("p (s t) -> p s t", s=ST)
        tab_1 = ta_flat.rearrange("p (s t) -> p s t", s=ST)
        tab_2 = ao_flat.rearrange("p (s t) -> p s t", s=ST)
        vrow = attn_flat[0:64, 0:P]
        ldt_in = attn_flat[0:ST, 140:142]
        relb = attn_flat[0:BUCKETS + 1, 128:128 + HEADS]
        bline = attn_flat[0:HEADS, 256:256 + N_HOT]
        junk = attn_flat[:, 1024:2048]
        hot = ssm_flat[0:BUCKETS + 1, 1600:1600 + N_HOT]
        gv = ssm_flat[:, 0:1024]
        gt_ = ssm_flat[:, 1024:2048]
        gluT = gv.rearrange("p (j t) -> p j t", j=KS)
        rT = ta_flat.rearrange("p (k t) -> p k t", k=KD)
        y_sb = qk_flat.rearrange("p (a n) -> p a n", a=TT)
        at[0] = 1024
        acc = carve(2048).rearrange("p (a n) -> p a n", a=TT)
        b1all = carve(2048)[0:NE, :]
        xeT = carve(1024).rearrange("p (k s) -> p k s", k=KD)
        actT = carve(1024).rearrange("p (k s) -> p k s", k=KD)
        act_t = carve(1024)
        y_e = carve(1024)
        g_c, u_c, th_c = carve(512), carve(512), carve(512)
        pick = carve(256).rearrange("p (a s) -> p a s", a=TT)
        pickg = carve(256).rearrange("p (a s) -> p a s", a=TT)
        pickT = carve(256)
        sel = carve(128)[0:NE, :]
        wr = carve(256).rearrange("p (k e) -> p k e", k=KD)
        row_of = carve(130).rearrange("p (a e) -> p a e", a=TT)
        gate_of = carve(130).rearrange("p (a e) -> p a e", a=TT)
        b2all = carve(1024)[0:NE, :]
        gT = carve(T)[0:NE, :]
        br = carve(NE)[0:1, :]
        assert at[0] <= 13824
        h2 = hT[:, :, :].rearrange("p k t -> p (k t)").rearrange("p (a n) -> p a n", a=TT)

        sm = [0]

        def little(n):
            sm[0] += n
            assert sm[0] <= 640
            return small[:, sm[0] - n:sm[0]]

        vcol = little(60)
        ldt, cond_c, dcol = vcol[:, 0:16], vcol[:, 16:24], vcol[:, 24:28]
        are, aim = vcol[:, 28:44], vcol[:, 44:60]
        ss = little(2)
        ms = little(2)
        rstd = little(2)
        nhalf = little(2)
        lam, theta, rho, ec, es, zre, zim, m1, m2, m3, m4 = (little(16) for _ in range(11))
        mx = little(2)
        sums = little(2)
        lgr = little(64).rearrange("p (a e) -> p a e", a=TT)
        msk = little(64).rearrange("p (a e) -> p a e", a=TT)
        gat = little(64).rearrange("p (a e) -> p a e", a=TT)
        one_hot = little(32)
        top = little(16).rearrange("p (a e) -> p a e", a=TT)
        topx = little(16).rearrange("p (a e) -> p a e", a=TT)
        idf = little(16).rearrange("p (a e) -> p a e", a=TT)
        ms2 = little(2)

        slot_in = [sem(f"slot_in{s}") for s in range(SLOTS)]
        const_in, vec_in, x_in, param_in, x_again = sem("const_in"), sem("vec_in"), sem("x_in"), sem("param_in"), sem("x_again")
        bada_in = [sem("bada_in0"), sem("bada_in1")]
        grow_in = sem("grow_in")
        bias_out, bias_in = sem("bias_out"), [sem("bias_in0"), sem("bias_in1")]
        moe_in = sem("moe_in")
        fill_done, dve_emptied, act_emptied = sem("fill_done"), sem("dve_emptied"), sem("act_emptied")
        emptied_sem = {"dve": dve_emptied, "act": act_emptied}
        v_step, a_step, g_step = sem("v_step"), sem("a_step"), sem("g_step")
        relb_ready, vrow_ready = sem("relb_ready"), sem("vrow_ready")
        vrow_turned, vcol_ready, cond_ready = sem("vrow_turned"), sem("vcol_ready"), sem("cond_ready")
        dt_ready, theta_ready, sine_ready, gauss = sem("dt_ready"), sem("theta_ready"), sem("sine_ready"), sem("nhalf_ready")
        bc_padded, bc_turned, bc_ready = sem("bc_padded"), sem("bc_turned"), sem("bc_ready")
        bline_done, bline_ready = sem("bline_done"), sem("bline_ready")
        squares, rstd_ready, normed = sem("squares"), sem("rstd_ready"), sem("normed")
        h_turned, hT_ready, rT_ready = sem("h_turned"), sem("hT_ready"), sem("rT_ready")
        bu_done, bu_read, x_ready, y_done = sem("bu_done"), sem("bu_read"), sem("x_ready"), sem("y_done")
        y_read = sem("y_read")
        s_done, logits_ready, exp_done, probs_ready, p_turned, pT_ready = (
            sem("s_done"), sem("logits_ready"), sem("exp_done"), sem("probs_ready"), sem("p_turned"), sem("pT_ready"))
        pv_done, att_ready, max_ready = sem("pv_done"), sem("att_ready"), sem("max_ready")
        gelu_in, gelu_th, gelu_out = sem("gelu_in"), sem("gelu_th"), sem("gelu_out")
        glu_ready, merged_ready = sem("glu_ready"), sem("merged_ready")
        x1_ready = sem("x1_ready")
        logit_done, top_ready, topexp, mask_ready, rank_done, route_ready = (
            sem("logit_done"), sem("top_ready"), sem("topexp"), sem("mask_ready"), sem("rank_done"), sem("route_ready"))
        gates_turned, gT_ready, b2_done, acc_init = sem("gates_turned"), sem("gT_ready"), sem("b2_done"), sem("acc_init")
        sel_ready, pick_ready, pickg_ready = sem("sel_ready"), sem("pick_ready"), sem("pickg_ready")
        up_done, g_ready, gate_th, act_ready = sem("up_done"), sem("g_ready"), sem("gate_th"), sem("act_ready")
        gather_done, xe_ready = sem("gather_done"), sem("xe_ready")
        act_turned, actT_ready = sem("act_turned"), sem("actT_ready")
        pick_turned, pickT_ready = sem("pick_turned"), sem("pickT_ready")
        down_done, ye_ready = sem("down_done"), sem("ye_ready")
        comb_done, acc_done = sem("comb_done"), sem("acc_done")
        out_ready, stored = sem("out_ready"), sem("stored")

        def broadcast(vec, n0, n1):
            return vec[0:1, n0:n1].broadcast_to([P, n1 - n0])

        def moe_source(e, s):
            if s < 4:
                col = 512 * (s // 2) + FF * (s % 2)
                return w_exp_in[0][bass.ds(e, 1), :, col:col + 512].rearrange("o (k p) n -> (o p) k n", p=P)
            r = 512 * (s - 4)
            return w_exp_out[0][bass.ds(e, 1), r:r + 512, :].rearrange("o (k p) n -> (o p) k n", p=P)

        def slot(s, k):
            return ring[:, s, :].rearrange("p (k n) -> p k n", k=k)

        block = ctx.enter_context(nc.Block())

        @block.sync
        def _(sp):
            def source(name):
                if name in ADA:
                    return w_ada[0][:, ADA_COL[name]:ADA_COL[name] + 512], 8
                if name == "glu":
                    return w_glu[0], 4
                if name == "ao":
                    return w_att_out[0], 4
                if name == "so":
                    return w_ssm_out[0], 4
                if name in ("wo0", "wo1"):
                    n = 512 * int(name[2])
                    return w_out[0][:, n:n + 512], 8
                col = {"q": 0, "k": 1, "v": 2, "u": 3, "ga0": 4, "ga1": 5, "gs0": 6, "gs1": 7}[name] * 512
                return w_in[0][:, col:col + 512], 8

            sp.dma_start(cst[:, :], const[:, 0:C_HOT]).then_inc(const_in, 16)
            sp.dma_start(hot, const[0:BUCKETS + 1, C_HOT:C_N]).then_inc(const_in, 16)
            for n, name in enumerate(MIX):
                s = n % MIX_SLOTS
                if n >= MIX_SLOTS:
                    sp.wait_ge(fill_done, used_up(n - MIX_SLOTS))
                src, k = source(name)
                sp.dma_start(slot(s, k), src.rearrange("(k p) n -> p k n", p=P)).then_inc(slot_in[s], 16)
            for s in range(SLOTS):
                if s < MIX_SLOTS:
                    last = max(n for n in range(len(MIX)) if n % MIX_SLOTS == s)
                    sp.wait_ge(fill_done, used_up(last))
                else:
                    sp.wait_ge(x_ready, 8)
                sp.dma_start(slot(s, 8 if s < 4 else 4), moe_source(0, s)).then_inc(slot_in[s], 16)

            def expert_weights(i, e):
                for s in range(SLOTS):
                    if s < 4:
                        sp.wait_ge(up_done, 4 * i + (s - 3))
                    else:
                        sp.wait_ge(down_done, 2 * i + (s - 5))
                    sp.dma_start(slot(s, 8 if s < 4 else 4), moe_source(e, s)).then_inc(slot_in[s], 16)

            with sp.Fori(1, NE) as i:
                expert_weights(i, i)
            sp.wait_ge(route_ready, 1)
            more = sp.value_load(flag[0:1, 0:1], min_val=0, max_val=1)
            with sp.If(more > 0):
                with sp.Fori(NE, 2 * NE) as i:
                    expert_weights(i, i - NE)
            for a in range(TT):
                sp.wait_ge(out_ready, a + 1)
                sp.dma_start(out[0, a * P:(a + 1) * P, :], xs[:, a, :]).then_inc(stored, 16)
            sp.wait_ge(stored, 16 * TT)

        @block.gpsimd
        def _(pool):
            pool.dma_start(vrow[16:24, :], c.rearrange("o (k p) -> (o k) p", p=P)).then_inc(vec_in, 16)
            pool.dma_start(vrow[24:28, :], ssm_d.rearrange("o (k p) -> (o k) p", p=P)).then_inc(vec_in, 16)
            pool.dma_start(vrow[28:44, :], ssm_a_re[0].rearrange("(s a) p -> s (a p)", a=2)).then_inc(vec_in, 16)
            pool.dma_start(vrow[44:60, :], ssm_a_im[0].rearrange("(s a) p -> s (a p)", a=2)).then_inc(vec_in, 16)
            pool.dma_start(ldt_in, ssm_log_dt[0].rearrange("(s a) -> s a", a=2)).then_inc(vec_in, 16)
            for a in range(TT):
                pool.dma_start(xs[:, a, :], x[0, a * P:(a + 1) * P, :]).then_inc(x_in, 16)
            
            def ada_bias(n):
                name = ADA[n]
                if n >= 2:
                    pool.wait_ge(dve_emptied, emptied(FILL[(ADA[n - 2], 0)])[1])
                pool.dma_start(bada[:, n % 2, :], broadcast(b_ada, ADA_COL[name], ADA_COL[name] + 512)
                               ).then_inc(bada_in[n % 2], 16)
                if name in G_USERS:
                    m = G_USERS.index(name)
                    if m:
                        pool.wait_ge(dve_emptied, emptied(FILL[(G_USERS[m - 1], 0)])[1])
                    g = {"sc1": g_pre_mix, "gt1": g_post_mix, "sc2": g_pre_ffn, "gt2": g_post_ffn}[name[:3]]
                    pool.dma_start(grow, broadcast(g, 512 * (m % 2), 512 * (m % 2) + 512)).then_inc(grow_in, 16)

            ada_bias(0)
            ada_bias(1)
            for r, b in enumerate((ssm_b_re, ssm_b_im)):
                pool.dma_start(b_in[:, r, :, :], b[0].rearrange("(s a) p c -> (a p) s c", a=2)).then_inc(param_in, 16)
            for r, cc in enumerate((ssm_c_re, ssm_c_im)):
                pool.dma_start(c_in[:, r, :, :], cc[0].rearrange("(j g) c p -> (g c) j p", j=4)).then_inc(param_in, 16)
            pool.memset(relb, MASKED).then_inc(g_step, 1)
            pool.wait_ge(g_step, 1)
            pool.dma_start(relb[0:BUCKETS, :], rel_bias).then_inc(relb_ready, 16)
            pool.memset(nhalf, -0.5).then_inc(g_step, 1)
            pool.wait_ge(g_step, 2)
            steps = [2]

            def root(n, bias, slot_n):
                pool.wait_ge(squares, slot_n + 1)
                pool.tensor_scalar(ms[:, n:n + 1], ss[:, n:n + 1], 1.0 / D, bias, ALU.mult, ALU.add).then_inc(g_step, 1)
                steps[0] += 1
                pool.wait_ge(g_step, steps[0])
                pool.tensor_tensor(rstd[:, n:n + 1], ms[:, n:n + 1], nhalf[:, 0:1], ALU.pow).then_inc(rstd_ready, 1)

            for n in range(TT):
                root(n, EPS, n)
            for n in range(2, 4):
                ada_bias(n)
            pool.wait_ge(bline_ready, 1)
            pool.dma_start(bias_line, bline).then_inc(bias_out, 16)
            pool.wait_ge(bias_out, 16)
            pool.dma_start(bias_rows[:, :, 0:N_HOT],
                           bias_line.rearrange("h (o n) -> h o n", o=1).broadcast_to([HEADS, P, N_HOT])
                           ).then_inc(bias_out, 16)
            pool.wait_ge(bias_out, 32)

            def bias_matrix(h):
                if h >= 2:
                    pool.wait_ge(logits_ready, h - 1)
                else:
                    pool.wait_ge(vcol_ready, 1)
                for a, (lo, hi) in enumerate(((0, P), (P, 3 * P))):
                    src = bass.AP(tensor=bias_rows.tensor, offset=h * P * 512 + T - 1 - a * P,
                                  ap=[[511, P], [1, hi - lo]])
                    pool.dma_start(bias_m[h % 2][:, lo:hi], src).then_inc(bias_in[h % 2], 16)

            bias_matrix(0)
            bias_matrix(1)
            ada_bias(4)
            ada_bias(5)
            bias_matrix(2)
            ada_bias(6)
            bias_matrix(3)
            ada_bias(7)
            bias_matrix(4)
            ada_bias(8)
            bias_matrix(5)
            ada_bias(9)
            bias_matrix(6)
            bias_matrix(7)
            ada_bias(10)
            ada_bias(11)
            pool.wait_ge(h_turned, 4)
            for a in range(TT):
                pool.dma_start(xs[:, a, :], x[0, a * P:(a + 1) * P, :]).then_inc(x_again, 16)
            for n in range(TT):
                root(n, 4.0 * EPS, 2 + n)
            pool.wait_ge(x1_ready, TT)
            pool.dma_start(b1all, b_exp_in[0]).then_inc(moe_in, 16)
            pool.dma_start(b2all, b_exp_out[0]).then_inc(moe_in, 16)
            pool.dma_start(wr, w_router[0].rearrange("(k p) e -> p k e", p=P)).then_inc(moe_in, 16)
            pool.dma_start(br[:, :], b_router).then_inc(moe_in, 16)
            for n in range(TT):
                root(n, EPS, 4 + n)
            for n in range(TT):
                root(n, EPS, 6 + n)

        @block.tensor
        def _(pe):
            seen = {s: 0 for s in range(MIX_SLOTS)}

            def arrive(name):
                n = MIX.index(name)
                pe.wait_ge(slot_in[n % MIX_SLOTS], 16 * (n // MIX_SLOTS + 1))
                return n % MIX_SLOTS

            def free_bank(f):
                if f >= 2:
                    who, count = emptied(f - 2)
                    pe.wait_ge(emptied_sem[who], count)
                return bank[4 + f % 2]

            pe.wait_ge(const_in, 32)
            pe.wait_ge(vec_in, 80)
            pe.wait_ge(vrow_ready, 1)
            pe.transpose(bank[3][:, 0:60], vrow[0:60, :], ident[0:60, 0:60]).then_inc(vrow_turned, 1)
            pe.wait_ge(relb_ready, 16)
            pe.matmul(bank[6][0:HEADS, 0:N_HOT], relb, hot,
                      start=True, stop=True).then_inc(bline_done, 1)

            def ada(name):
                s = arrive(name)
                f = FILL[(name, 0)]
                b = free_bank(f)
                w = slot(s, 8)
                for k in range(KD):
                    mm = pe.matmul(b[:, :], cond_b[:, k, :], w[:, k, :], start=k == 0, stop=k == KD - 1)
                mm.then_inc(fill_done, 1)

            def features(name, b, k_n, rhs):
                s = MIX.index(name) % MIX_SLOTS
                f = FILL[(name, b)]
                out_b = free_bank(f)
                w = slot(s, k_n)
                for m in range(2):
                    col = (2 * b + m) * P
                    for k in range(k_n):
                        mm = pe.matmul(out_b[:, m * T:(m + 1) * T], w[:, k, col:col + P], rhs[:, k, :],
                                       start=k == 0, stop=k == k_n - 1)
                mm.then_inc(fill_done, 1)

            def tokens(name, a, lhs):
                s = MIX.index(name) % MIX_SLOTS
                f = FILL[(name, a)]
                out_b = free_bank(f)
                w = slot(s, 8)
                for k in range(KD):
                    mm = pe.matmul(out_b[:, :], lhs[:, k, a * P:(a + 1) * P], w[:, k, :],
                                   start=k == 0, stop=k == KD - 1)
                mm.then_inc(fill_done, 1)

            pe.wait_ge(cond_ready, 1)
            for name in ADA[0:4]:
                ada(name)
            pe.wait_ge(bc_padded, 1)
            for r in range(2):
                for j in range(4):
                    mm = pe.transpose(bank[r][:, j * P:(j + 1) * P],
                                      b_bar[:, r, 4 * j:4 * j + 4, :].rearrange("p s c -> p (s c)"), ident)
            mm.then_inc(bc_turned, 1)
            pe.wait_ge(bc_padded, 2)
            pe.wait_ge(vcol_ready, 1)
            for r in range(2):
                for j in range(4):
                    mm = pe.transpose(bank[2 + r][:, j * P:(j + 1) * P], c_pad[:, r, j, :], ident)
            mm.then_inc(bc_turned, 1)
            for g in range(4):
                if g == 0:
                    pe.wait_ge(normed, TT)
                    pe.wait_ge(bline_ready, 1)
                if g >= 2:
                    pe.wait_ge(hT_ready, g - 1)
                for kk in range(2):
                    for a in range(TT):
                        k = 2 * g + kk
                        mm = pe.transpose(bank[6 + g % 2][:, kk * T + a * P:kk * T + (a + 1) * P],
                                          xs[:, a, k * P:(k + 1) * P], ident)
                mm.then_inc(h_turned, 1)
            pe.wait_ge(hT_ready, 4)
            arrive("u")
            for b in range(2):
                features("u", b, 8, hT)

            def inputs_to_states(n):
                if n == 0:
                    pe.wait_ge(bc_ready, 2)
                    pe.wait_ge(act_emptied, emptied(FILL[("u", 1)])[1])
                else:
                    pe.wait_ge(bu_read, n)
                for m in range(2):
                    st = 2 * n + m
                    j, q = st // 4, st % 4
                    for r in range(2):
                        mm = pe.matmul(bank[m][:, r * T:(r + 1) * T], BT[32 * q:32 * q + 32, r, j, :],
                                       uT[32 * q:32 * q + 32, j, :], start=True, stop=True,
                                       tile_position=(32 * q, 0))
                mm.then_inc(bu_done, 1)

            def states_to_outputs(n):
                pe.wait_ge(x_ready, n + 1)
                j = n // 2
                if n % 2 == 0 and j >= 1:
                    pe.wait_ge(y_read, j)
                for m in range(2):
                    st = 2 * n + m
                    q = st % 4
                    o = bank[2][32 * q:32 * q + 32, 0:T]
                    pe.matmul(o, CT[:, 0, j, 32 * q:32 * q + 32], xre[n % 2][:, m * T:(m + 1) * T],
                              start=True, stop=False, tile_position=(0, 32 * q))
                    mm = pe.matmul(o, CT[:, 1, j, 32 * q:32 * q + 32], xim[n % 2][:, m * T:(m + 1) * T],
                                   start=False, stop=True, tile_position=(0, 32 * q))
                mm.then_inc(y_done, 1)

            seq = [("q", 0), ("q", 1), ("k", 0), ("k", 1), ("v", 0), ("v", 1), ("ga0", 0), ("ga0", 1)]
            for n, (name, b) in enumerate(seq):
                inputs_to_states(n)
                if b == 0:
                    arrive(name)
                if name == "v":
                    tokens(name, b, hT)
                else:
                    features(name, b, 8, hT)
                if n >= 1:
                    states_to_outputs(n - 1)
            arrive("ga1")
            features("ga1", 0, 8, hT)
            states_to_outputs(7)
            features("ga1", 1, 8, hT)

            def scores(h):
                if h >= 2:
                    pe.wait_ge(pT_ready, h - 1)
                if h == 0:
                    pe.wait_ge(act_emptied, emptied(FILL[("v", 1)])[1])
                r = 64 * (h % 2)
                o = bank[6 + h % 2]
                for a in range(TT):
                    mm = pe.matmul(o[:, a * P:a * P + (a + 1) * P], qT[r:r + 64, h // 2, a * P:(a + 1) * P],
                                   kT[r:r + 64, h // 2, 0:(a + 1) * P], start=True, stop=True,
                                   tile_position=(r, 0))
                mm.then_inc(s_done, 1)

            scores(0)
            for h in range(HEADS):
                if h < HEADS - 1:
                    scores(h + 1)
                if h < 6:
                    ada(ADA[4 + h])
                pe.wait_ge(probs_ready, h + 1)
                for b in range(3):
                    mm = pe.transpose(bank[6 + h % 2][:, b * P:(b + 1) * P], lg_m[h % 2][:, b * P:(b + 1) * P], ident)
                mm.then_inc(p_turned, 1)
                pe.wait_ge(pT_ready, h + 1)
                if h % 2 == 0 and h >= 2:
                    pe.wait_ge(att_ready, h // 2)
                r = 64 * (h % 2)
                o = bank[3][r:r + 64, 0:T]
                pe.matmul(o, vv[:, 0, h * HD:(h + 1) * HD], pt_m[h % 2][:, 0:T], start=True, stop=False,
                          tile_position=(0, r))
                pe.matmul(o[:, P:T], vv[:, 1, h * HD:(h + 1) * HD], pt_m[h % 2][:, T:3 * P],
                          start=False, stop=True, tile_position=(0, r)).then_inc(pv_done, 1)
            for name in ("gs0", "gs1"):
                arrive(name)
                for b in range(2):
                    features(name, b, 8, hT)
            pe.wait_ge(gelu_out, 1)
            arrive("glu")
            for b in range(4):
                features("glu", b, 4, uT)
            pe.wait_ge(att_ready, 4)
            arrive("ao")
            for b in range(4):
                features("ao", b, 4, attT)
            pe.wait_ge(glu_ready, 1)
            arrive("so")
            for b in range(4):
                features("so", b, 4, gluT)
            ada("gt2a")
            ada("gt2b")
            pe.wait_ge(merged_ready, 4)
            for name in ("wo0", "wo1"):
                arrive(name)
                for a in range(TT):
                    tokens(name, a, aoT)

            for g in range(4):
                if g == 0:
                    pe.wait_ge(normed, 2 * TT)
                if g >= 2:
                    pe.wait_ge(rT_ready, g - 1)
                for kk in range(2):
                    for a in range(TT):
                        k = 2 * g + kk
                        mm = pe.transpose(bank[6 + g % 2][:, kk * T + a * P:kk * T + (a + 1) * P],
                                          h2[:, a, k * P:(k + 1) * P], ident)
                mm.then_inc(h_turned, 1)
            pe.wait_ge(rT_ready, 4)
            pe.wait_ge(moe_in, 64)
            for a in range(TT):
                for k in range(KD):
                    pe.matmul(bank[0][:, a * NE:(a + 1) * NE], rT[:, k, a * P:(a + 1) * P], wr[:, k, :],
                              start=k == 0, stop=False)
                mm = pe.matmul(bank[0][:, a * NE:(a + 1) * NE], ones[0:1, :], br[:, :], start=False, stop=True)
            mm.then_inc(logit_done, 1)
            pe.wait_ge(mask_ready, 1)
            pe.matmul(bank[1][:, 0:NE], tri, msk[:, 0, :], start=True, stop=True)
            pe.matmul(bank[1][:, NE:2 * NE], ones, msk[:, 0, :], start=True, stop=False)
            pe.matmul(bank[1][:, NE:2 * NE], tri, msk[:, 1, :], start=False, stop=True)
            pe.matmul(bank[1][:, 2 * NE:3 * NE], ones, msk[:, 0, :], start=True, stop=False)
            pe.matmul(bank[1][:, 2 * NE:3 * NE], ones, msk[:, 1, :], start=False, stop=True).then_inc(rank_done, 1)
            for a in range(TT):
                mm = pe.transpose(bank[2][0:NE, a * P:(a + 1) * P], gat[:, a, :], ident)
            mm.then_inc(gates_turned, 1)
            pe.wait_ge(gT_ready, 1)
            for a in range(TT):
                for n in range(2):
                    mm = pe.matmul(bank[4 + 2 * a + n][:, :], gT[:, a * P:(a + 1) * P], b2all[:, 512 * n:512 * n + 512],
                                   start=True, stop=True)
            mm.then_inc(b2_done, 1)

            def gather(i):
                pe.wait_ge(pick_ready, i + 1)
                pe.wait_ge(acc_done, 4 * i)
                for k in range(KD):
                    for a in range(TT):
                        mm = pe.matmul(bank[6 + k // 4][:, (k % 4) * P:(k % 4 + 1) * P],
                                       h2[:, a, k * P:(k + 1) * P], pick[:, a, :], start=a == 0, stop=a == TT - 1)
                mm.then_inc(gather_done, 1)

            def arrived(s, i):
                first = len([n for n in range(len(MIX)) if n % MIX_SLOTS == s]) if s < MIX_SLOTS else 0
                pe.wait_ge(slot_in[s], i * 16 + 16 * (first + 1))

            def up(i, s):
                arrived(s, i)
                w = slot(s, 8)
                col = 512 * (s // 2) + FF * (s % 2)
                for k in range(KD):
                    pe.matmul(bank[s][:, :], xeT[:, k, :], w[:, k, :], start=k == 0, stop=False)
                pe.matmul(bank[s][:, :], sel, b1all[:, col:col + 512], start=False, stop=True
                          ).then_inc(up_done, 1)

            def turn_act(i, half):
                pe.wait_ge(act_ready, 2 * i + half + 1)
                for k in range(4):
                    mm = pe.transpose(bank[half][:, k * P:(k + 1) * P],
                                      act_t[:, half * 512 + k * P:half * 512 + (k + 1) * P], ident)
                mm.then_inc(act_turned, 1)

            def down(i, half):
                pe.wait_ge(actT_ready, 2 * i + half + 1)
                arrived(4 + half, i)
                if half == 0:
                    pe.wait_ge(ye_ready, i + 1)
                w = slot(4 + half, 4)
                for k in range(4):
                    for n in range(2):
                        mm = pe.matmul(bank[4 + n][:, :], actT[:, 4 * half + k, :], w[:, k, 512 * n:512 * n + 512],
                                       start=half == 0 and k == 0, stop=half == 1 and k == 3)
                mm.then_inc(down_done, 1)

            def combine(i, q):
                if q == 0:
                    pe.wait_ge(pickT_ready, i + 2)
                    pe.wait_ge(ye_ready, i + 2)
                    pe.wait_ge(act_ready, 2 * i + 2)
                    pe.wait_ge(xe_ready, i + 2)
                a, n = q // 2, q % 2
                pe.matmul(bank[(2, 3, 6, 7)[q]][:, :], pickT[:, a * P:(a + 1) * P], y_e[:, 512 * n:512 * n + 512],
                          start=True, stop=True).then_inc(comb_done, 1)

            def expert(i, before):
                pe.wait_ge(xe_ready, i + 1)
                pe.wait_ge(sel_ready, i + 1)
                pe.wait_ge(pickT_ready, i + 1)
                up(i, 0)
                up(i, 1)
                if before:
                    for q in range(4):
                        combine(i - 1, q)
                pe.wait_ge(acc_done, 4 * i + 1)
                up(i, 2)
                pe.wait_ge(acc_done, 4 * i + 2)
                up(i, 3)
                turn_act(i, 0)
                gather(i + 1)
                down(i, 0)
                turn_act(i, 1)
                pe.wait_ge(actT_ready, 2 * i + 1)
                pe.wait_ge(pickg_ready, i + 1)
                for a in range(TT):
                    mm = pe.transpose(bank[0][:, a * P:(a + 1) * P], pickg[:, a, :], ident)
                mm.then_inc(pick_turned, 1)
                down(i, 1)

            pe.wait_ge(acc_init, 1)
            gather(0)
            with pe.Fori(0, NE) as i:
                expert(i, True)
            for q in range(4):
                combine(NE - 1, q)
            pe.wait_ge(route_ready, 1)
            more = pe.value_load(flag[0:1, 0:1], min_val=0, max_val=1)
            with pe.If(more > 0):
                with pe.Fori(NE, 2 * NE) as i:
                    expert(i, False)
                    for q in range(4):
                        combine(i, q)

        @block.scalar
        def _(act):
            st = Steps(act, a_step)
            act.wait_ge(vcol_ready, 1)
            act.activation(m4[:, 0:8], cond_c, ACT.Tanh, scale=0.5).then_inc(dt_ready, 1)
            act.activation(ldt, ldt, ACT.Exp).then_inc(dt_ready, 1)
            act.wait_ge(theta_ready, 1)
            act.activation(rho, rho, ACT.Exp).then_inc(sine_ready, 1)
            act.wait_ge(theta_ready, 2)
            act.activation(es, theta, ACT.Sin).then_inc(sine_ready, 1)
            act.activation(ec, theta, ACT.Sin, scale=0.5).then_inc(sine_ready, 1)
            act.wait_ge(bline_done, 1)
            act.wait_ge(vrow_turned, 1)
            act.activation(bline, bank[6][0:HEADS, 0:N_HOT], ACT.Copy).then_inc(bline_ready, 1)

            def square(n, src, first):
                if not first:
                    st.settle()
                st.do(act.activation(junk, src, ACT.Square, accum_out=ss[:, n:n + 1]))

            act.wait_ge(x_in, 16 * TT)
            for n in range(TT):
                act.activation(junk, xs[:, n, :], ACT.Square, accum_out=ss[:, n:n + 1]).then_inc(squares, 1)
                act.wait_ge(squares, n + 1)
            for r in range(2):
                if r == 0:
                    act.wait_ge(bc_turned, 1)
                act.activation(BT[:, r, :, :].rearrange("p j s -> p (j s)"), bank[r][:, :], ACT.Copy).then_inc(
                    *((a_step, 1) if r == 0 else (bc_ready, 1)))
            st.n += 1
            act.wait_ge(bc_turned, 2)
            for r in range(2):
                act.activation(CT[:, r, :, :].rearrange("p j s -> p (j s)"), bank[2 + r][:, :], ACT.Copy).then_inc(
                    *((a_step, 1) if r == 0 else (bc_ready, 1)))
            st.n += 1

            for g in range(4):
                act.wait_ge(h_turned, g + 1)
                act.activation(hT[:, 2 * g:2 * g + 2, :].rearrange("p k t -> p (k t)"), bank[6 + g % 2][:, :],
                               ACT.Copy).then_inc(hT_ready, 1)

            def empty(name, b, dst, func=ACT.Copy, scale=1.0):
                f = FILL[(name, b)]
                act.wait_ge(fill_done, f + 1)
                act.activation(dst, bank[4 + f % 2][:, :], func, scale=scale).then_inc(act_emptied, 1)

            def two(view, b):
                return view[:, 2 * b:2 * b + 2, :].rearrange("p k t -> p (k t)")

            for b in range(2):
                empty("u", b, two(uT, b))
            for b in range(2):
                empty("q", b, two(qT, b))
            for b in range(2):
                empty("k", b, two(kT, b))
            for b in range(2):
                empty("v", b, vv[:, b, :])
            for n in range(2):
                for b in range(2):
                    empty(f"ga{n}", b, two(ga_t, 2 * n + b), ACT.Tanh, 0.5)

            for h in range(HEADS):
                act.wait_ge(max_ready, h + 1)
                lo = lg_m[h % 2]
                act.activation(lo[:, 0:P], lo[:, 0:P], ACT.Exp, bias=mx[:, 0:1], accum_out=sums[:, 0:1]).then_inc(exp_done, 1)
                act.activation(lo[:, P:3 * P], lo[:, P:3 * P], ACT.Exp, bias=mx[:, 1:2], accum_out=sums[:, 1:2]).then_inc(exp_done, 1)
                act.wait_ge(p_turned, h + 1)
                if h >= 2:
                    act.wait_ge(pv_done, h - 1)
                act.activation(pt_m[h % 2], bank[6 + h % 2][:, 0:3 * P], ACT.Copy).then_inc(pT_ready, 1)
                if h % 2 == 1:
                    act.wait_ge(pv_done, h + 1)
                    j = h // 2
                    act.activation(attT[:, j, :], bank[3][:, 0:T], ACT.Copy).then_inc(att_ready, 1)
            act.wait_ge(s_done, HEADS)
            for n in range(2):
                for b in range(2):
                    empty(f"gs{n}", b, two(gs_t, 2 * n + b), ACT.Tanh, 0.5)
            act.wait_ge(gelu_in, 1)
            act.activation(gt_, gt_, ACT.Tanh, scale=GELU_C).then_inc(gelu_th, 1)
            act.wait_ge(gelu_out, 1)
            for b in range(2):
                empty("glu", b, gv[:, 512 * b:512 * b + 512])
            for b in range(2):
                empty("glu", 2 + b, gt_[:, 512 * b:512 * b + 512], ACT.Tanh, 0.25)
            for b in range(4):
                empty("ao", b, two(aoT, b))
            for name, n in (("wo0", 0), ("wo1", 1)):
                for a in range(TT):
                    empty(name, a, y_sb[:, a, 512 * n:512 * n + 512])

            act.wait_ge(act_emptied, emptied(FILL[("wo1", 1)])[1])
            for n in range(TT):
                act.activation(junk, y_sb[:, n, :], ACT.Square, accum_out=ss[:, n:n + 1]).then_inc(squares, 1)
                act.wait_ge(squares, TT + n + 1)
            for n in range(TT):
                act.wait_ge(x1_ready, n + 1)
                act.activation(junk, xs[:, n, :], ACT.Square, accum_out=ss[:, n:n + 1]).then_inc(squares, 1)
                act.wait_ge(squares, 2 * TT + n + 1)
            for g in range(4):
                act.wait_ge(h_turned, 4 + g + 1)
                act.activation(rT[:, 2 * g:2 * g + 2, :].rearrange("p k t -> p (k t)"), bank[6 + g % 2][:, :],
                               ACT.Copy).then_inc(rT_ready, 1)
            act.wait_ge(top_ready, 1)
            for a in range(TT):
                act.activation(topx[:, a, 0:TOPK], top[:, a, 0:TOPK], ACT.Exp, bias=ms2[:, a:a + 1],
                               accum_out=sums[:, a:a + 1]).then_inc(topexp, 1)
            act.wait_ge(gates_turned, 1)
            act.activation(gT[:, :], bank[2][0:NE, 0:T], ACT.Copy).then_inc(gT_ready, 1)

            def rows_in(i):
                act.wait_ge(gather_done, i + 1)
                for n in range(2):
                    last = act.activation(xeT[:, 4 * n:4 * n + 4, :].rearrange("p k s -> p (k s)"), bank[6 + n][:, :], ACT.Copy)
                last.then_inc(xe_ready, 1)

            def expert(i):
                for half in range(2):
                    act.wait_ge(g_ready, 2 * i + half + 1)
                    act.activation(th_c, g_c, ACT.Tanh, scale=ALPHA / 2).then_inc(gate_th, 1)
                act.wait_ge(act_turned, 2 * i + 1)
                act.activation(actT[:, 0:4, :].rearrange("p k s -> p (k s)"), bank[0][:, :], ACT.Copy).then_inc(actT_ready, 1)
                rows_in(i + 1)
                act.wait_ge(act_turned, 2 * i + 2)
                act.activation(actT[:, 4:8, :].rearrange("p k s -> p (k s)"), bank[1][:, :], ACT.Copy).then_inc(actT_ready, 1)
                act.wait_ge(pick_turned, i + 1)
                act.wait_ge(comb_done, 4 * i + 4)
                act.activation(pickT, bank[0][:, 0:T], ACT.Copy).then_inc(pickT_ready, 1)
                act.wait_ge(down_done, 2 * i + 2)
                for n in range(2):
                    last = act.activation(y_e[:, 512 * n:512 * n + 512], bank[4 + n][:, :], ACT.Copy)
                last.then_inc(ye_ready, 1)

            rows_in(0)
            with act.Fori(0, NE) as i:
                expert(i)
            act.wait_ge(route_ready, 1)
            more = act.value_load(flag[0:1, 0:1], min_val=0, max_val=1)
            with act.If(more > 0):
                with act.Fori(NE, 2 * NE) as i:
                    expert(i)
            act.wait_ge(normed, 3 * TT)
            for n in range(TT):
                act.activation(act_t, acc[:, n, :], ACT.Square, accum_out=ss[:, n:n + 1]).then_inc(squares, 1)
                act.wait_ge(squares, 3 * TT + n + 1)

        @block.vector
        def _(dve):
            V = Steps(dve, v_step)
            tt, ts, stt = dve.tensor_tensor, dve.tensor_scalar, dve.scalar_tensor_tensor

            def chain(ins):
                V.do(ins)
                V.settle()

            dve.wait_ge(vec_in, 80)
            dve.tensor_copy(vrow[0:ST, :].rearrange("s (a p) -> s a p", a=2),
                            ldt_in.rearrange("s (a o) -> s a o", o=1).broadcast_to([ST, 2, GP])).then_inc(vrow_ready, 1)
            dve.wait_ge(vrow_turned, 1)
            dve.tensor_copy(vcol, bank[3][:, 0:60]).then_inc(vcol_ready, 1)
            dve.wait_ge(vcol_ready, 1)
            dve.wait_ge(dt_ready, 2)
            chain(stt(cond_c, m4[:, 0:8], 1.0, cond_c, ALU.add, ALU.mult))
            for k in range(KD):
                last = ts(cond_b[:, k, :], ones, cond_c[:, k:k + 1], 0.5, ALU.mult, ALU.mult)
            last.then_inc(cond_ready, 1)
            V.do(ts(lam, are, -1e-4, None, ALU.min))
            chain(tt(theta, aim, ldt, ALU.mult))
            tt(rho, lam, ldt, ALU.mult).then_inc(theta_ready, 1)
            chain(ts(m1, theta, 1.0 / (2 * math.pi), ROUND, ALU.mult, ALU.add))
            chain(ts(m1, m1, -ROUND, None, ALU.add))
            rest = 2 * math.pi - 6.28125
            c2 = float(np.float32(np.round(rest * 2 ** 22) / 2 ** 22))
            for cc in (6.28125, c2, rest - c2):
                chain(stt(theta, m1, -cc, theta, ALU.mult, ALU.add))
            ts(theta, theta, 3.1415925, -3.1415925, ALU.min, ALU.max).then_inc(theta_ready, 1)
            dve.wait_ge(sine_ready, 3)
            chain(tt(ec, ec, ec, ALU.mult))
            chain(ts(ec, ec, -2.0, 1.0, ALU.mult, ALU.add))
            chain(tt(m1, rho, ec, ALU.mult))
            chain(tt(m2, rho, es, ALU.mult))
            chain(tt(m3, lam, lam, ALU.mult))
            chain(tt(m4, aim, aim, ALU.mult))
            chain(ts(m1, m1, -1.0, None, ALU.add))
            chain(tt(m3, m3, m4, ALU.add))
            chain(dve.reciprocal(m3, m3))
            chain(tt(zre, m1, lam, ALU.mult))
            chain(tt(m4, m2, aim, ALU.mult))
            chain(tt(zre, zre, m4, ALU.add))
            chain(tt(zim, m2, lam, ALU.mult))
            chain(tt(m4, m1, aim, ALU.mult))
            chain(tt(zim, zim, m4, ALU.subtract))
            chain(tt(zre, zre, m3, ALU.mult))
            chain(tt(zim, zim, m3, ALU.mult))
            dve.memset(b_bar, 0.0).then_inc(v_step, 1)
            V.n += 1
            dve.wait_ge(param_in, 64)
            V.settle()

            def over_c(v):
                return v.rearrange("p (s o) -> p s o", o=1).broadcast_to([P, ST, GC])

            for r, (a, b, op) in enumerate(((0, 1, ALU.subtract), (1, 0, ALU.add))):
                V.do(tt(b_tmp, b_in[:, a, :, :], over_c(zre), ALU.mult))
                chain(tt(b_tmp2, b_in[:, b, :, :], over_c(zim), ALU.mult))
                for g in range(2):
                    rows = slice(64 * g, 64 * g + 64)
                    last = tt(b_bar[rows, r, :, GC * g:GC * g + GC], b_tmp[rows], b_tmp2[rows], op)
                    if r == 0 or g == 0:
                        chain(last)
            last.then_inc(bc_padded, 1)
            for r in range(2):
                for g in range(2):
                    last = ts(c_pad[:, r, :, 64 * g:64 * g + 64], c_in[:, r, :, :], cst[:, C_EVEN + g:C_EVEN + g + 1],
                              1.0 if r == 0 else -1.0, ALU.mult, ALU.mult)
            last.then_inc(bc_padded, 1)

            def empty_ada(name):
                n = ADA.index(name)
                f = FILL[(name, 0)]
                col = 512 * (name[3] == "b")
                kind = name[:2]
                dve.wait_ge(fill_done, f + 1)
                dve.wait_ge(bada_in[n % 2], 16 * (n // 2 + 1))
                src, bia = bank[4 + f % 2][:, :], bada[:, n % 2, :]
                if kind == "sh":
                    tt(row_b[:, col:col + 512], src, bia, ALU.add).then_inc(dve_emptied, 1)
                    return
                dst = (row_a if kind == "sc" else row_g if name[2] == "1" else row_g2)[:, col:col + 512]
                dve.wait_ge(grow_in, 16 * (G_USERS.index(name) + 1))
                chain(tt(dst, src, bia, ALU.add))
                stt(dst, dst, 1.0 if kind == "sc" else 0.0, grow, ALU.add, ALU.mult
                    ).then_inc(dve_emptied, 1)

            dve.memset(tab_c[:, :, 0:1], 1.0)
            V.do(dve.memset(tab_s[:, :, 0:1], 0.0))
            V.do(dve.tensor_copy(m1, ec))
            chain(dve.tensor_copy(m2, es))

            def level(n):
                chain(tt(m3, m1, m1, ALU.mult))
                chain(tt(m4, m2, m2, ALU.mult))
                chain(tt(m3, m3, m4, ALU.add))
                chain(ts(m3, m3, -0.5, 1.5, ALU.mult, ALU.add))
                chain(tt(m1, m1, m3, ALU.mult))
                chain(tt(m2, m2, m3, ALU.mult))

                def over_t(v):
                    return v.rearrange("p (s o) -> p s o", o=1).broadcast_to([P, ST, n])

                a, b = tab_1[:, :, 0:n], tab_2[:, :, 0:n]
                chain(tt(a, tab_c[:, :, 0:n], over_t(m1), ALU.mult))
                chain(tt(b, tab_s[:, :, 0:n], over_t(m2), ALU.mult))
                chain(tt(tab_c[:, :, n:2 * n], a, b, ALU.subtract))
                chain(tt(a, tab_c[:, :, 0:n], over_t(m2), ALU.mult))
                chain(tt(b, tab_s[:, :, 0:n], over_t(m1), ALU.mult))
                chain(tt(tab_s[:, :, n:2 * n], a, b, ALU.add))
                chain(tt(m3, m1, m1, ALU.mult))
                chain(tt(m4, m2, m2, ALU.mult))
                chain(stt(m2, m1, 2.0, m2, ALU.mult, ALU.mult))
                chain(tt(m1, m3, m4, ALU.subtract))

            for n, name in enumerate(ADA[0:4]):
                empty_ada(name)
                level(1 << n)
            dve.wait_ge(dve_emptied, 4)
            for a in range(TT):
                dve.wait_ge(rstd_ready, a + 1)
                chain(stt(xs[:, a, :], xs[:, a, :], rstd[:, a:a + 1], row_a[:, :], ALU.mult, ALU.mult))
                tt(xs[:, a, :], xs[:, a, :], row_b[:, :], ALU.add).then_inc(normed, 1)
            for n in range(4, 8):
                level(1 << n)

            def skip(j):
                dve.wait_ge(y_done, 2 * j + 2)
                stt(uT[:, j, :], uT[:, j, :], dcol[:, j:j + 1], bank[2][:, 0:T],
                    ALU.mult, ALU.add).then_inc(y_read, 1)

            def by_tile(v):
                return v.rearrange("p (m t) -> p m t", m=2)

            zr3, zi3, tp3 = by_tile(zr), by_tile(zi), by_tile(tp)
            for n in range(8):
                tc = tab_c[:, 2 * n:2 * n + 2, :]
                tsn = tab_s[:, 2 * n:2 * n + 2, :]
                dve.wait_ge(bu_done, n + 1)
                chain(tt(zr3, bu_re, tc, ALU.mult))
                chain(tt(tp3, bu_im, tsn, ALU.mult))
                chain(tt(zr3, zr3, tp3, ALU.add))
                chain(tt(tp3, bu_re, tsn, ALU.mult))
                tt(zi3, bu_im, tc, ALU.mult).then_inc(bu_read, 1)
                dve.wait_ge(bu_read, n + 1)
                V.settle()
                chain(tt(zi3, zi3, tp3, ALU.subtract))
                if n >= 3 and n % 2:
                    skip((n - 3) // 2)
                for m in range(2):
                    decay = rho[:, 2 * n + m:2 * n + m + 1].broadcast_to([P, T])
                    for z in (zr, zi):
                        v = z[:, m * T:(m + 1) * T]
                        chain(dve.tensor_tensor_scan(v, decay, v, 0.0, ALU.mult, ALU.add))
                V.settle()
                if n >= 2:
                    dve.wait_ge(y_done, n - 1)
                xr_, xi_ = xre[n % 2], xim[n % 2]
                xr3, xi3 = by_tile(xr_), by_tile(xi_)
                chain(tt(xr3, zr3, tc, ALU.mult))
                chain(tt(tp3, zi3, tsn, ALU.mult))
                chain(tt(xi3, zi3, tc, ALU.mult))
                chain(tt(zr3, zr3, tsn, ALU.mult))
                chain(tt(xr_, xr_, tp, ALU.subtract))
                tt(xi_, xi_, zr, ALU.add).then_inc(x_ready, 1)
                dve.wait_ge(x_ready, n + 1)
                V.settle()

            skip(3)

            def head(h):
                dve.wait_ge(s_done, h + 1)
                dve.wait_ge(bias_in[h % 2], 32 * (h // 2 + 1))
                if h >= 2:
                    dve.wait_ge(p_turned, h - 1)
                lo = lg_m[h % 2]
                stt(lo, bank[6 + h % 2][:, 0:3 * P], HD ** -0.5, bias_m[h % 2], ALU.mult, ALU.add).then_inc(logits_ready, 1)
                dve.wait_ge(logits_ready, h + 1)
                V.do(dve.reduce_max(m1[:, 0:1], lo[:, 0:P], AX))
                chain(dve.reduce_max(m1[:, 1:2], lo[:, P:3 * P], AX))
                ts(mx, m1[:, 0:2], -1.0, None, ALU.mult).then_inc(max_ready, 1)
                dve.wait_ge(exp_done, 2 * h + 2)
                chain(dve.reciprocal(m2[:, 0:2], sums))
                V.do(ts(lo[:, 0:P], lo[:, 0:P], m2[:, 0:1], None, ALU.mult))
                ts(lo[:, P:3 * P], lo[:, P:3 * P], m2[:, 1:2], None, ALU.mult).then_inc(probs_ready, 1)
                V.settle()

            for h in range(HEADS):
                if h < 6:
                    empty_ada(ADA[4 + h])
                head(h)

            yv = uT.rearrange("p j t -> p (j t)")
            dve.wait_ge(y_read, 4)
            chain(tt(gt_, yv, yv, ALU.mult))
            chain(ts(gt_, gt_, 0.044715, 1.0, ALU.mult, ALU.add))
            tt(gt_, gt_, yv, ALU.mult).then_inc(gelu_in, 1)
            dve.wait_ge(gelu_th, 1)
            stt(yv, gt_, 1.0, yv, ALU.add, ALU.mult).then_inc(gelu_out, 1)
            dve.wait_ge(act_emptied, emptied(FILL[("glu", 3)])[1])
            stt(gv, gt_, 1.0, gv, ALU.add, ALU.mult).then_inc(glu_ready, 1)
            dve.wait_ge(act_emptied, emptied(FILL[("ao", 3)])[1])
            chain(stt(ao_flat, ta_flat, 1.0, ao_flat, ALU.add, ALU.mult))
            for b in range(4):
                f = FILL[("so", b)]
                v = slice(512 * b, 512 * b + 512)
                dve.wait_ge(fill_done, f + 1)
                stt(qk_flat[:, v], qk_flat[:, v], 1.0, bank[4 + f % 2][:, :], ALU.add, ALU.mult).then_inc(dve_emptied, 1)
                dve.wait_ge(dve_emptied, emptied(f)[1])
                stt(ao_flat[:, v], qk_flat[:, v], 0.25, ao_flat[:, v], ALU.mult, ALU.add).then_inc(merged_ready, 1)
            empty_ada("gt2a")
            empty_ada("gt2b")

            dve.wait_ge(x_again, 16 * TT)
            for a in range(TT):
                dve.wait_ge(rstd_ready, TT + a + 1)
                chain(stt(y_sb[:, a, :], y_sb[:, a, :], rstd[:, a:a + 1], row_g[:, :], ALU.mult, ALU.mult))
                tt(xs[:, a, :], xs[:, a, :], y_sb[:, a, :], ALU.add).then_inc(x1_ready, 1)
            dve.wait_ge(dve_emptied, emptied(FILL[("gt2b", 0)])[1])
            for a in range(TT):
                dve.wait_ge(rstd_ready, 2 * TT + a + 1)
                chain(stt(h2[:, a, :], xs[:, a, :], rstd[:, a:a + 1], row_a[:, :], ALU.mult, ALU.mult))
                tt(h2[:, a, :], h2[:, a, :], row_b[:, :], ALU.add).then_inc(normed, 1)
            dve.wait_ge(logit_done, 1)
            chain(dve.tensor_copy(lgr.rearrange("p a e -> p (a e)"), bank[0][:, 0:2 * NE]))
            for a in range(TT):
                chain(dve.max(top[:, a, :], lgr[:, a, :]))
            V.settle()
            for a in range(TT):
                chain(dve.max_index(idx[:, a, :], top[:, a, :], lgr[:, a, :]))
                last = ts(ms2[:, a:a + 1], top[:, a, 0:1], -1.0, None, ALU.mult)
            last.then_inc(top_ready, 1)
            V.settle()
            chain(dve.tensor_copy(idf.rearrange("p a e -> p (a e)"), idx[:, :, :].rearrange("p a e -> p (a e)")))
            dve.wait_ge(topexp, 2)
            chain(dve.reciprocal(m2[:, 0:2], sums))
            for a in range(TT):
                chain(ts(topx[:, a, 0:TOPK], topx[:, a, 0:TOPK], m2[:, a:a + 1], None, ALU.mult))
                for j in range(TOPK):
                    key = idf[:, a, j:j + 1]
                    if j == 0:
                        chain(ts(msk[:, a, :], iota[:, 0:NE], key, None, ALU.is_equal))
                        chain(ts(gat[:, a, :], iota[:, 0:NE], key, topx[:, a, 0:1], ALU.is_equal, ALU.mult))
                    else:
                        chain(stt(msk[:, a, :], iota[:, 0:NE], key, msk[:, a, :], ALU.is_equal, ALU.add))
                        chain(ts(one_hot, iota[:, 0:NE], key, topx[:, a, j:j + 1], ALU.is_equal, ALU.mult))
                        chain(tt(gat[:, a, :], gat[:, a, :], one_hot, ALU.add))
            dve.sem_inc(mask_ready, 1)
            dve.wait_ge(rank_done, 1)
            V.do(dve.memset(gate_of, 0.0))
            V.do(dve.memset(row_of, NOWHERE))
            V.do(dve.memset(pickT, 0.0))
            chain(dve.memset(y_e, 0.0))
            for a in range(TT):
                chain(ts(row_of[:, a, 0:NE], msk[:, a, :], -NOWHERE, NOWHERE, ALU.mult, ALU.add))
                chain(tt(row_of[:, a, 0:NE], row_of[:, a, 0:NE], bank[1][:, a * NE:(a + 1) * NE], ALU.add))
                V.do(ts(row_of[:, a, NE:2 * NE], row_of[:, a, 0:NE], -float(CAP), None, ALU.add))
                V.do(ts(gate_of[:, a, 0:NE], gat[:, a, :], 0.5, None, ALU.mult))
                V.do(ts(gate_of[:, a, NE:2 * NE], gat[:, a, :], 0.5, None, ALU.mult))
            chain(dve.reduce_max(m1[:, 0:1], bank[1][:, 2 * NE:3 * NE], AX))
            ts(flag[:, :], m1[:, 0:1], float(CAP), None, ALU.is_gt).then_inc(route_ready, 1)
            dve.wait_ge(b2_done, 1)
            for q in range(4):
                last = dve.tensor_copy(acc[:, q // 2, 512 * (q % 2):512 * (q % 2) + 512], bank[4 + q][:, :])
                V.do(last)
            V.settle()
            dve.sem_inc(pickT_ready, 1)
            dve.sem_inc(ye_ready, 1)
            dve.sem_inc(acc_init, 1)

            def rows_of(i):
                for a in range(TT):
                    last = ts(pick[:, a, :], iota, row_of[:, a, bass.ds(i, 1)], None, ALU.is_equal)
                last.then_inc(pick_ready, 1)

            def swiglu(i, half):
                dve.wait_ge(up_done, 4 * i + 2 * half + 2)
                ts(g_c, bank[2 * half][:, :], LIMIT, None, ALU.min).then_inc(g_ready, 1)
                V.do(ts(u_c, bank[2 * half + 1][:, :], LIMIT, -LIMIT, ALU.min, ALU.max))
                dve.wait_ge(g_ready, 2 * i + half + 1)
                V.settle()
                chain(stt(u_c, u_c, 1.0, g_c, ALU.add, ALU.mult))
                dve.wait_ge(gate_th, 2 * i + half + 1)
                stt(act_t[:, 512 * half:512 * half + 512], th_c, 1.0, u_c, ALU.add, ALU.mult).then_inc(act_ready, 1)
                dve.wait_ge(act_ready, 2 * i + half + 1)

            def add_up(i):
                for q in range(4):
                    v = acc[:, q // 2, 512 * (q % 2):512 * (q % 2) + 512]
                    dve.wait_ge(comb_done, 4 * i + q + 5)
                    tt(v, v, bank[(2, 3, 6, 7)[q]][:, :], ALU.add).then_inc(acc_done, 1)

            PER = 4

            def expert(i, e, before):
                V.at = start + i * PER
                V.n = 0
                dve.tensor_copy(sel, ident[0:NE, bass.ds(e, 1)].broadcast_to([NE, P])).then_inc(sel_ready, 1)
                swiglu(i, 0)
                if before:
                    add_up(i - 1)
                dve.wait_ge(gather_done, i + 1)
                rows_of(i + 1)
                for a in range(TT):
                    last = ts(pickg[:, a, :], iota, row_of[:, a, bass.ds(i, 1)], gate_of[:, a, bass.ds(i, 1)],
                              ALU.is_equal, ALU.mult)
                last.then_inc(pickg_ready, 1)
                swiglu(i, 1)
                assert V.n == PER, V.n

            rows_of(0)
            start = V.n
            with dve.Fori(0, NE) as i:
                expert(i, i, True)
            add_up(NE - 1)
            dve.wait_ge(route_ready, 1)
            more = dve.value_load(flag[0:1, 0:1], min_val=0, max_val=1)
            with dve.If(more > 0):
                with dve.Fori(NE, 2 * NE) as i:
                    expert(i, i - NE, False)
                    add_up(i)
            dve.drain()
            dve.sem_inc(normed, TT)
            for a in range(TT):
                dve.wait_ge(rstd_ready, 3 * TT + a + 1)
                stt(acc[:, a, :], acc[:, a, :], rstd[:, a:a + 1], row_g2, ALU.mult, ALU.mult).then_inc(acc_init, 1)
                dve.wait_ge(acc_init, 2 + a)
                tt(xs[:, a, :], xs[:, a, :], acc[:, a, :], ALU.add).then_inc(out_ready, 1)


_INS = ["x", "c", "rel_bias", "w_ada", "b_ada", "g_pre_mix", "g_post_mix", "g_pre_ffn", "g_post_ffn", "w_in",
        "ssm_a_re", "ssm_a_im", "ssm_log_dt", "ssm_b_re", "ssm_b_im", "ssm_c_re", "ssm_c_im", "ssm_d", "w_glu",
        "w_ssm_out", "w_att_out", "w_out", "w_router", "b_router", "w_exp_in", "b_exp_in", "w_exp_out", "b_exp_out"]


def kernel(**inputs):
    import concourse.bacc as _bacc
    from concourse.bass_utils import run_bass_kernel_spmd as _run

    nc = _bacc.Bacc("TRN2", target_bir_lowering=False, num_devices=1)
    arrays, args = {}, []
    for name in _INS:
        a = np.ascontiguousarray(inputs[name])
        arrays[f"in_{name}"] = a
        args.append(nc.dram_tensor(f"in_{name}", a.shape, mybir.dt.from_np(a.dtype), kind="ExternalInput").ap())
    arrays["in_const"] = constants()
    args.append(nc.dram_tensor("in_const", (P, C_N), F32, kind="ExternalInput").ap())
    args.append(nc.dram_tensor("bias_line", (HEADS, N_HOT), F32, kind="Internal").ap())
    args.append(nc.dram_tensor("bias_rows", (HEADS, P, 512), F32, kind="Internal").ap())
    args.append(nc.dram_tensor("out_0", (1, T, D), F32, kind="ExternalOutput").ap())
    build(nc, *args)
    r = _run(nc, [arrays], core_ids=[0])
    return r.results[0]["out_0"]
```

```python
from contextlib import ExitStack
import math

import numpy as np

import concourse.bass as bass
from concourse import mybir

F32 = mybir.dt.float32
F32R = mybir.dt.float32r
I32 = mybir.dt.int32
U32 = mybir.dt.uint32
ALU = mybir.AluOpType
ACT = mybir.ActivationFunctionType
AX = mybir.AxisListType.X

P = 128
D = 1024
T = 256
TT = T // P
KD = D // P
HEADS, HD = 8, 64
AW = HEADS * HD
SW = D // 2
KS = SW // P
GROUPS, GC, GP = 32, 16, 64
ST = GROUPS * GP // P
BUCKETS, MAX_DIST = 32, 128
NE, TOPK, FF = 32, 4, 1024
CAP = P
LIMIT, ALPHA = 7.0, 1.702
EPS = 1e-6
MASKED = -1.0e30
NOWHERE = 1000.0
GELU_C = math.sqrt(2.0 / math.pi)
ROUND = 12582912.0

C_ID, C_ONE, C_TRI, C_IOTA = 0, P, 2 * P, 3 * P
C_EVEN = 4 * P
C_ODD = C_EVEN + 1
C_HOT = C_ODD + 1
N_HOT = 2 * T - 1
C_N = C_HOT + N_HOT

MIX = (["sh1a", "sh1b", "sc1a", "sc1b", "u", "q", "k", "v", "ga0", "ga1",
        "gt1a", "gt1b", "sh2a", "sh2b", "sc2a", "sc2b", "gs0", "gs1", "glu", "ao", "so",
        "gt2a", "gt2b", "wo0", "wo1"])
ADA = ["sh1a", "sh1b", "sc1a", "sc1b", "gt1a", "gt1b", "sh2a", "sh2b", "sc2a", "sc2b", "gt2a", "gt2b"]
G_USERS = [n for n in ADA if n[:2] != "sh"]
ADA_COL = {n: 512 * (2 * ["sh1", "sc1", "gt1", "sh2", "sc2", "gt2"].index(n[:3]) + (n[3] == "b")) for n in ADA}
MIX_SLOTS = 4
PW = 4096
HALVES = 12
HW = 2048
SLOTS = 4
POOL_SLOT = 3
USES = HALVES // SLOTS

FILLS = []
for name in MIX:
    if name in ADA:
        FILLS.append((name, 0, "dve"))
    elif name in ("glu", "ao"):
        FILLS += [(name, b, "act") for b in range(4)]
    elif name == "so":
        FILLS += [(name, b, "dve") for b in range(4)]
    else:
        FILLS += [(name, b, "act") for b in range(2)]
FILL = {(name, b): f for f, (name, b, _) in enumerate(FILLS)}


def used_up(n):
    return 1 + max(f for f, (name, _, _) in enumerate(FILLS) if name == MIX[n])


def emptied(f):
    who = FILLS[f][2]
    return who, sum(x[2] == who for x in FILLS[:f + 1])


def constants():
    c = np.zeros((P, C_N), np.float32)
    c[:, C_ID:C_ID + P] = np.eye(P)
    c[:, C_ONE:C_ONE + P] = 1.0
    c[:, C_TRI:C_TRI + P] = np.triu(np.ones((P, P)), 1)
    c[:, C_IOTA:C_IOTA + P] = np.arange(P)[None, :]
    exact = BUCKETS // 2
    for j in range(N_HOT):
        dist = T - 1 - j
        if dist < 0:
            c[BUCKETS, C_HOT + j] = 1.0
            continue
        large = exact + int(np.float32(np.log(np.float32(max(dist, 1)) / np.float32(exact)))
                            / np.float32(math.log(MAX_DIST / exact)) * np.float32(BUCKETS - exact))
        c[dist if dist < exact else min(large, BUCKETS - 1), C_HOT + j] = 1.0
    even = (np.arange(P) // GC) % 2 == 0
    c[:, C_EVEN] = even
    c[:, C_ODD] = ~even
    return c


class Steps:

    def __init__(self, eng, sem):
        self.eng, self.sem, self.n, self.at = eng, sem, 0, 0

    def do(self, ins):
        ins.then_inc(self.sem, 1)
        self.n += 1

    def settle(self):
        self.eng.wait_ge(self.sem, self.at + self.n)


def build(nc, x, c, rel_bias, w_ada, b_ada, g_pre_mix, g_post_mix, g_pre_ffn, g_post_ffn, w_in,
          ssm_a_re, ssm_a_im, ssm_log_dt, ssm_b_re, ssm_b_im, ssm_c_re, ssm_c_im, ssm_d, w_glu,
          w_ssm_out, w_att_out, w_out, w_router, b_router, w_exp_in, b_exp_in, w_exp_out, b_exp_out,
          const, bias_line, bias_rows, out):
    ctx = ExitStack()
    with ctx:
        def sb(name, shape, dt=F32):
            return ctx.enter_context(nc.sbuf_tensor(name, shape, dt))

        def sem(name):
            return ctx.enter_context(nc.semaphore(name))

        cst = sb("cst", [P, C_HOT])
        xs = sb("xs", [P, TT, D])
        hT = sb("hT", [P, KD, T])
        row_a = sb("row_a", [P, D])
        row_b = sb("row_b", [P, D])
        row_g = sb("row_g", [P, D])
        small = sb("small", [P, 640])
        flag = sb("flag", [P, 8], I32)
        idx = sb("idx", [P, TT, 8], U32)
        with ExitStack() as mixer:
            ring = mixer.enter_context(nc.sbuf_tensor("ring", [P, MIX_SLOTS + 2, PW], F32))
            work = mixer.enter_context(nc.sbuf_tensor("work", [P, 19712], F32))
        w_hi = sb("w_hi", [P, SLOTS, HW], F32R)
        w_lo = sb("w_lo", [P, SLOTS, HW], F32R)
        w_raw = sb("w_raw", [P, SLOTS, HW])
        h2_hi, h2_lo = sb("h2_hi", [P, TT, D], F32R), sb("h2_lo", [P, TT, D], F32R)
        b1_hl = sb("b1_hl", [2 * NE, 2 * FF], F32R)
        xe_hi, xe_lo = sb("xe_hi", [P, KD, P], F32R), sb("xe_lo", [P, KD, P], F32R)
        aT_hi, aT_lo = sb("aT_hi", [P, KD, P], F32R), sb("aT_lo", [P, KD, P], F32R)
        y_hi, y_lo = sb("y_hi", [P, D], F32R), sb("y_lo", [P, D], F32R)
        pick = sb("pick", [P, TT, P], F32R)
        pick_t = sb("pick_t", [P, TT, P], F32R)
        pickT = sb("pickT", [P, T], F32R)
        sel = sb("sel", [2 * NE, P], F32R)
        ident_r = sb("ident_r", [P, P], F32R)
        gate_hl = sb("gate_hl", [P, TT, 2 * NE, 2], F32R)
        route = sb("route", [P, 704])
        gap = sb("gap", [P, 15104 - 14272])
        sb("row_g2_place", [P, D])
        tail = sb("tail", [P, 3072])
        psum = ctx.enter_context(nc.psum_tensor("psum", [P, 8, 512], F32))
        bank = [psum[:, i, :] for i in range(8)]
        bu_re, bu_im = psum[:, 0:2, 0:T], psum[:, 0:2, T:2 * T]

        at = [0]

        def carve(n, where=None):
            start = at[0] if where is None else where
            if where is None:
                at[0] += n
                assert at[0] <= 19712
            return work[:, start:start + n]

        ident = cst[:, C_ID:C_ID + P]
        ones = cst[:, C_ONE:C_ONE + P]
        tri = cst[:, C_TRI:C_TRI + P]
        iota = cst[:, C_IOTA:C_IOTA + P]

        uT = carve(1024).rearrange("p (j t) -> p j t", j=KS)
        qk_flat = carve(2048)
        qT = qk_flat[:, 0:1024].rearrange("p (j t) -> p j t", j=4)
        kT = qk_flat[:, 1024:2048].rearrange("p (j t) -> p j t", j=4)
        gs_t = qk_flat.rearrange("p (j t) -> p j t", j=KD)
        vv = carve(1024).rearrange("p (a n) -> p a n", a=TT)
        attT = carve(1024).rearrange("p (j t) -> p j t", j=4)
        ta_flat = carve(2048)
        ga_t = ta_flat.rearrange("p (j t) -> p j t", j=KD)
        ao_flat = carve(2048)
        aoT = ao_flat.rearrange("p (j t) -> p j t", j=KD)
        ssm_flat = carve(3584)
        zr, zi, tp = (ssm_flat[:, 512 * n:512 * n + 512] for n in range(3))
        xre = [ssm_flat[:, 1536 + 1024 * n:2048 + 1024 * n] for n in range(2)]
        xim = [ssm_flat[:, 2048 + 1024 * n:2560 + 1024 * n] for n in range(2)]
        attn_flat = carve(2304)
        bias_m = [attn_flat[:, 384 * n:384 * n + 384] for n in range(2)]
        lg_m = [attn_flat[:, 768 + 384 * n:1152 + 384 * n] for n in range(2)]
        pt_m = [attn_flat[:, 1536 + 384 * n:1920 + 384 * n] for n in range(2)]
        btct = carve(2048)
        BT = btct[:, 0:1024].rearrange("p (r j s) -> p r j s", r=2, j=4)
        CT = btct[:, 1024:2048].rearrange("p (r j s) -> p r j s", r=2, j=4)
        row_g2 = btct[:, 0:1024]
        bada = carve(1024).rearrange("p (b n) -> p b n", b=2)
        grow = carve(512)
        cond_b = carve(1024).rearrange("p (k m) -> p k m", k=KD)
        b_in = qk_flat[:, 0:512].rearrange("p (r s c) -> p r s c", r=2, s=ST)
        b_bar = qk_flat[:, 512:1536].rearrange("p (r s c) -> p r s c", r=2, s=ST)
        b_tmp = qk_flat[:, 1536:1792].rearrange("p (s c) -> p s c", s=ST)
        b_tmp2 = qk_flat[:, 1792:2048].rearrange("p (s c) -> p s c", s=ST)
        c_in = ssm_flat[:, 0:512].rearrange("p (r j s) -> p r j s", r=2, j=4)
        c_pad = ssm_flat[:, 512:1536].rearrange("p (r j s) -> p r j s", r=2, j=4)
        tab_c = ring[:, MIX_SLOTS, :].rearrange("p (s t) -> p s t", s=ST)
        tab_s = ring[:, MIX_SLOTS + 1, :].rearrange("p (s t) -> p s t", s=ST)
        tab_1 = ta_flat.rearrange("p (s t) -> p s t", s=ST)
        tab_2 = ao_flat.rearrange("p (s t) -> p s t", s=ST)
        vrow = attn_flat[0:64, 0:P]
        ldt_in = attn_flat[0:ST, 140:142]
        relb = attn_flat[0:BUCKETS + 1, 128:128 + HEADS]
        bline = attn_flat[0:HEADS, 256:256 + N_HOT]
        junk = ssm_flat[:, 2304:3328]
        hot = ssm_flat[0:BUCKETS + 1, 1600:1600 + N_HOT]
        gv = ssm_flat[:, 0:1024]
        gt_ = ssm_flat[:, 1024:2048]
        gluT = gv.rearrange("p (j t) -> p j t", j=KS)
        rT = ta_flat.rearrange("p (k t) -> p k t", k=KD)
        y_sb = qk_flat.rearrange("p (a n) -> p a n", a=TT)
        acc = hT[:, :, :].rearrange("p k t -> p (k t)").rearrange("p (a n) -> p a n", a=TT)
        g_c, u_c, th_c = row_a[:, 0:512], row_a[:, 512:1024], row_b[:, 0:512]
        act_t = row_g[:, :]
        ro = [0]

        def routing(n):
            ro[0] += n
            assert ro[0] <= 704
            return route[:, ro[0] - n:ro[0]]

        wr = routing(256).rearrange("p (k e) -> p k e", k=KD)
        row_of = routing(130).rearrange("p (a e) -> p a e", a=TT)
        gT = routing(T)[0:NE, :]
        br = routing(NE)[0:1, :]
        sel_table = row_b[0:2 * NE, 512:512 + NE + 1]
        b1_raw = tail[0:2 * NE, 0:2 * FF]
        b2all = tail[0:NE, 2 * FF:2 * FF + D]
        h2 = hT[:, :, :].rearrange("p k t -> p (k t)").rearrange("p (a n) -> p a n", a=TT)

        sm = [0]

        def little(n):
            sm[0] += n
            assert sm[0] <= 640
            return small[:, sm[0] - n:sm[0]]

        vcol = little(60)
        ldt, cond_c, dcol = vcol[:, 0:16], vcol[:, 16:24], vcol[:, 24:28]
        are, aim = vcol[:, 28:44], vcol[:, 44:60]
        ss = little(2)
        ms = little(2)
        rstd = little(2)
        nhalf = little(2)
        lam, theta, rho, ec, es, zre, zim, m1, m2, m3, m4 = (little(16) for _ in range(11))
        gate_s = little(1)
        two_gates = little(2)
        mx = little(2)
        sums = little(2)
        lgr = little(64).rearrange("p (a e) -> p a e", a=TT)
        msk = little(64).rearrange("p (a e) -> p a e", a=TT)
        gat = little(64).rearrange("p (a e) -> p a e", a=TT)
        one_hot = little(32)
        top = little(16).rearrange("p (a e) -> p a e", a=TT)
        topx = little(16).rearrange("p (a e) -> p a e", a=TT)
        idf = little(16).rearrange("p (a e) -> p a e", a=TT)
        ms2 = little(2)

        slot_in = [sem(f"slot_in{s}") for s in range(MIX_SLOTS)]
        raw_in = [sem(f"raw_in{s}") for s in range(SLOTS)]
        lo_ready = [sem(f"lo_ready{s}") for s in range(SLOTS)]
        hi_ready, w_used = sem("hi_ready"), sem("w_used")
        const_in, vec_in, x_in, param_in, x_again = sem("const_in"), sem("vec_in"), sem("x_in"), sem("param_in"), sem("x_again")
        bada_in = [sem("bada_in0"), sem("bada_in1")]
        grow_in = sem("grow_in")
        bias_out, bias_in = sem("bias_out"), [sem("bias_in0"), sem("bias_in1")]
        moe_in = sem("moe_in")
        fill_done, dve_emptied, act_emptied = sem("fill_done"), sem("dve_emptied"), sem("act_emptied")
        emptied_sem = {"dve": dve_emptied, "act": act_emptied}
        v_step, a_step, g_step = sem("v_step"), sem("a_step"), sem("g_step")
        relb_ready, vrow_ready = sem("relb_ready"), sem("vrow_ready")
        vrow_turned, vcol_ready, cond_ready = sem("vrow_turned"), sem("vcol_ready"), sem("cond_ready")
        dt_ready, theta_ready, sine_ready, gauss = sem("dt_ready"), sem("theta_ready"), sem("sine_ready"), sem("nhalf_ready")
        bc_padded, bc_turned, bc_ready = sem("bc_padded"), sem("bc_turned"), sem("bc_ready")
        bline_done, bline_ready = sem("bline_done"), sem("bline_ready")
        squares, rstd_ready, normed = sem("squares"), sem("rstd_ready"), sem("normed")
        h_turned, hT_ready, rT_ready = sem("h_turned"), sem("hT_ready"), sem("rT_ready")
        bu_done, bu_read, x_ready, y_done = sem("bu_done"), sem("bu_read"), sem("x_ready"), sem("y_done")
        y_read = sem("y_read")
        s_done, logits_ready, exp_done, probs_ready, p_turned, pT_ready = (
            sem("s_done"), sem("logits_ready"), sem("exp_done"), sem("probs_ready"), sem("p_turned"), sem("pT_ready"))
        pv_done, att_ready, max_ready = sem("pv_done"), sem("att_ready"), sem("max_ready")
        gelu_in, gelu_th, gelu_out = sem("gelu_in"), sem("gelu_th"), sem("gelu_out")
        glu_ready, merged_ready = sem("glu_ready"), sem("merged_ready")
        x1_ready = sem("x1_ready")
        logit_done, top_ready, topexp, mask_ready, rank_done, route_ready = (
            sem("logit_done"), sem("top_ready"), sem("topexp"), sem("mask_ready"), sem("rank_done"), sem("route_ready"))
        gates_turned, gT_ready, b2_done, acc_init = sem("gates_turned"), sem("gT_ready"), sem("b2_done"), sem("acc_init")
        sel_ready, pick_ready, pick_t_ready = sem("sel_ready"), sem("pick_ready"), sem("pick_t_ready")
        h2_hi_ready, h2_ready, b1_hi_ready, b1_ready = sem("h2_hi_ready"), sem("h2_ready"), sem("b1_hi_ready"), sem("b1_ready")
        up_done, g_ready, gate_th, act_ready = sem("up_done"), sem("g_ready"), sem("gate_th"), sem("act_ready")
        gather_hi, gather_lo, xe_hi_ready, xe_ready = sem("gather_hi"), sem("gather_lo"), sem("xe_hi_ready"), sem("xe_ready")
        act_turned, aT_hi_ready, aT_ready = sem("act_turned"), sem("aT_hi_ready"), sem("aT_ready")
        pick_turned, pickT_ready = sem("pick_turned"), sem("pickT_ready")
        y_hi_ready, ye_ready = sem("y_hi_ready"), sem("ye_ready")
        comb_done, acc_done = sem("comb_done"), sem("acc_done")
        out_ready, stored = sem("out_ready"), sem("stored")

        def broadcast(vec, n0, n1):
            return vec[0:1, n0:n1].broadcast_to([P, n1 - n0])

        def moe_source(e, hs):
            if hs < 8:
                which, rows = hs // 2, 512 * (hs % 2)
                col = 512 * (which // 2) + FF * (which % 2)
                return w_exp_in[0][bass.ds(e, 1), rows:rows + 512, col:col + 512].rearrange(
                    "o (k p) n -> (o p) k n", p=P)
            rows = 256 * (hs - 8)
            return w_exp_out[0][bass.ds(e, 1), rows:rows + 256, :].rearrange("o (k p) n -> (o p) k n", p=P)

        def slot(s, k):
            return ring[:, s, :].rearrange("p (k n) -> p k n", k=k)

        block = ctx.enter_context(nc.Block())

        @block.sync
        def _(sp):
            def source(name):
                if name in ADA:
                    return w_ada[0][:, ADA_COL[name]:ADA_COL[name] + 512], 8
                if name == "glu":
                    return w_glu[0], 4
                if name == "ao":
                    return w_att_out[0], 4
                if name == "so":
                    return w_ssm_out[0], 4
                if name in ("wo0", "wo1"):
                    n = 512 * int(name[2])
                    return w_out[0][:, n:n + 512], 8
                col = {"q": 0, "k": 1, "v": 2, "u": 3, "ga0": 4, "ga1": 5, "gs0": 6, "gs1": 7}[name] * 512
                return w_in[0][:, col:col + 512], 8

            sp.dma_start(cst[:, :], const[:, 0:C_HOT]).then_inc(const_in, 16)
            sp.dma_start(hot, const[0:BUCKETS + 1, C_HOT:C_N]).then_inc(const_in, 16)
            for n, name in enumerate(MIX):
                s = n % MIX_SLOTS
                if n >= MIX_SLOTS:
                    sp.wait_ge(fill_done, used_up(n - MIX_SLOTS))
                src, k = source(name)
                sp.dma_start(slot(s, k), src.rearrange("(k p) n -> p k n", p=P)).then_inc(slot_in[s], 16)

            def load(e, hs):
                sp.dma_start(w_raw[:, hs % SLOTS, :].rearrange("p (k n) -> p k n", k=4 if hs < 8 else 2),
                             moe_source(e, hs)).then_inc(raw_in[hs % SLOTS], 16)

            def stream(i0, i1, e0):
                with sp.Fori(i0, i1 - 1) as i:
                    for hs in range(SLOTS, HALVES + SLOTS):
                        sp.wait_ge(lo_ready[hs % SLOTS], i * USES + hs // SLOTS)
                        load(i - e0 if hs < HALVES else i - e0 + 1, hs % HALVES)
                for hs in range(SLOTS, HALVES):
                    sp.wait_ge(lo_ready[hs % SLOTS], (i1 - 1) * USES + hs // SLOTS)
                    load(i1 - 1 - e0, hs)

            sp.wait_ge(x_ready, 8)
            for hs in range(SLOTS):
                load(0, hs)
            stream(0, NE, 0)
            sp.wait_ge(route_ready, 1)
            more = sp.value_load(flag[0:1, 0:1], min_val=0, max_val=1)
            with sp.If(more > 0):
                for hs in range(SLOTS):
                    sp.wait_ge(lo_ready[hs], NE * USES)
                    load(0, hs)
                stream(NE, 2 * NE, NE)
            for a in range(TT):
                sp.wait_ge(out_ready, a + 1)
                sp.dma_start(out[0, a * P:(a + 1) * P, :], xs[:, a, :]).then_inc(stored, 16)
            sp.wait_ge(stored, 16 * TT)

        @block.gpsimd
        def _(pool):
            pool.dma_start(vrow[16:24, :], c.rearrange("o (k p) -> (o k) p", p=P)).then_inc(vec_in, 16)
            pool.dma_start(vrow[24:28, :], ssm_d.rearrange("o (k p) -> (o k) p", p=P)).then_inc(vec_in, 16)
            pool.dma_start(vrow[28:44, :], ssm_a_re[0].rearrange("(s a) p -> s (a p)", a=2)).then_inc(vec_in, 16)
            pool.dma_start(vrow[44:60, :], ssm_a_im[0].rearrange("(s a) p -> s (a p)", a=2)).then_inc(vec_in, 16)
            pool.dma_start(ldt_in, ssm_log_dt[0].rearrange("(s a) -> s a", a=2)).then_inc(vec_in, 16)
            for a in range(TT):
                pool.dma_start(xs[:, a, :], x[0, a * P:(a + 1) * P, :]).then_inc(x_in, 16)
            
            def ada_bias(n):
                name = ADA[n]
                if n >= 2:
                    pool.wait_ge(dve_emptied, emptied(FILL[(ADA[n - 2], 0)])[1])
                pool.dma_start(bada[:, n % 2, :], broadcast(b_ada, ADA_COL[name], ADA_COL[name] + 512)
                               ).then_inc(bada_in[n % 2], 16)
                if name in G_USERS:
                    m = G_USERS.index(name)
                    if m:
                        pool.wait_ge(dve_emptied, emptied(FILL[(G_USERS[m - 1], 0)])[1])
                    g = {"sc1": g_pre_mix, "gt1": g_post_mix, "sc2": g_pre_ffn, "gt2": g_post_ffn}[name[:3]]
                    pool.dma_start(grow, broadcast(g, 512 * (m % 2), 512 * (m % 2) + 512)).then_inc(grow_in, 16)

            ada_bias(0)
            ada_bias(1)
            for r, b in enumerate((ssm_b_re, ssm_b_im)):
                pool.dma_start(b_in[:, r, :, :], b[0].rearrange("(s a) p c -> (a p) s c", a=2)).then_inc(param_in, 16)
            for r, cc in enumerate((ssm_c_re, ssm_c_im)):
                pool.dma_start(c_in[:, r, :, :], cc[0].rearrange("(j g) c p -> (g c) j p", j=4)).then_inc(param_in, 16)
            pool.memset(relb, MASKED).then_inc(g_step, 1)
            pool.wait_ge(g_step, 1)
            pool.dma_start(relb[0:BUCKETS, :], rel_bias).then_inc(relb_ready, 16)
            pool.memset(nhalf, -0.5).then_inc(g_step, 1)
            pool.wait_ge(g_step, 2)
            steps = [2]

            def root(n, bias, slot_n):
                pool.wait_ge(squares, slot_n + 1)
                pool.tensor_scalar(ms[:, n:n + 1], ss[:, n:n + 1], 1.0 / D, bias, ALU.mult, ALU.add).then_inc(g_step, 1)
                steps[0] += 1
                pool.wait_ge(g_step, steps[0])
                pool.tensor_tensor(rstd[:, n:n + 1], ms[:, n:n + 1], nhalf[:, 0:1], ALU.pow).then_inc(rstd_ready, 1)

            for n in range(TT):
                root(n, EPS, n)
            for n in range(2, 4):
                ada_bias(n)
            pool.wait_ge(bline_ready, 1)
            pool.dma_start(bias_line, bline).then_inc(bias_out, 16)
            pool.wait_ge(bias_out, 16)
            pool.dma_start(bias_rows[:, :, 0:N_HOT],
                           bias_line.rearrange("h (o n) -> h o n", o=1).broadcast_to([HEADS, P, N_HOT])
                           ).then_inc(bias_out, 16)
            pool.wait_ge(bias_out, 32)

            def bias_matrix(h):
                if h >= 2:
                    pool.wait_ge(logits_ready, h - 1)
                else:
                    pool.wait_ge(vcol_ready, 1)
                for a, (lo, hi) in enumerate(((0, P), (P, 3 * P))):
                    src = bass.AP(tensor=bias_rows.tensor, offset=h * P * 512 + T - 1 - a * P,
                                  ap=[[511, P], [1, hi - lo]])
                    pool.dma_start(bias_m[h % 2][:, lo:hi], src).then_inc(bias_in[h % 2], 16)

            bias_matrix(0)
            bias_matrix(1)
            ada_bias(4)
            ada_bias(5)
            bias_matrix(2)
            ada_bias(6)
            bias_matrix(3)
            ada_bias(7)
            bias_matrix(4)
            ada_bias(8)
            bias_matrix(5)
            ada_bias(9)
            bias_matrix(6)
            bias_matrix(7)
            ada_bias(10)
            ada_bias(11)
            pool.wait_ge(h_turned, 4)
            for a in range(TT):
                pool.dma_start(xs[:, a, :], x[0, a * P:(a + 1) * P, :]).then_inc(x_again, 16)
            for n in range(TT):
                root(n, 4.0 * EPS, 2 + n)
            pool.wait_ge(x1_ready, TT)
            for r in range(2):
                pool.dma_start(b1_raw[r * NE:(r + 1) * NE, :], b_exp_in[0]).then_inc(moe_in, 16)
            pool.dma_start(b2all, b_exp_out[0]).then_inc(moe_in, 16)
            pool.dma_start(wr, w_router[0].rearrange("(k p) e -> p k e", p=P)).then_inc(moe_in, 16)
            pool.dma_start(br[:, :], b_router).then_inc(moe_in, 16)
            for n in range(TT):
                root(n, EPS, 4 + n)

            def low_parts(i):
                for hs in range(POOL_SLOT, HALVES, SLOTS):
                    pool.wait_ge(hi_ready, i * HALVES + (hs + 1))
                    pool.tensor_tensor(w_lo[:, POOL_SLOT, :], w_raw[:, POOL_SLOT, :], w_hi[:, POOL_SLOT, :].bitcast(F32),
                                       ALU.subtract).then_inc(lo_ready[POOL_SLOT], 1)

            with pool.Fori(0, NE) as i:
                low_parts(i)
            pool.wait_ge(route_ready, 1)
            more = pool.value_load(flag[0:1, 0:1], min_val=0, max_val=1)
            with pool.If(more > 0):
                with pool.Fori(NE, 2 * NE) as i:
                    low_parts(i)
            for n in range(TT):
                root(n, EPS, 6 + n)

        @block.tensor
        def _(pe):
            seen = {s: 0 for s in range(MIX_SLOTS)}

            def arrive(name):
                n = MIX.index(name)
                pe.wait_ge(slot_in[n % MIX_SLOTS], 16 * (n // MIX_SLOTS + 1))
                return n % MIX_SLOTS

            def free_bank(f):
                if f >= 2:
                    who, count = emptied(f - 2)
                    pe.wait_ge(emptied_sem[who], count)
                return bank[4 + f % 2]

            pe.wait_ge(const_in, 32)
            pe.wait_ge(vec_in, 80)
            pe.wait_ge(vrow_ready, 1)
            pe.transpose(bank[3][:, 0:60], vrow[0:60, :], ident[0:60, 0:60]).then_inc(vrow_turned, 1)
            pe.wait_ge(relb_ready, 16)
            pe.matmul(bank[6][0:HEADS, 0:N_HOT], relb, hot,
                      start=True, stop=True).then_inc(bline_done, 1)

            def ada(name):
                s = arrive(name)
                f = FILL[(name, 0)]
                b = free_bank(f)
                w = slot(s, 8)
                for k in range(KD):
                    mm = pe.matmul(b[:, :], cond_b[:, k, :], w[:, k, :], start=k == 0, stop=k == KD - 1)
                mm.then_inc(fill_done, 1)

            def features(name, b, k_n, rhs):
                s = MIX.index(name) % MIX_SLOTS
                f = FILL[(name, b)]
                out_b = free_bank(f)
                w = slot(s, k_n)
                for m in range(2):
                    col = (2 * b + m) * P
                    for k in range(k_n):
                        mm = pe.matmul(out_b[:, m * T:(m + 1) * T], w[:, k, col:col + P], rhs[:, k, :],
                                       start=k == 0, stop=k == k_n - 1)
                mm.then_inc(fill_done, 1)

            def tokens(name, a, lhs):
                s = MIX.index(name) % MIX_SLOTS
                f = FILL[(name, a)]
                out_b = free_bank(f)
                w = slot(s, 8)
                for k in range(KD):
                    mm = pe.matmul(out_b[:, :], lhs[:, k, a * P:(a + 1) * P], w[:, k, :],
                                   start=k == 0, stop=k == KD - 1)
                mm.then_inc(fill_done, 1)

            pe.wait_ge(cond_ready, 1)
            for name in ADA[0:4]:
                ada(name)
            pe.wait_ge(bc_padded, 1)
            for r in range(2):
                for j in range(4):
                    mm = pe.transpose(bank[r][:, j * P:(j + 1) * P],
                                      b_bar[:, r, 4 * j:4 * j + 4, :].rearrange("p s c -> p (s c)"), ident)
            mm.then_inc(bc_turned, 1)
            pe.wait_ge(bc_padded, 2)
            pe.wait_ge(vcol_ready, 1)
            for r in range(2):
                for j in range(4):
                    mm = pe.transpose(bank[2 + r][:, j * P:(j + 1) * P], c_pad[:, r, j, :], ident)
            mm.then_inc(bc_turned, 1)
            for g in range(4):
                if g == 0:
                    pe.wait_ge(normed, TT)
                    pe.wait_ge(bline_ready, 1)
                if g >= 2:
                    pe.wait_ge(hT_ready, g - 1)
                for kk in range(2):
                    for a in range(TT):
                        k = 2 * g + kk
                        mm = pe.transpose(bank[6 + g % 2][:, kk * T + a * P:kk * T + (a + 1) * P],
                                          xs[:, a, k * P:(k + 1) * P], ident)
                mm.then_inc(h_turned, 1)
            pe.wait_ge(hT_ready, 4)
            arrive("u")
            for b in range(2):
                features("u", b, 8, hT)

            def inputs_to_states(n):
                if n == 0:
                    pe.wait_ge(bc_ready, 2)
                    pe.wait_ge(act_emptied, emptied(FILL[("u", 1)])[1])
                else:
                    pe.wait_ge(bu_read, n)
                for m in range(2):
                    st = 2 * n + m
                    j, q = st // 4, st % 4
                    for r in range(2):
                        mm = pe.matmul(bank[m][:, r * T:(r + 1) * T], BT[32 * q:32 * q + 32, r, j, :],
                                       uT[32 * q:32 * q + 32, j, :], start=True, stop=True,
                                       tile_position=(32 * q, 0))
                mm.then_inc(bu_done, 1)

            def states_to_outputs(n):
                pe.wait_ge(x_ready, n + 1)
                j = n // 2
                if n % 2 == 0 and j >= 1:
                    pe.wait_ge(y_read, j)
                for m in range(2):
                    st = 2 * n + m
                    q = st % 4
                    o = bank[2][32 * q:32 * q + 32, 0:T]
                    pe.matmul(o, CT[:, 0, j, 32 * q:32 * q + 32], xre[n % 2][:, m * T:(m + 1) * T],
                              start=True, stop=False, tile_position=(0, 32 * q))
                    mm = pe.matmul(o, CT[:, 1, j, 32 * q:32 * q + 32], xim[n % 2][:, m * T:(m + 1) * T],
                                   start=False, stop=True, tile_position=(0, 32 * q))
                mm.then_inc(y_done, 1)

            seq = [("q", 0), ("q", 1), ("k", 0), ("k", 1), ("v", 0), ("v", 1), ("ga0", 0), ("ga0", 1)]
            for n, (name, b) in enumerate(seq):
                inputs_to_states(n)
                if b == 0:
                    arrive(name)
                if name == "v":
                    tokens(name, b, hT)
                else:
                    features(name, b, 8, hT)
                if n >= 1:
                    states_to_outputs(n - 1)
            arrive("ga1")
            features("ga1", 0, 8, hT)
            states_to_outputs(7)
            features("ga1", 1, 8, hT)

            def scores(h):
                if h >= 2:
                    pe.wait_ge(pT_ready, h - 1)
                if h == 0:
                    pe.wait_ge(act_emptied, emptied(FILL[("v", 1)])[1])
                r = 64 * (h % 2)
                o = bank[6 + h % 2]
                for a in range(TT):
                    mm = pe.matmul(o[:, a * P:a * P + (a + 1) * P], qT[r:r + 64, h // 2, a * P:(a + 1) * P],
                                   kT[r:r + 64, h // 2, 0:(a + 1) * P], start=True, stop=True,
                                   tile_position=(r, 0))
                mm.then_inc(s_done, 1)

            scores(0)
            for h in range(HEADS):
                if h < HEADS - 1:
                    scores(h + 1)
                if h < 6:
                    ada(ADA[4 + h])
                pe.wait_ge(probs_ready, h + 1)
                for b in range(3):
                    mm = pe.transpose(bank[6 + h % 2][:, b * P:(b + 1) * P], lg_m[h % 2][:, b * P:(b + 1) * P], ident)
                mm.then_inc(p_turned, 1)
                pe.wait_ge(pT_ready, h + 1)
                if h % 2 == 0 and h >= 2:
                    pe.wait_ge(att_ready, h // 2)
                r = 64 * (h % 2)
                o = bank[3][r:r + 64, 0:T]
                pe.matmul(o, vv[:, 0, h * HD:(h + 1) * HD], pt_m[h % 2][:, 0:T], start=True, stop=False,
                          tile_position=(0, r))
                pe.matmul(o[:, P:T], vv[:, 1, h * HD:(h + 1) * HD], pt_m[h % 2][:, T:3 * P],
                          start=False, stop=True, tile_position=(0, r)).then_inc(pv_done, 1)
            for name in ("gs0", "gs1"):
                arrive(name)
                for b in range(2):
                    features(name, b, 8, hT)
            pe.wait_ge(gelu_out, 1)
            arrive("glu")
            for b in range(4):
                features("glu", b, 4, uT)
            pe.wait_ge(att_ready, 4)
            arrive("ao")
            for b in range(4):
                features("ao", b, 4, attT)
            pe.wait_ge(glu_ready, 1)
            arrive("so")
            for b in range(4):
                features("so", b, 4, gluT)
            ada("gt2a")
            ada("gt2b")
            pe.wait_ge(merged_ready, 4)
            for name in ("wo0", "wo1"):
                arrive(name)
                for a in range(TT):
                    tokens(name, a, aoT)

            for g in range(4):
                if g == 0:
                    pe.wait_ge(normed, 2 * TT)
                if g >= 2:
                    pe.wait_ge(rT_ready, g - 1)
                for kk in range(2):
                    for a in range(TT):
                        k = 2 * g + kk
                        mm = pe.transpose(bank[6 + g % 2][:, kk * T + a * P:kk * T + (a + 1) * P],
                                          h2[:, a, k * P:(k + 1) * P], ident)
                mm.then_inc(h_turned, 1)
            pe.wait_ge(rT_ready, 4)
            pe.wait_ge(moe_in, 80)
            for a in range(TT):
                for k in range(KD):
                    pe.matmul(bank[0][:, a * NE:(a + 1) * NE], rT[:, k, a * P:(a + 1) * P], wr[:, k, :],
                              start=k == 0, stop=False)
                mm = pe.matmul(bank[0][:, a * NE:(a + 1) * NE], ones[0:1, :], br[:, :], start=False, stop=True)
            mm.then_inc(logit_done, 1)
            pe.wait_ge(mask_ready, 1)
            pe.matmul(bank[1][:, 0:NE], tri, msk[:, 0, :], start=True, stop=True)
            pe.matmul(bank[1][:, NE:2 * NE], ones, msk[:, 0, :], start=True, stop=False)
            pe.matmul(bank[1][:, NE:2 * NE], tri, msk[:, 1, :], start=False, stop=True)
            pe.matmul(bank[1][:, 2 * NE:3 * NE], ones, msk[:, 0, :], start=True, stop=False)
            pe.matmul(bank[1][:, 2 * NE:3 * NE], ones, msk[:, 1, :], start=False, stop=True).then_inc(rank_done, 1)
            for a in range(TT):
                mm = pe.transpose(bank[2][0:NE, a * P:(a + 1) * P], gat[:, a, :], ident)
            mm.then_inc(gates_turned, 1)
            pe.wait_ge(gT_ready, 1)
            for a in range(TT):
                for n in range(2):
                    mm = pe.matmul(bank[4 + 2 * a + n][:, :], gT[:, a * P:(a + 1) * P], b2all[:, 512 * n:512 * n + 512],
                                   start=True, stop=True)
            mm.then_inc(b2_done, 1)

            def gather(i, part, done):
                if part is h2_hi:
                    pe.wait_ge(pick_ready, i + 1)
                else:
                    pe.wait_ge(xe_hi_ready, i + 1)
                for k in range(KD):
                    for a in range(TT):
                        mm = pe.matmul(bank[6 + k // 4][:, (k % 4) * P:(k % 4 + 1) * P],
                                       part[:, a, k * P:(k + 1) * P], pick[:, a, :], start=a == 0, stop=a == TT - 1)
                mm.then_inc(done, 1)

            def products(i, hs, k_n, n_n, x_hi, x_lo, k0, outs, start):
                pe.wait_ge(lo_ready[hs % SLOTS], i * USES + (hs // SLOTS + 1))
                hi = w_hi[:, hs % SLOTS, :].rearrange("p (k n) -> p k n", k=k_n)
                lo = w_lo[:, hs % SLOTS, :].rearrange("p (k n) -> p k n", k=k_n)
                for k in range(k_n):
                    for w in (hi, lo):
                        for n in range(n_n):
                            pe.matmul(outs[n], x_hi[:, k0 + k, :], w[:, k, 512 * n:512 * n + 512],
                                      start=start and k == 0 and w is hi, stop=False)
                if hs == 0:
                    pe.wait_ge(xe_ready, i + 1)
                for k in range(k_n):
                    for n in range(n_n):
                        mm = pe.matmul(outs[n], x_lo[:, k0 + k, :], hi[:, k, 512 * n:512 * n + 512],
                                       start=False, stop=hs == HALVES - 1 and k == k_n - 1)
                mm.then_inc(w_used, 1)

            def up(i, hs):
                s = hs // 2
                products(i, hs, 4, 1, xe_hi, xe_lo, 4 * (hs % 2), [bank[s]], hs % 2 == 0)
                if hs % 2:
                    col = 512 * (s // 2) + FF * (s % 2)
                    pe.matmul(bank[s], sel[:, :], b1_hl[:, col:col + 512], start=False, stop=True).then_inc(up_done, 1)

            def turn_act(i, half):
                pe.wait_ge(act_ready, 2 * i + (half + 1))
                for k in range(4):
                    mm = pe.transpose(bank[half][:, k * P:(k + 1) * P],
                                      act_t[:, half * 512 + k * P:half * 512 + (k + 1) * P], ident)
                mm.then_inc(act_turned, 1)

            def down(i, hs):
                if hs % 2 == 0:
                    pe.wait_ge(aT_ready, 2 * i + (hs // 2 - 3))
                products(i, hs, 2, 2, aT_hi, aT_lo, 2 * (hs - 8), [bank[4], bank[5]], hs == 8)

            def turn_picks(i, e):
                pe.wait_ge(pick_t_ready, i + 2)
                for a in range(TT):
                    pe.matmul(bank[2][:, a * P:(a + 1) * P], pick_t[:, a, :], ident_r[:, :], start=True, stop=True)
                for a in range(TT):
                    mm = pe.matmul(bank[2][:, T:T + 2], pick_t[:, a, :],
                                   gate_hl[:, a, bass.ds(e, 1), :].rearrange("p o g -> p (o g)"),
                                   start=a == 0, stop=a == TT - 1)
                mm.then_inc(pick_turned, 1)

            def combine(i):
                pe.wait_ge(pickT_ready, i + 2)
                pe.wait_ge(ye_ready, i + 2)
                for q in range(4):
                    a, n = q // 2, q % 2
                    for y in (y_hi, y_lo):
                        mm = pe.matmul(bank[(2, 3, 6, 7)[q]], pickT[:, a * P:(a + 1) * P],
                                       y[:, 512 * n:512 * n + 512], start=y is y_hi, stop=y is y_lo)
                    mm.then_inc(comb_done, 1)

            def expert(i, before):
                pe.wait_ge(xe_hi_ready, i + 1)
                pe.wait_ge(sel_ready, i + 1)
                for hs in range(3):
                    up(i, hs)
                if before:
                    combine(i - 1)
                up(i, 3)
                pe.wait_ge(acc_done, 4 * i + 1)
                up(i, 4)
                up(i, 5)
                turn_act(i, 0)
                pe.wait_ge(acc_done, 4 * i + 2)
                up(i, 6)
                up(i, 7)
                pe.wait_ge(acc_done, 4 * i + 4)
                gather(i + 1, h2_hi, gather_hi)
                pe.wait_ge(ye_ready, i + 1)
                down(i, 8)
                turn_act(i, 1)
                down(i, 9)
                gather(i + 1, h2_lo, gather_lo)
                down(i, 10)
                turn_picks(i, i)
                down(i, 11)

            def combine_last(i):
                pe.wait_ge(xe_ready, i + 2)
                combine(i)

            pe.wait_ge(gT_ready, 1)
            turn_picks(-1, 0)
            pe.wait_ge(acc_init, 1)
            pe.wait_ge(h2_ready, 1)
            gather(0, h2_hi, gather_hi)
            gather(0, h2_lo, gather_lo)
            pe.wait_ge(b1_ready, 1)
            with pe.Fori(0, NE) as i:
                expert(i, True)
            combine_last(NE - 1)
            pe.wait_ge(route_ready, 1)
            more = pe.value_load(flag[0:1, 0:1], min_val=0, max_val=1)
            with pe.If(more > 0):
                with pe.Fori(NE, 2 * NE) as i:
                    expert(i, False)
                    combine_last(i)

        @block.scalar
        def _(act):
            st = Steps(act, a_step)
            act.wait_ge(vcol_ready, 1)
            act.activation(m4[:, 0:8], cond_c, ACT.Tanh, scale=0.5).then_inc(dt_ready, 1)
            act.activation(ldt, ldt, ACT.Exp).then_inc(dt_ready, 1)
            act.wait_ge(theta_ready, 1)
            act.activation(rho, rho, ACT.Exp).then_inc(sine_ready, 1)
            act.wait_ge(theta_ready, 2)
            act.activation(es, theta, ACT.Sin).then_inc(sine_ready, 1)
            act.activation(ec, theta, ACT.Sin, scale=0.5).then_inc(sine_ready, 1)
            act.wait_ge(bline_done, 1)
            act.wait_ge(vrow_turned, 1)
            act.activation(bline, bank[6][0:HEADS, 0:N_HOT], ACT.Copy).then_inc(bline_ready, 1)

            def square(n, src, first):
                if not first:
                    st.settle()
                st.do(act.activation(junk, src, ACT.Square, accum_out=ss[:, n:n + 1]))

            act.wait_ge(x_in, 16 * TT)
            for n in range(TT):
                act.activation(junk, xs[:, n, :], ACT.Square, accum_out=ss[:, n:n + 1]).then_inc(squares, 1)
                act.wait_ge(squares, n + 1)
            for r in range(2):
                if r == 0:
                    act.wait_ge(bc_turned, 1)
                act.activation(BT[:, r, :, :].rearrange("p j s -> p (j s)"), bank[r][:, :], ACT.Copy).then_inc(
                    *((a_step, 1) if r == 0 else (bc_ready, 1)))
            st.n += 1
            act.wait_ge(bc_turned, 2)
            for r in range(2):
                act.activation(CT[:, r, :, :].rearrange("p j s -> p (j s)"), bank[2 + r][:, :], ACT.Copy).then_inc(
                    *((a_step, 1) if r == 0 else (bc_ready, 1)))
            st.n += 1

            for g in range(4):
                act.wait_ge(h_turned, g + 1)
                act.activation(hT[:, 2 * g:2 * g + 2, :].rearrange("p k t -> p (k t)"), bank[6 + g % 2][:, :],
                               ACT.Copy).then_inc(hT_ready, 1)

            def empty(name, b, dst, func=ACT.Copy, scale=1.0):
                f = FILL[(name, b)]
                act.wait_ge(fill_done, f + 1)
                act.activation(dst, bank[4 + f % 2][:, :], func, scale=scale).then_inc(act_emptied, 1)

            def two(view, b):
                return view[:, 2 * b:2 * b + 2, :].rearrange("p k t -> p (k t)")

            for b in range(2):
                empty("u", b, two(uT, b))
            for b in range(2):
                empty("q", b, two(qT, b))
            for b in range(2):
                empty("k", b, two(kT, b))
            for b in range(2):
                empty("v", b, vv[:, b, :])
            for n in range(2):
                for b in range(2):
                    empty(f"ga{n}", b, two(ga_t, 2 * n + b), ACT.Tanh, 0.5)

            for h in range(HEADS):
                act.wait_ge(max_ready, h + 1)
                lo = lg_m[h % 2]
                act.activation(lo[:, 0:P], lo[:, 0:P], ACT.Exp, bias=mx[:, 0:1], accum_out=sums[:, 0:1]).then_inc(exp_done, 1)
                act.activation(lo[:, P:3 * P], lo[:, P:3 * P], ACT.Exp, bias=mx[:, 1:2], accum_out=sums[:, 1:2]).then_inc(exp_done, 1)
                act.wait_ge(p_turned, h + 1)
                if h >= 2:
                    act.wait_ge(pv_done, h - 1)
                act.activation(pt_m[h % 2], bank[6 + h % 2][:, 0:3 * P], ACT.Copy).then_inc(pT_ready, 1)
                if h % 2 == 1:
                    act.wait_ge(pv_done, h + 1)
                    j = h // 2
                    act.activation(attT[:, j, :], bank[3][:, 0:T], ACT.Copy).then_inc(att_ready, 1)
            act.wait_ge(s_done, HEADS)
            for n in range(2):
                for b in range(2):
                    empty(f"gs{n}", b, two(gs_t, 2 * n + b), ACT.Tanh, 0.5)
            act.wait_ge(gelu_in, 1)
            act.activation(gt_, gt_, ACT.Tanh, scale=GELU_C).then_inc(gelu_th, 1)
            act.wait_ge(gelu_out, 1)
            for b in range(2):
                empty("glu", b, gv[:, 512 * b:512 * b + 512])
            for b in range(2):
                empty("glu", 2 + b, gt_[:, 512 * b:512 * b + 512], ACT.Tanh, 0.25)
            for b in range(4):
                empty("ao", b, two(aoT, b))
            for name, n in (("wo0", 0), ("wo1", 1)):
                for a in range(TT):
                    empty(name, a, y_sb[:, a, 512 * n:512 * n + 512])

            act.wait_ge(act_emptied, emptied(FILL[("wo1", 1)])[1])
            for n in range(TT):
                act.activation(junk, y_sb[:, n, :], ACT.Square, accum_out=ss[:, n:n + 1]).then_inc(squares, 1)
                act.wait_ge(squares, TT + n + 1)
            for n in range(TT):
                act.wait_ge(x1_ready, n + 1)
                act.activation(junk, xs[:, n, :], ACT.Square, accum_out=ss[:, n:n + 1]).then_inc(squares, 1)
                act.wait_ge(squares, 2 * TT + n + 1)
            for g in range(4):
                act.wait_ge(h_turned, 4 + g + 1)
                act.activation(rT[:, 2 * g:2 * g + 2, :].rearrange("p k t -> p (k t)"), bank[6 + g % 2][:, :],
                               ACT.Copy).then_inc(rT_ready, 1)
            act.wait_ge(top_ready, 1)
            for a in range(TT):
                act.activation(topx[:, a, 0:TOPK], top[:, a, 0:TOPK], ACT.Exp, bias=ms2[:, a:a + 1],
                               accum_out=sums[:, a:a + 1]).then_inc(topexp, 1)
            act.wait_ge(gates_turned, 1)
            act.activation(gT[:, :], bank[2][0:NE, 0:T], ACT.Copy).then_inc(gT_ready, 1)

            act.wait_ge(normed, 2 * TT)
            act.activation(h2_hi[:, :, :], h2, ACT.Copy).then_inc(h2_hi_ready, 1)
            act.wait_ge(moe_in, 80)
            act.wait_ge(logit_done, 1)
            act.activation(b1_hl[:, :], b1_raw, ACT.Copy).then_inc(b1_hi_ready, 1)

            def high(i, hs):
                act.wait_ge(raw_in[hs % SLOTS], i * (16 * USES) + (16 * (hs // SLOTS) + 16))
                act.wait_ge(w_used, i * HALVES + (hs + 1))
                act.activation(w_hi[:, hs % SLOTS, :], w_raw[:, hs % SLOTS, :], ACT.Copy).then_inc(hi_ready, 1)

            def rows_in(i, part, done, n_done):
                act.wait_ge(done, i + 1)
                for n in range(2):
                    last = act.activation(part[:, 4 * n:4 * n + 4, :].rearrange("p k s -> p (k s)"), bank[6 + n], ACT.Copy)
                last.then_inc(n_done, 1)

            def gate_tanh(i, half):
                act.wait_ge(g_ready, 2 * i + (half + 1))
                act.activation(th_c, g_c, ACT.Tanh, scale=ALPHA / 2).then_inc(gate_th, 1)

            def act_high(i, half):
                act.wait_ge(act_turned, 2 * i + (half + 1))
                act.activation(aT_hi[:, 4 * half:4 * half + 4, :].rearrange("p k s -> p (k s)"), bank[half], ACT.Copy
                               ).then_inc(aT_hi_ready, 1)

            def picks_in(i):
                act.wait_ge(pick_turned, i + 2)
                act.activation(two_gates, bank[2][:, T:T + 2], ACT.Copy, accum_out=gate_s)
                act.activation(pickT[:, :], bank[2][:, 0:T], ACT.Copy).then_inc(pickT_ready, 1)

            def out_high(i):
                act.wait_ge(w_used, i * HALVES + (HALVES + SLOTS))
                act.wait_ge(pickT_ready, i + 2)
                for n in range(2):
                    act.activation(y_hi[:, 512 * n:512 * n + 512], bank[4 + n], ACT.Copy, scale=gate_s
                                   ).then_inc(y_hi_ready, 1)

            def expert(i, before):
                high(i, 0)
                high(i, 1)
                if before:
                    rows_in(i, xe_lo, gather_lo, xe_ready)
                    picks_in(i - 1)
                high(i, 2)
                if before:
                    out_high(i - 1)
                for hs in range(3, 8):
                    high(i, hs)
                gate_tanh(i, 0)
                high(i, 8)
                high(i, 9)
                act_high(i, 0)
                high(i, 10)
                gate_tanh(i, 1)
                rows_in(i + 1, xe_hi, gather_hi, xe_hi_ready)
                high(i, 11)
                act_high(i, 1)

            def expert_last(i):
                picks_in(i)
                out_high(i)
                rows_in(i + 1, xe_lo, gather_lo, xe_ready)

            act.wait_ge(acc_init, 1)
            act.sem_inc(w_used, SLOTS)
            rows_in(0, xe_hi, gather_hi, xe_hi_ready)
            with act.Fori(0, NE) as i:
                expert(i, True)
            expert_last(NE - 1)
            act.wait_ge(route_ready, 1)
            more = act.value_load(flag[0:1, 0:1], min_val=0, max_val=1)
            with act.If(more > 0):
                with act.Fori(NE, 2 * NE) as i:
                    expert(i, False)
                    expert_last(i)
            act.wait_ge(normed, 3 * TT)
            for n in range(TT):
                act.activation(act_t, acc[:, n, :], ACT.Square, accum_out=ss[:, n:n + 1]).then_inc(squares, 1)
                act.wait_ge(squares, 3 * TT + n + 1)

        @block.vector
        def _(dve):
            V = Steps(dve, v_step)
            tt, ts, stt = dve.tensor_tensor, dve.tensor_scalar, dve.scalar_tensor_tensor

            def chain(ins):
                V.do(ins)
                V.settle()

            dve.wait_ge(vec_in, 80)
            dve.tensor_copy(vrow[0:ST, :].rearrange("s (a p) -> s a p", a=2),
                            ldt_in.rearrange("s (a o) -> s a o", o=1).broadcast_to([ST, 2, GP])).then_inc(vrow_ready, 1)
            dve.wait_ge(vrow_turned, 1)
            dve.tensor_copy(vcol, bank[3][:, 0:60]).then_inc(vcol_ready, 1)
            dve.wait_ge(vcol_ready, 1)
            dve.wait_ge(dt_ready, 2)
            chain(stt(cond_c, m4[:, 0:8], 1.0, cond_c, ALU.add, ALU.mult))
            for k in range(KD):
                last = ts(cond_b[:, k, :], ones, cond_c[:, k:k + 1], 0.5, ALU.mult, ALU.mult)
            last.then_inc(cond_ready, 1)
            V.do(ts(lam, are, -1e-4, None, ALU.min))
            chain(tt(theta, aim, ldt, ALU.mult))
            tt(rho, lam, ldt, ALU.mult).then_inc(theta_ready, 1)
            chain(ts(m1, theta, 1.0 / (2 * math.pi), ROUND, ALU.mult, ALU.add))
            chain(ts(m1, m1, -ROUND, None, ALU.add))
            rest = 2 * math.pi - 6.28125
            c2 = float(np.float32(np.round(rest * 2 ** 22) / 2 ** 22))
            for cc in (6.28125, c2, rest - c2):
                chain(stt(theta, m1, -cc, theta, ALU.mult, ALU.add))
            ts(theta, theta, 3.1415925, -3.1415925, ALU.min, ALU.max).then_inc(theta_ready, 1)
            dve.wait_ge(sine_ready, 3)
            chain(tt(ec, ec, ec, ALU.mult))
            chain(ts(ec, ec, -2.0, 1.0, ALU.mult, ALU.add))
            chain(tt(m1, rho, ec, ALU.mult))
            chain(tt(m2, rho, es, ALU.mult))
            chain(tt(m3, lam, lam, ALU.mult))
            chain(tt(m4, aim, aim, ALU.mult))
            chain(ts(m1, m1, -1.0, None, ALU.add))
            chain(tt(m3, m3, m4, ALU.add))
            chain(dve.reciprocal(m3, m3))
            chain(tt(zre, m1, lam, ALU.mult))
            chain(tt(m4, m2, aim, ALU.mult))
            chain(tt(zre, zre, m4, ALU.add))
            chain(tt(zim, m2, lam, ALU.mult))
            chain(tt(m4, m1, aim, ALU.mult))
            chain(tt(zim, zim, m4, ALU.subtract))
            chain(tt(zre, zre, m3, ALU.mult))
            chain(tt(zim, zim, m3, ALU.mult))
            dve.memset(b_bar, 0.0).then_inc(v_step, 1)
            V.n += 1
            dve.wait_ge(param_in, 64)
            V.settle()

            def over_c(v):
                return v.rearrange("p (s o) -> p s o", o=1).broadcast_to([P, ST, GC])

            for r, (a, b, op) in enumerate(((0, 1, ALU.subtract), (1, 0, ALU.add))):
                V.do(tt(b_tmp, b_in[:, a, :, :], over_c(zre), ALU.mult))
                chain(tt(b_tmp2, b_in[:, b, :, :], over_c(zim), ALU.mult))
                for g in range(2):
                    rows = slice(64 * g, 64 * g + 64)
                    last = tt(b_bar[rows, r, :, GC * g:GC * g + GC], b_tmp[rows], b_tmp2[rows], op)
                    if r == 0 or g == 0:
                        chain(last)
            last.then_inc(bc_padded, 1)
            for r in range(2):
                for g in range(2):
                    last = ts(c_pad[:, r, :, 64 * g:64 * g + 64], c_in[:, r, :, :], cst[:, C_EVEN + g:C_EVEN + g + 1],
                              1.0 if r == 0 else -1.0, ALU.mult, ALU.mult)
            last.then_inc(bc_padded, 1)

            def empty_ada(name):
                n = ADA.index(name)
                f = FILL[(name, 0)]
                col = 512 * (name[3] == "b")
                kind = name[:2]
                dve.wait_ge(fill_done, f + 1)
                dve.wait_ge(bada_in[n % 2], 16 * (n // 2 + 1))
                src, bia = bank[4 + f % 2][:, :], bada[:, n % 2, :]
                if kind == "sh":
                    tt(row_b[:, col:col + 512], src, bia, ALU.add).then_inc(dve_emptied, 1)
                    return
                dst = (row_a if kind == "sc" else row_g if name[2] == "1" else row_g2)[:, col:col + 512]
                dve.wait_ge(grow_in, 16 * (G_USERS.index(name) + 1))
                chain(tt(dst, src, bia, ALU.add))
                stt(dst, dst, 1.0 if kind == "sc" else 0.0, grow, ALU.add, ALU.mult
                    ).then_inc(dve_emptied, 1)

            dve.memset(tab_c[:, :, 0:1], 1.0)
            V.do(dve.memset(tab_s[:, :, 0:1], 0.0))
            V.do(dve.tensor_copy(m1, ec))
            chain(dve.tensor_copy(m2, es))

            def level(n):
                chain(tt(m3, m1, m1, ALU.mult))
                chain(tt(m4, m2, m2, ALU.mult))
                chain(tt(m3, m3, m4, ALU.add))
                chain(ts(m3, m3, -0.5, 1.5, ALU.mult, ALU.add))
                chain(tt(m1, m1, m3, ALU.mult))
                chain(tt(m2, m2, m3, ALU.mult))

                def over_t(v):
                    return v.rearrange("p (s o) -> p s o", o=1).broadcast_to([P, ST, n])

                a, b = tab_1[:, :, 0:n], tab_2[:, :, 0:n]
                chain(tt(a, tab_c[:, :, 0:n], over_t(m1), ALU.mult))
                chain(tt(b, tab_s[:, :, 0:n], over_t(m2), ALU.mult))
                chain(tt(tab_c[:, :, n:2 * n], a, b, ALU.subtract))
                chain(tt(a, tab_c[:, :, 0:n], over_t(m2), ALU.mult))
                chain(tt(b, tab_s[:, :, 0:n], over_t(m1), ALU.mult))
                chain(tt(tab_s[:, :, n:2 * n], a, b, ALU.add))
                chain(tt(m3, m1, m1, ALU.mult))
                chain(tt(m4, m2, m2, ALU.mult))
                chain(stt(m2, m1, 2.0, m2, ALU.mult, ALU.mult))
                chain(tt(m1, m3, m4, ALU.subtract))

            for n, name in enumerate(ADA[0:4]):
                empty_ada(name)
                level(1 << n)
            dve.wait_ge(dve_emptied, 4)
            for a in range(TT):
                dve.wait_ge(rstd_ready, a + 1)
                chain(stt(xs[:, a, :], xs[:, a, :], rstd[:, a:a + 1], row_a[:, :], ALU.mult, ALU.mult))
                tt(xs[:, a, :], xs[:, a, :], row_b[:, :], ALU.add).then_inc(normed, 1)
            for n in range(4, 8):
                level(1 << n)

            def skip(j):
                dve.wait_ge(y_done, 2 * j + 2)
                stt(uT[:, j, :], uT[:, j, :], dcol[:, j:j + 1], bank[2][:, 0:T],
                    ALU.mult, ALU.add).then_inc(y_read, 1)

            def by_tile(v):
                return v.rearrange("p (m t) -> p m t", m=2)

            zr3, zi3, tp3 = by_tile(zr), by_tile(zi), by_tile(tp)
            for n in range(8):
                tc = tab_c[:, 2 * n:2 * n + 2, :]
                tsn = tab_s[:, 2 * n:2 * n + 2, :]
                dve.wait_ge(bu_done, n + 1)
                chain(tt(zr3, bu_re, tc, ALU.mult))
                chain(tt(tp3, bu_im, tsn, ALU.mult))
                chain(tt(zr3, zr3, tp3, ALU.add))
                chain(tt(tp3, bu_re, tsn, ALU.mult))
                tt(zi3, bu_im, tc, ALU.mult).then_inc(bu_read, 1)
                dve.wait_ge(bu_read, n + 1)
                V.settle()
                chain(tt(zi3, zi3, tp3, ALU.subtract))
                if n >= 3 and n % 2:
                    skip((n - 3) // 2)
                for m in range(2):
                    decay = rho[:, 2 * n + m:2 * n + m + 1].broadcast_to([P, T])
                    for z in (zr, zi):
                        v = z[:, m * T:(m + 1) * T]
                        chain(dve.tensor_tensor_scan(v, decay, v, 0.0, ALU.mult, ALU.add))
                V.settle()
                if n >= 2:
                    dve.wait_ge(y_done, n - 1)
                xr_, xi_ = xre[n % 2], xim[n % 2]
                xr3, xi3 = by_tile(xr_), by_tile(xi_)
                chain(tt(xr3, zr3, tc, ALU.mult))
                chain(tt(tp3, zi3, tsn, ALU.mult))
                chain(tt(xi3, zi3, tc, ALU.mult))
                chain(tt(zr3, zr3, tsn, ALU.mult))
                chain(tt(xr_, xr_, tp, ALU.subtract))
                tt(xi_, xi_, zr, ALU.add).then_inc(x_ready, 1)
                dve.wait_ge(x_ready, n + 1)
                V.settle()

            skip(3)

            def head(h):
                dve.wait_ge(s_done, h + 1)
                dve.wait_ge(bias_in[h % 2], 32 * (h // 2 + 1))
                if h >= 2:
                    dve.wait_ge(p_turned, h - 1)
                lo = lg_m[h % 2]
                stt(lo, bank[6 + h % 2][:, 0:3 * P], HD ** -0.5, bias_m[h % 2], ALU.mult, ALU.add).then_inc(logits_ready, 1)
                dve.wait_ge(logits_ready, h + 1)
                V.do(dve.reduce_max(m1[:, 0:1], lo[:, 0:P], AX))
                chain(dve.reduce_max(m1[:, 1:2], lo[:, P:3 * P], AX))
                ts(mx, m1[:, 0:2], -1.0, None, ALU.mult).then_inc(max_ready, 1)
                dve.wait_ge(exp_done, 2 * h + 2)
                chain(dve.reciprocal(m2[:, 0:2], sums))
                V.do(ts(lo[:, 0:P], lo[:, 0:P], m2[:, 0:1], None, ALU.mult))
                ts(lo[:, P:3 * P], lo[:, P:3 * P], m2[:, 1:2], None, ALU.mult).then_inc(probs_ready, 1)
                V.settle()

            for h in range(HEADS):
                if h < 6:
                    empty_ada(ADA[4 + h])
                head(h)

            yv = uT.rearrange("p j t -> p (j t)")
            dve.wait_ge(y_read, 4)
            chain(tt(gt_, yv, yv, ALU.mult))
            chain(ts(gt_, gt_, 0.044715, 1.0, ALU.mult, ALU.add))
            tt(gt_, gt_, yv, ALU.mult).then_inc(gelu_in, 1)
            dve.wait_ge(gelu_th, 1)
            stt(yv, gt_, 1.0, yv, ALU.add, ALU.mult).then_inc(gelu_out, 1)
            dve.wait_ge(act_emptied, emptied(FILL[("glu", 3)])[1])
            stt(gv, gt_, 1.0, gv, ALU.add, ALU.mult).then_inc(glu_ready, 1)
            dve.wait_ge(act_emptied, emptied(FILL[("ao", 3)])[1])
            chain(stt(ao_flat, ta_flat, 1.0, ao_flat, ALU.add, ALU.mult))
            for b in range(4):
                f = FILL[("so", b)]
                v = slice(512 * b, 512 * b + 512)
                dve.wait_ge(fill_done, f + 1)
                stt(qk_flat[:, v], qk_flat[:, v], 1.0, bank[4 + f % 2][:, :], ALU.add, ALU.mult).then_inc(dve_emptied, 1)
                dve.wait_ge(dve_emptied, emptied(f)[1])
                stt(ao_flat[:, v], qk_flat[:, v], 0.25, ao_flat[:, v], ALU.mult, ALU.add).then_inc(merged_ready, 1)
            empty_ada("gt2a")
            empty_ada("gt2b")

            dve.wait_ge(x_again, 16 * TT)
            for a in range(TT):
                dve.wait_ge(rstd_ready, TT + a + 1)
                chain(stt(y_sb[:, a, :], y_sb[:, a, :], rstd[:, a:a + 1], row_g[:, :], ALU.mult, ALU.mult))
                tt(xs[:, a, :], xs[:, a, :], y_sb[:, a, :], ALU.add).then_inc(x1_ready, 1)
            dve.wait_ge(dve_emptied, emptied(FILL[("gt2b", 0)])[1])
            for a in range(TT):
                dve.wait_ge(rstd_ready, 2 * TT + a + 1)
                chain(stt(h2[:, a, :], xs[:, a, :], rstd[:, a:a + 1], row_a[:, :], ALU.mult, ALU.mult))
                tt(h2[:, a, :], h2[:, a, :], row_b[:, :], ALU.add).then_inc(normed, 1)
            dve.wait_ge(logit_done, 1)
            chain(dve.tensor_copy(lgr.rearrange("p a e -> p (a e)"), bank[0][:, 0:2 * NE]))
            for a in range(TT):
                chain(dve.max(top[:, a, :], lgr[:, a, :]))
            V.settle()
            for a in range(TT):
                chain(dve.max_index(idx[:, a, :], top[:, a, :], lgr[:, a, :]))
                last = ts(ms2[:, a:a + 1], top[:, a, 0:1], -1.0, None, ALU.mult)
            last.then_inc(top_ready, 1)
            V.settle()
            chain(dve.tensor_copy(idf.rearrange("p a e -> p (a e)"), idx[:, :, :].rearrange("p a e -> p (a e)")))
            dve.wait_ge(topexp, 2)
            chain(dve.reciprocal(m2[:, 0:2], sums))
            for a in range(TT):
                chain(ts(topx[:, a, 0:TOPK], topx[:, a, 0:TOPK], m2[:, a:a + 1], None, ALU.mult))
                for j in range(TOPK):
                    key = idf[:, a, j:j + 1]
                    if j == 0:
                        chain(ts(msk[:, a, :], iota[:, 0:NE], key, None, ALU.is_equal))
                        chain(ts(gat[:, a, :], iota[:, 0:NE], key, topx[:, a, 0:1], ALU.is_equal, ALU.mult))
                    else:
                        chain(stt(msk[:, a, :], iota[:, 0:NE], key, msk[:, a, :], ALU.is_equal, ALU.add))
                        chain(ts(one_hot, iota[:, 0:NE], key, topx[:, a, j:j + 1], ALU.is_equal, ALU.mult))
                        chain(tt(gat[:, a, :], gat[:, a, :], one_hot, ALU.add))
            dve.sem_inc(mask_ready, 1)
            dve.wait_ge(h2_hi_ready, 1)
            for a in range(TT):
                last = tt(h2_lo[:, a, :], h2[:, a, :], h2_hi[:, a, :].bitcast(F32), ALU.subtract)
            last.then_inc(h2_ready, 1)
            dve.wait_ge(b1_hi_ready, 1)
            low = slice(NE, 2 * NE)
            tt(b1_hl[low, :], b1_raw[low, :], b1_hl[low, :].bitcast(F32), ALU.subtract).then_inc(b1_ready, 1)
            dve.wait_ge(rank_done, 1)
            V.do(dve.memset(row_of, NOWHERE))
            for a in range(TT):
                V.do(ts(pick_t[:, a, :], ones, 0.0, None, ALU.mult))
            V.do(dve.tensor_copy(ident_r[:, :], ident))
            V.do(tt(sel_table, ident[0:2 * NE, 0:NE + 1], ident[0:2 * NE, NE:2 * NE + 1], ALU.add))
            V.settle()
            dve.wait_ge(gates_turned, 1)
            for a in range(TT):
                V.do(ts(gat[:, a, :], gat[:, a, :], 0.5, None, ALU.mult))
                V.do(ts(row_of[:, a, 0:NE], msk[:, a, :], -NOWHERE, NOWHERE, ALU.mult, ALU.add))
            V.settle()
            for a in range(TT):
                for h in range(2):
                    V.do(dve.tensor_copy(gate_hl[:, a, h * NE:(h + 1) * NE, 0], gat[:, a, :]))
                V.do(tt(row_of[:, a, 0:NE], row_of[:, a, 0:NE], bank[1][:, a * NE:(a + 1) * NE], ALU.add))
            V.settle()
            for a in range(TT):
                for h in range(2):
                    V.do(tt(gate_hl[:, a, h * NE:(h + 1) * NE, 1], gat[:, a, :],
                            gate_hl[:, a, h * NE:(h + 1) * NE, 0].bitcast(F32), ALU.subtract))
                V.do(ts(row_of[:, a, NE:2 * NE], row_of[:, a, 0:NE], -float(CAP), None, ALU.add))
            chain(dve.reduce_max(m1[:, 0:1], bank[1][:, 2 * NE:3 * NE], AX))
            ts(flag[:, 0:1], m1[:, 0:1], float(CAP), None, ALU.is_gt).then_inc(route_ready, 1)
            dve.wait_ge(h2_ready, 1)
            dve.wait_ge(b2_done, 1)
            for q in range(4):
                V.do(dve.tensor_copy(acc[:, q // 2, 512 * (q % 2):512 * (q % 2) + 512], bank[4 + q][:, :]))
            V.settle()
            dve.sem_inc(pick_t_ready, 1)
            dve.sem_inc(acc_init, 1)

            def low_part(i, hs):
                dve.wait_ge(hi_ready, i * HALVES + (hs + 1))
                tt(w_lo[:, hs % SLOTS, :], w_raw[:, hs % SLOTS, :], w_hi[:, hs % SLOTS, :].bitcast(F32), ALU.subtract
                   ).then_inc(lo_ready[hs % SLOTS], 1)

            def one_hots(dst, i, ready):
                for a in range(TT):
                    last = ts(dst[:, a, :], iota, row_of[:, a, bass.ds(i, 1)], None, ALU.is_equal)
                last.then_inc(ready, 1)

            def clamp(i, half):
                dve.wait_ge(up_done, 4 * i + (2 * half + 2))
                ts(g_c, bank[2 * half][:, :], LIMIT, None, ALU.min).then_inc(g_ready, 1)
                V.do(ts(u_c, bank[2 * half + 1][:, :], LIMIT, -LIMIT, ALU.min, ALU.max))

            def times_gate(i, half):
                dve.wait_ge(g_ready, 2 * i + (half + 1))
                V.settle()
                V.do(stt(u_c, u_c, 1.0, g_c, ALU.add, ALU.mult))

            def swish(i, half):
                dve.wait_ge(gate_th, 2 * i + (half + 1))
                V.settle()
                stt(act_t[:, 512 * half:512 * half + 512], th_c, 1.0, u_c, ALU.add, ALU.mult).then_inc(act_ready, 1)

            def act_low(i, half):
                dve.wait_ge(aT_hi_ready, 2 * i + (half + 1))
                v = aT_lo[:, 4 * half:4 * half + 4, :].rearrange("p k s -> p (k s)")
                hi = aT_hi[:, 4 * half:4 * half + 4, :].rearrange("p k s -> p (k s)")
                tt(v, bank[half], hi.bitcast(F32), ALU.subtract).then_inc(aT_ready, 1)

            def out_low(i):
                for n in range(2):
                    v = slice(512 * n, 512 * n + 512)
                    dve.wait_ge(y_hi_ready, 2 * i + (n + 3))
                    last = stt(y_lo[:, v], bank[4 + n], gate_s, y_hi[:, v].bitcast(F32), ALU.mult, ALU.subtract)
                last.then_inc(ye_ready, 1)

            def add_up(i, q):
                v = acc[:, q // 2, 512 * (q % 2):512 * (q % 2) + 512]
                dve.wait_ge(comb_done, 4 * i + (q + 5))
                tt(v, v, bank[(2, 3, 6, 7)[q]][:, :], ALU.add).then_inc(acc_done, 1)

            PER = 4

            def expert(i, e, before):
                V.at = start + i * PER
                V.n = 0
                dve.tensor_copy(sel[:, :], sel_table[:, bass.ds(e, 1)].broadcast_to([2 * NE, P])).then_inc(sel_ready, 1)
                low_part(i, 0)
                low_part(i, 1)
                dve.wait_ge(gather_lo, i + 1)
                one_hots(pick, i + 1, pick_ready)
                low_part(i, 2)
                if before:
                    out_low(i - 1)
                dve.wait_ge(pickT_ready, i + 1)
                one_hots(pick_t, i, pick_t_ready)
                low_part(i, 4)
                low_part(i, 5)
                if before:
                    for q in range(4):
                        add_up(i - 1, q)
                low_part(i, 6)
                clamp(i, 0)
                times_gate(i, 0)
                swish(i, 0)
                low_part(i, 8)
                act_low(i, 0)
                low_part(i, 9)
                dve.wait_ge(act_ready, 2 * i + 1)
                clamp(i, 1)
                times_gate(i, 1)
                swish(i, 1)
                low_part(i, 10)
                act_low(i, 1)
                dve.wait_ge(act_ready, 2 * i + 2)
                assert V.n == PER, V.n

            def expert_last(i):
                out_low(i)
                for q in range(4):
                    add_up(i, q)

            one_hots(pick, 0, pick_ready)
            start = V.n
            with dve.Fori(0, NE) as i:
                expert(i, i, True)
            expert_last(NE - 1)
            dve.wait_ge(route_ready, 1)
            more = dve.value_load(flag[0:1, 0:1], min_val=0, max_val=1)
            with dve.If(more > 0):
                with dve.Fori(NE, 2 * NE) as i:
                    expert(i, i - NE, False)
                    expert_last(i)
            dve.drain()
            dve.sem_inc(normed, TT)
            for a in range(TT):
                dve.wait_ge(rstd_ready, 3 * TT + a + 1)
                stt(acc[:, a, :], acc[:, a, :], rstd[:, a:a + 1], row_g2, ALU.mult, ALU.mult).then_inc(acc_init, 1)
                dve.wait_ge(acc_init, 2 + a)
                tt(xs[:, a, :], xs[:, a, :], acc[:, a, :], ALU.add).then_inc(out_ready, 1)


_INS = ["x", "c", "rel_bias", "w_ada", "b_ada", "g_pre_mix", "g_post_mix", "g_pre_ffn", "g_post_ffn", "w_in",
        "ssm_a_re", "ssm_a_im", "ssm_log_dt", "ssm_b_re", "ssm_b_im", "ssm_c_re", "ssm_c_im", "ssm_d", "w_glu",
        "w_ssm_out", "w_att_out", "w_out", "w_router", "b_router", "w_exp_in", "b_exp_in", "w_exp_out", "b_exp_out"]


def kernel(**inputs):
    import concourse.bacc as _bacc
    from concourse.bass_utils import run_bass_kernel_spmd as _run

    nc = _bacc.Bacc("TRN2", target_bir_lowering=False, num_devices=1)
    arrays, args = {}, []
    for name in _INS:
        a = np.ascontiguousarray(inputs[name])
        arrays[f"in_{name}"] = a
        args.append(nc.dram_tensor(f"in_{name}", a.shape, mybir.dt.from_np(a.dtype), kind="ExternalInput").ap())
    arrays["in_const"] = constants()
    args.append(nc.dram_tensor("in_const", (P, C_N), F32, kind="ExternalInput").ap())
    args.append(nc.dram_tensor("bias_line", (HEADS, N_HOT), F32, kind="Internal").ap())
    args.append(nc.dram_tensor("bias_rows", (HEADS, P, 512), F32, kind="Internal").ap())
    args.append(nc.dram_tensor("out_0", (1, T, D), F32, kind="ExternalOutput").ap())
    build(nc, *args)
    r = _run(nc, [arrays], core_ids=[0])
    return r.results[0]["out_0"]
```

```python
from contextlib import ExitStack
import math

import numpy as np

import concourse.bass as bass
from concourse import mybir

F32 = mybir.dt.float32
F32R = mybir.dt.float32r
I32 = mybir.dt.int32
U32 = mybir.dt.uint32
ALU = mybir.AluOpType
ACT = mybir.ActivationFunctionType
AX = mybir.AxisListType.X

P = 128
D = 1024
T = 256
TT = T // P
KD = D // P
HEADS, HD = 8, 64
AW = HEADS * HD
SW = D // 2
KS = SW // P
GROUPS, GC, GP = 32, 16, 64
ST = GROUPS * GP // P
BUCKETS, MAX_DIST = 32, 128
NE, TOPK, FF = 32, 4, 1024
CAP = P
LIMIT, ALPHA = 7.0, 1.702
EPS = 1e-6
MASKED = -1.0e30
NOWHERE = 1000.0
GELU_C = math.sqrt(2.0 / math.pi)
ROUND = 12582912.0

C_ID, C_ONE, C_TRI, C_IOTA = 0, P, 2 * P, 3 * P
C_EVEN = 4 * P
C_ODD = C_EVEN + 1
C_HOT = C_ODD + 1
N_HOT = 2 * T - 1
C_N = C_HOT + N_HOT

MIX = ["sc1a", "sc1b", "sh1a", "sh1b", "u", "gt1a", "q", "gt1b", "k", "sh2a", "v", "sh2b", "ga0", "ga1",
       "sc2a", "gs0", "sc2b", "gs1", "gt2a", "glu", "gt2b", "ao", "so", "wo0", "wo1"]
ADA = ["sc1a", "sc1b", "sh1a", "sh1b", "gt1a", "gt1b", "sh2a", "sh2b", "sc2a", "sc2b", "gt2a", "gt2b"]
ADA_BANK = [4, 5, 4, 5, 3, 3, 3, 3, 0, 1, 0, 1]
SPLIT_ADA = 4
ADA_HEAD = {1: 8, 2: 9, 4: 10, 5: 11}
ADA_ROW = {n: 2 * ["sh1", "sc1", "gt1", "sh2", "sc2", "gt2"].index(n[:3]) + (n[3] == "b") for n in ADA}
MIX_SLOTS = 4
PW = 4096
HALVES = 12
HW = 2048
SLOTS = 4
POOL_SLOT = 3
USES = HALVES // SLOTS

FILLS = []
for name in MIX:
    if name in ("glu", "ao"):
        FILLS += [(name, b, "act") for b in range(4)]
    elif name == "so":
        FILLS += [(name, b, "dve") for b in range(4)]
    elif name not in ADA and name[:2] != "wo":
        FILLS += [(name, b, "act") for b in range(2)]
FILLS += [(f"wo{n}", a, "act") for a in range(TT) for n in range(2)]
FILL = {(name, b): f for f, (name, b, _) in enumerate(FILLS)}


def used_up(n):
    return 1 + max(f for f, (name, _, _) in enumerate(FILLS) if name == MIX[n])


def emptied(f):
    who = FILLS[f][2]
    return who, sum(x[2] == who for x in FILLS[:f + 1])


def constants():
    c = np.zeros((P, C_N), np.float32)
    c[:, C_ID:C_ID + P] = np.eye(P)
    c[:, C_ONE:C_ONE + P] = 1.0
    c[:, C_TRI:C_TRI + P] = np.triu(np.ones((P, P)), 1)
    c[:, C_IOTA:C_IOTA + P] = np.arange(P)[None, :]
    exact = BUCKETS // 2
    for j in range(N_HOT):
        dist = T - 1 - j
        if dist < 0:
            c[BUCKETS, C_HOT + j] = 1.0
            continue
        large = exact + int(np.float32(np.log(np.float32(max(dist, 1)) / np.float32(exact)))
                            / np.float32(math.log(MAX_DIST / exact)) * np.float32(BUCKETS - exact))
        c[dist if dist < exact else min(large, BUCKETS - 1), C_HOT + j] = 1.0
    even = (np.arange(P) // GC) % 2 == 0
    c[:, C_EVEN] = even
    c[:, C_ODD] = ~even
    return c


class Steps:

    def __init__(self, eng, sem):
        self.eng, self.sem, self.n, self.at = eng, sem, 0, 0

    def do(self, ins):
        ins.then_inc(self.sem, 1)
        self.n += 1

    def settle(self):
        self.eng.wait_ge(self.sem, self.at + self.n)


def build(nc, x, c, rel_bias, w_ada, b_ada, g_pre_mix, g_post_mix, g_pre_ffn, g_post_ffn, w_in,
          ssm_a_re, ssm_a_im, ssm_log_dt, ssm_b_re, ssm_b_im, ssm_c_re, ssm_c_im, ssm_d, w_glu,
          w_ssm_out, w_att_out, w_out, w_router, b_router, w_exp_in, b_exp_in, w_exp_out, b_exp_out,
          const, bias_line, bias_rows, out):
    ctx = ExitStack()
    with ctx:
        def sb(name, shape, dt=F32):
            return ctx.enter_context(nc.sbuf_tensor(name, shape, dt))

        def sem(name):
            return ctx.enter_context(nc.semaphore(name))

        cst = sb("cst", [P, C_HOT])
        xs = sb("xs", [P, TT, D])
        hT = sb("hT", [P, KD, T])
        row_a = sb("row_a", [P, D])
        row_b = sb("row_b", [P, D])
        row_g = sb("row_g", [P, D])
        small = sb("small", [P, 640])
        flag = sb("flag", [P, 8], I32)
        idx = sb("idx", [P, TT, 8], U32)
        with ExitStack() as mixer:
            ring = mixer.enter_context(nc.sbuf_tensor("ring", [P, MIX_SLOTS + 2, PW], F32))
            work = mixer.enter_context(nc.sbuf_tensor("work", [P, 19712], F32))
        w_hi = sb("w_hi", [P, SLOTS, HW], F32R)
        w_lo = sb("w_lo", [P, SLOTS, HW], F32R)
        w_raw = sb("w_raw", [P, SLOTS, HW])
        h2_hi, h2_lo = sb("h2_hi", [P, TT, D], F32R), sb("h2_lo", [P, TT, D], F32R)
        b1_hl = sb("b1_hl", [2 * NE, 2 * FF], F32R)
        xe_hi = sb("xe_hi", [P, KD, 2 * P], F32R)
        aT_hi, aT_lo = sb("aT_hi", [P, KD, P], F32R), sb("aT_lo", [P, KD, P], F32R)
        y_hi, y_lo = sb("y_hi", [P, D], F32R), sb("y_lo", [P, D], F32R)
        pick = sb("pick", [P, TT, 2 * P], F32R)
        pick_t = sb("pick_t", [P, TT, P], F32R)
        pickT = sb("pickT", [P, T], F32R)
        sel = sb("sel", [2 * NE, P], F32R)
        ident_r = sb("ident_r", [P, P], F32R)
        gate_hl = sb("gate_hl", [P, TT, 2 * NE, 2], F32R)
        route = sb("route", [P, 704])
        gap = sb("gap", [P, 15104 - 14528])
        sb("row_g2_place", [P, D])
        with nc.sbuf_tensor("tail", [P, 3072], F32) as tail_tensor:
            tail = tail_tensor
        xe_lo = sb("xe_lo", [P, KD, 2 * P], F32R)
        psum = ctx.enter_context(nc.psum_tensor("psum", [P, 8, 512], F32))
        bank = [psum[:, i, :] for i in range(8)]
        bu_re, bu_im = psum[:, 0:2, 0:T], psum[:, 0:2, T:2 * T]

        at = [0]

        def carve(n):
            at[0] += n
            assert at[0] <= 19712
            return work[:, at[0] - n:at[0]]

        ident = cst[:, C_ID:C_ID + P]
        ones = cst[:, C_ONE:C_ONE + P]
        tri = cst[:, C_TRI:C_TRI + P]
        iota = cst[:, C_IOTA:C_IOTA + P]

        uT = carve(1024).rearrange("p (j t) -> p j t", j=KS)
        qk_flat = carve(2048)
        qT = qk_flat[:, 0:1024].rearrange("p (j t) -> p j t", j=4)
        kT = qk_flat[:, 1024:2048].rearrange("p (j t) -> p j t", j=4)
        gs_t = xs[:, :, :].rearrange("p a n -> p (a n)").rearrange("p (j t) -> p j t", j=KD)
        gs_flat = xs[:, :, :].rearrange("p a n -> p (a n)")
        vv = carve(1024).rearrange("p (a n) -> p a n", a=TT)
        att_flat = carve(1024)
        attT = att_flat.rearrange("p (j t) -> p j t", j=4)
        ta_flat = carve(2048)
        ga_t = ta_flat.rearrange("p (j t) -> p j t", j=KD)
        ao_flat = carve(2048)
        aoT = ao_flat.rearrange("p (j t) -> p j t", j=KD)
        ssm_flat = carve(3584)
        z_re = [ssm_flat[:, 0:512], att_flat[:, 0:512]]
        z_im = [ssm_flat[:, 512:1024], att_flat[:, 512:1024]]
        tp = ssm_flat[:, 1024:1536]
        xre = [ssm_flat[:, 1536 + 1024 * n:2048 + 1024 * n] for n in range(2)]
        xim = [ssm_flat[:, 2048 + 1024 * n:2560 + 1024 * n] for n in range(2)]
        attn_flat = carve(2304)
        bias_m = [attn_flat[:, 384 * n:384 * n + 384] for n in range(2)]
        lg_m = [attn_flat[:, 768 + 384 * n:1152 + 384 * n] for n in range(2)]
        pt_m = [attn_flat[:, 1536 + 384 * n:1920 + 384 * n] for n in range(2)]
        turn_tmp = attn_flat[:, 1536:2048]
        btct = carve(2048)
        BT = btct[:, 0:1024].rearrange("p (r j s) -> p r j s", r=2, j=4)
        CT = btct[:, 1024:2048].rearrange("p (r j s) -> p r j s", r=2, j=4)
        row_g2 = btct[:, 0:1024]
        cond_b = carve(1024)[:, 0:512].rearrange("p (k m) -> p k m", k=KD // 2)
        ada_acc = carve(1024).rearrange("p (b n) -> p b n", b=2)
        b_rows = carve(512)[0:len(ADA), :]
        b_in = qk_flat[:, 0:512].rearrange("p (r s c) -> p r s c", r=2, s=ST)
        b_bar = qk_flat[:, 512:1536].rearrange("p (r s c) -> p r s c", r=2, s=ST)
        b_tmp = qk_flat[:, 1536:1792].rearrange("p (s c) -> p s c", s=ST)
        b_tmp2 = qk_flat[:, 1792:2048].rearrange("p (s c) -> p s c", s=ST)
        c_in = ssm_flat[:, 0:512].rearrange("p (r j s) -> p r j s", r=2, j=4)
        c_pad = ssm_flat[:, 512:1536].rearrange("p (r j s) -> p r j s", r=2, j=4)
        tab_c = ring[:, MIX_SLOTS, :].rearrange("p (s t) -> p s t", s=ST)
        tab_s = ring[:, MIX_SLOTS + 1, :].rearrange("p (s t) -> p s t", s=ST)
        tab_1 = ta_flat.rearrange("p (s t) -> p s t", s=ST)
        tab_2 = ao_flat.rearrange("p (s t) -> p s t", s=ST)
        vrow = attn_flat[0:64, 0:P]
        ldt_in = attn_flat[0:ST, 140:142]
        relb = attn_flat[0:BUCKETS + 1, 128:128 + HEADS]
        bline = attn_flat[0:HEADS, 256:256 + N_HOT]
        junk = ssm_flat[:, 2304:3328]
        hot = ssm_flat[0:BUCKETS + 1, 1600:1600 + N_HOT]
        gv = ssm_flat[:, 0:1024]
        gt_ = ssm_flat[:, 1024:2048]
        gluT = gv.rearrange("p (j t) -> p j t", j=KS)
        rT = ta_flat.rearrange("p (k t) -> p k t", k=KD)
        y_sb = qk_flat.rearrange("p (a n) -> p a n", a=TT)
        acc = hT[:, :, :].rearrange("p k t -> p (k t)").rearrange("p (a n) -> p a n", a=TT)
        g_c, u_c, th_c = row_a[:, 0:512], row_a[:, 512:1024], row_b[:, 0:512]
        act_t = row_g[:, :]
        ro = [0]

        def routing(n):
            ro[0] += n
            assert ro[0] <= 704
            return route[:, ro[0] - n:ro[0]]

        wr = routing(256).rearrange("p (k e) -> p k e", k=KD)
        row_of = routing(132).rearrange("p (a e) -> p a e", a=TT)
        gT = routing(T)[0:NE, :]
        br = routing(NE)[0:1, :]
        chosen = row_g[:, 0:TT * TOPK * NE].rearrange("p (a j e) -> p a j e", a=TT, j=TOPK)
        weighed = row_g[:, 512:512 + TT * TOPK * NE].rearrange("p (a j e) -> p a j e", a=TT, j=TOPK)
        sel_table = row_b[0:2 * NE, 512:512 + NE + 1]
        b1_raw = tail[0:2 * NE, 0:2 * FF]
        b2all = tail[0:NE, 2 * FF:2 * FF + D]
        h2 = hT[:, :, :].rearrange("p k t -> p (k t)").rearrange("p (a n) -> p a n", a=TT)

        sm = [0]

        def little(n):
            sm[0] += n
            assert sm[0] <= 640
            return small[:, sm[0] - n:sm[0]]

        vcol = little(60)
        ldt, cond_c, dcol = vcol[:, 0:16], vcol[:, 16:24], vcol[:, 24:28]
        are, aim = vcol[:, 28:44], vcol[:, 44:60]
        ss = little(2)
        ms = little(2)
        rstd = little(2)
        nhalf = little(2)
        lam, theta, rho, ec, es, zre, zim, m1, m2, m3, m4 = (little(16) for _ in range(11))
        e_re, e_im, n1, n2 = (little(16) for _ in range(4))
        ss_y = little(4)
        gate_s = little(1)
        two_gates = little(2)
        mx = little(2)
        sums = little(2)
        lgr = little(64).rearrange("p (a e) -> p a e", a=TT)
        msk = little(64).rearrange("p (a e) -> p a e", a=TT)
        gat = little(64).rearrange("p (a e) -> p a e", a=TT)
        top = little(16).rearrange("p (a e) -> p a e", a=TT)
        topx = little(16).rearrange("p (a e) -> p a e", a=TT)
        idf = little(16).rearrange("p (a e) -> p a e", a=TT)
        ms2 = little(2)

        slot_in = [sem(f"slot_in{s}") for s in range(MIX_SLOTS)]
        raw_in = [sem(f"raw_in{s}") for s in range(SLOTS)]
        lo_ready = [sem(f"lo_ready{s}") for s in range(SLOTS)]
        hi_ready, w_used = sem("hi_ready"), sem("w_used")
        hot_in = sem("hot_in")
        const_in, vec_in, x_in, param_in, x_again = sem("const_in"), sem("vec_in"), sem("x_in"), sem("param_in"), sem("x_again")
        b_rows_in, g_pre_in, g_mix_in, g_ffn_in, g_post_in = (
            sem("b_rows_in"), sem("g_pre_in"), sem("g_mix_in"), sem("g_ffn_in"), sem("g_post_in"))
        ada_summed, ada_done, ada_emptied, scaled = sem("ada_summed"), sem("ada_done"), sem("ada_emptied"), sem("scaled")
        angle_ready = sem("angle_ready")
        trig_ready, tables_shared, tables_begun, tables_ready, z_ready = (
            sem("trig_ready"), sem("tables_shared"), sem("tables_begun"), sem("tables_ready"), sem("z_ready"))
        bias_out, bias_in = sem("bias_out"), [sem("bias_in0"), sem("bias_in1")]
        moe_in = sem("moe_in")
        fill_done, dve_emptied, act_emptied = sem("fill_done"), sem("dve_emptied"), sem("act_emptied")
        emptied_sem = {"dve": dve_emptied, "act": act_emptied}
        v_step, g_step = sem("v_step"), sem("g_step")
        relb_ready, vrow_ready = sem("relb_ready"), sem("vrow_ready")
        vrow_turned, vcol_ready, cond_ready = sem("vrow_turned"), sem("vcol_ready"), sem("cond_ready")
        dt_ready, theta_ready, sine_ready = sem("dt_ready"), sem("theta_ready"), sem("sine_ready")
        bc_padded, bc_turned, bc_ready = sem("bc_padded"), sem("bc_turned"), sem("bc_ready")
        bline_done, bline_ready = sem("bline_done"), sem("bline_ready")
        squares, rstd_ready, normed = sem("squares"), sem("rstd_ready"), sem("normed")
        h_turned, hT_ready, rT_ready = sem("h_turned"), sem("hT_ready"), sem("rT_ready")
        bu_done, bu_read, x_ready, y_done = sem("bu_done"), sem("bu_read"), sem("x_ready"), sem("y_done")
        y_read = sem("y_read")
        s_done, logits_ready, exp_done, probs_ready, p_turned, pT_ready = (
            sem("s_done"), sem("logits_ready"), sem("exp_done"), sem("probs_ready"), sem("p_turned"), sem("pT_ready"))
        pv_done, att_ready, max_ready = sem("pv_done"), sem("att_ready"), sem("max_ready")
        gelu_in, gelu_th, gelu_out = sem("gelu_in"), sem("gelu_th"), sem("gelu_out")
        glu_ready, merged_ready = sem("glu_ready"), sem("merged_ready")
        x1_ready, x1_squares = sem("x1_ready"), sem("x1_squares")
        logit_done, top_ready, topexp, mask_ready, rank_done, route_ready = (
            sem("logit_done"), sem("top_ready"), sem("topexp"), sem("mask_ready"), sem("rank_done"), sem("route_ready"))
        gates_ready = sem("gates_ready")
        gates_turned, gT_ready, b2_done, acc_init = sem("gates_turned"), sem("gT_ready"), sem("b2_done"), sem("acc_init")
        sel_ready, pick_ready, pick_t_ready = sem("sel_ready"), sem("pick_ready"), sem("pick_t_ready")
        h2_hi_ready, h2_ready, b1_hi_ready, b1_ready = sem("h2_hi_ready"), sem("h2_ready"), sem("b1_hi_ready"), sem("b1_ready")
        up_done, g_ready, gate_th, act_ready = sem("up_done"), sem("g_ready"), sem("gate_th"), sem("act_ready")
        gathered, xe_in = sem("gathered"), sem("xe_in")
        act_turned, aT_hi_ready, aT_ready = sem("act_turned"), sem("aT_hi_ready"), sem("aT_ready")
        pick_turned, pickT_ready = sem("pick_turned"), sem("pickT_ready")
        y_hi_ready, ye_ready = sem("y_hi_ready"), sem("ye_ready")
        comb_done, acc_done = sem("comb_done"), sem("acc_done")
        out_ready, stored = sem("out_ready"), sem("stored")

        def broadcast(vec, n0, n1):
            return vec[0:1, n0:n1].broadcast_to([P, n1 - n0])

        def moe_source(e, hs):
            if hs < 8:
                which, rows = hs // 2, 512 * (hs % 2)
                col = 512 * (which // 2) + FF * (which % 2)
                return w_exp_in[0][bass.ds(e, 1), rows:rows + 512, col:col + 512].rearrange(
                    "o (k p) n -> (o p) k n", p=P)
            rows = 256 * (hs - 8)
            return w_exp_out[0][bass.ds(e, 1), rows:rows + 256, :].rearrange("o (k p) n -> (o p) k n", p=P)

        def by_tile(v):
            return v.rearrange("p (m t) -> p m t", m=2)

        def unit(eng, steps):
            steps.do(eng.tensor_tensor(n1, e_re, e_re, ALU.mult))
            steps.do(eng.tensor_tensor(n2, e_im, e_im, ALU.mult))
            steps.settle()
            steps.do(eng.tensor_tensor(n1, n1, n2, ALU.add))
            steps.settle()
            steps.do(eng.tensor_scalar(n1, n1, -0.5, 1.5, ALU.mult, ALU.add))
            steps.settle()
            steps.do(eng.tensor_tensor(e_re, e_re, n1, ALU.mult))
            steps.do(eng.tensor_tensor(e_im, e_im, n1, ALU.mult))
            steps.settle()

        def double(eng, steps, n, tiles):
            def over_t(v):
                v = v[:, tiles]
                return v.rearrange("p (s o) -> p s o", o=1).broadcast_to([P, tiles.stop - tiles.start, n])

            a, b = tab_1[:, tiles, 0:n], tab_2[:, tiles, 0:n]
            tc, tsn = tab_c[:, tiles, :], tab_s[:, tiles, :]
            steps.do(eng.tensor_tensor(a, tc[:, :, 0:n], over_t(e_re), ALU.mult))
            steps.do(eng.tensor_tensor(b, tsn[:, :, 0:n], over_t(e_im), ALU.mult))
            steps.settle()
            steps.do(eng.tensor_tensor(tc[:, :, n:2 * n], a, b, ALU.subtract))
            steps.settle()
            steps.do(eng.tensor_tensor(a, tc[:, :, 0:n], over_t(e_im), ALU.mult))
            steps.do(eng.tensor_tensor(b, tsn[:, :, 0:n], over_t(e_re), ALU.mult))
            steps.settle()
            steps.do(eng.tensor_tensor(tsn[:, :, n:2 * n], a, b, ALU.add))

        def level(eng, steps, n):
            unit(eng, steps)
            double(eng, steps, n, slice(0, ST))
            steps.do(eng.tensor_tensor(n1, e_re, e_re, ALU.mult))
            steps.do(eng.tensor_tensor(n2, e_im, e_im, ALU.mult))
            steps.settle()
            steps.do(eng.tensor_tensor(e_im, e_re, e_im, ALU.mult))
            steps.settle()
            steps.do(eng.tensor_scalar(e_im, e_im, 2.0, None, ALU.mult))
            steps.do(eng.tensor_tensor(e_re, n1, n2, ALU.subtract))
            steps.settle()

        def slot(s, k):
            return ring[:, s, :].rearrange("p (k n) -> p k n", k=k)

        block = ctx.enter_context(nc.Block())

        @block.sync
        def _(sp):
            def source(name):
                if name in ADA:
                    col = 512 * ADA_ROW[name]
                    return w_ada[0][:, col:col + 512], 8
                if name == "glu":
                    return w_glu[0], 4
                if name == "ao":
                    return w_att_out[0], 4
                if name == "so":
                    return w_ssm_out[0], 4
                if name in ("wo0", "wo1"):
                    n = 512 * int(name[2])
                    return w_out[0][:, n:n + 512], 8
                col = {"q": 0, "k": 1, "v": 2, "u": 3, "ga0": 4, "ga1": 5, "gs0": 6, "gs1": 7}[name] * 512
                return w_in[0][:, col:col + 512], 8

            sp.dma_start(vrow[16:24, :], c.rearrange("o (k p) -> (o k) p", p=P)).then_inc(vec_in, 16)
            sp.dma_start(vrow[24:28, :], ssm_d.rearrange("o (k p) -> (o k) p", p=P)).then_inc(vec_in, 16)
            sp.dma_start(vrow[28:44, :], ssm_a_re[0].rearrange("(s a) p -> s (a p)", a=2)).then_inc(vec_in, 16)
            sp.dma_start(vrow[44:60, :], ssm_a_im[0].rearrange("(s a) p -> s (a p)", a=2)).then_inc(vec_in, 16)
            sp.dma_start(ldt_in, ssm_log_dt[0].rearrange("(s a) -> s a", a=2)).then_inc(vec_in, 16)
            sp.dma_start(cst[:, :], const[:, 0:C_HOT]).then_inc(const_in, 16)
            for a in range(TT):
                sp.dma_start(xs[:, a, :], x[0, a * P:(a + 1) * P, :]).then_inc(x_in, 16)
            for n, name in enumerate(MIX):
                s = n % MIX_SLOTS
                if n == MIX_SLOTS:
                    sp.wait_ge(bline_ready, 1)
                    sp.dma_start(bias_line, bline).then_inc(bias_out, 16)
                    sp.wait_ge(bias_out, 16)
                    sp.dma_start(bias_rows[:, :, 0:N_HOT],
                                 bias_line.rearrange("h (o n) -> h o n", o=1).broadcast_to([HEADS, P, N_HOT])
                                 ).then_inc(bias_out, 16)
                if n >= MIX_SLOTS:
                    before = MIX[n - MIX_SLOTS]
                    if before in ADA:
                        m = ADA.index(before)
                        sp.wait_ge(ada_done if m < SPLIT_ADA else ada_summed, m + 1)
                    else:
                        sp.wait_ge(fill_done, used_up(n - MIX_SLOTS))
                src, k = source(name)
                sp.dma_start(slot(s, k), src.rearrange("(k p) n -> p k n", p=P)).then_inc(slot_in[s], 16)

            def load(e, hs):
                sp.dma_start(w_raw[:, hs % SLOTS, :].rearrange("p (k n) -> p k n", k=4 if hs < 8 else 2),
                             moe_source(e, hs)).then_inc(raw_in[hs % SLOTS], 16)

            def stream(i0, i1, e0):
                with sp.Fori(i0, i1 - 1) as i:
                    for hs in range(SLOTS, HALVES + SLOTS):
                        sp.wait_ge(lo_ready[hs % SLOTS], i * USES + hs // SLOTS)
                        load(i - e0 if hs < HALVES else i - e0 + 1, hs % HALVES)
                for hs in range(SLOTS, HALVES):
                    sp.wait_ge(lo_ready[hs % SLOTS], (i1 - 1) * USES + hs // SLOTS)
                    load(i1 - 1 - e0, hs)

            sp.wait_ge(x_ready, 8)
            for hs in range(SLOTS):
                load(0, hs)
            stream(0, NE, 0)
            sp.wait_ge(route_ready, 1)
            more = sp.value_load(flag[0:1, 0:1], min_val=0, max_val=1)
            with sp.If(more > 0):
                for hs in range(SLOTS):
                    sp.wait_ge(lo_ready[hs], NE * USES)
                    load(0, hs)
                stream(NE, 2 * NE, NE)
            for a in range(TT):
                sp.wait_ge(out_ready, a + 1)
                sp.dma_start(out[0, a * P:(a + 1) * P, :], xs[:, a, :]).then_inc(stored, 16)
            sp.wait_ge(stored, 16 * TT)

        @block.gpsimd
        def _(pool):
            G = Steps(pool, g_step)
            gtt = pool.tensor_tensor

            def gchain(ins):
                G.do(ins)
                G.settle()

            gchain(pool.memset(relb, MASKED))
            pool.dma_start(relb[0:BUCKETS, :], rel_bias).then_inc(relb_ready, 16)
            gchain(pool.memset(nhalf, -0.5))
            pool.dma_start(row_g[:, :], broadcast(g_post_mix, 0, D)).then_inc(g_mix_in, 16)

            def root(n, bias):
                gchain(pool.tensor_scalar(ms[:, n:n + 1], ss[:, n:n + 1], 1.0 / D, bias, ALU.mult, ALU.add))
                gtt(rstd[:, n:n + 1], ms[:, n:n + 1], nhalf[:, 0:1], ALU.pow).then_inc(rstd_ready, 1)

            for n in range(TT):
                pool.wait_ge(squares, n + 1)
                root(n, EPS)

            G.do(pool.memset(tab_c[:, :, 0:1], 1.0))
            G.do(pool.memset(tab_s[:, :, 0:1], 0.0))
            pool.wait_ge(trig_ready, 1)
            G.do(pool.tensor_copy(e_re, ec))
            gchain(pool.tensor_copy(e_im, es))

            for n in range(5):
                level(pool, G, 1 << n)
            pool.sem_inc(tables_begun, 1)
            pool.wait_ge(scaled, 1)
            pool.dma_start(row_a[:, :], broadcast(g_pre_ffn, 0, D)).then_inc(g_ffn_in, 16)
            pool.wait_ge(bias_out, 32)

            def bias_matrix(h):
                if h >= 2:
                    pool.wait_ge(logits_ready, h - 1)
                else:
                    pool.wait_ge(vcol_ready, 1)
                for a, (lo, hi) in enumerate(((0, P), (P, 3 * P))):
                    src = bass.AP(tensor=bias_rows.tensor, offset=h * P * 512 + T - 1 - a * P,
                                  ap=[[511, P], [1, hi - lo]])
                    pool.dma_start(bias_m[h % 2][:, lo:hi], src).then_inc(bias_in[h % 2], 16)

            bias_matrix(0)
            bias_matrix(1)
            pool.wait_ge(angle_ready, 1)
            double(pool, G, T // 2, slice(ST // 2, ST))
            G.settle()
            pool.sem_inc(tables_shared, 1)
            pool.wait_ge(tables_ready, 1)
            for n in range(8):
                tc = tab_c[:, 2 * n:2 * n + 2, :]
                tsn = tab_s[:, 2 * n:2 * n + 2, :]
                xr3, xi3, t3, zr3, zi3 = (by_tile(v) for v in (xre[n % 2], xim[n % 2], turn_tmp, z_re[n % 2], z_im[n % 2]))
                pool.wait_ge(z_ready, n + 1)
                if n >= 2:
                    pool.wait_ge(y_done, n - 1)
                G.do(gtt(xr3, zr3, tc, ALU.mult))
                G.do(gtt(t3, zi3, tsn, ALU.mult))
                gchain(gtt(xi3, zi3, tc, ALU.mult))
                gchain(gtt(xr3, xr3, t3, ALU.subtract))
                gchain(gtt(t3, zr3, tsn, ALU.mult))
                gtt(xi3, xi3, t3, ALU.add).then_inc(x_ready, 1)
                pool.wait_ge(x_ready, n + 1)
            pool.dma_start(row_g2, broadcast(g_post_ffn, 0, D)).then_inc(g_post_in, 16)
            bias_matrix(2)
            pool.wait_ge(y_done, 8)
            for r in range(2):
                pool.dma_start(b1_raw[r * NE:(r + 1) * NE, :], b_exp_in[0]).then_inc(moe_in, 16)
            for h in range(3, HEADS):
                bias_matrix(h)
            pool.wait_ge(ada_done, len(ADA))
            pool.dma_start(b2all, b_exp_out[0]).then_inc(moe_in, 16)
            pool.wait_ge(att_ready, 4)
            pool.dma_start(wr, w_router[0].rearrange("(k p) e -> p k e", p=P)).then_inc(moe_in, 16)
            pool.dma_start(br[:, :], b_router).then_inc(moe_in, 16)
            pool.wait_ge(merged_ready, 4)
            for a in range(TT):
                pool.dma_start(xs[:, a, :], x[0, a * P:(a + 1) * P, :]).then_inc(x_again, 16)
            for n in range(TT):
                pool.wait_ge(squares, TT + n + 1)
                gchain(gtt(ss[:, n:n + 1], ss_y[:, 2 * n:2 * n + 1], ss_y[:, 2 * n + 1:2 * n + 2], ALU.add))
                root(n, 4.0 * EPS)
                pool.wait_ge(x1_squares, n + 1)
                root(n, EPS)
            pool.wait_ge(b1_hi_ready, 1)
            low = slice(NE, 2 * NE)
            gtt(b1_hl[low, :], b1_raw[low, :], b1_hl[low, :].bitcast(F32), ALU.subtract).then_inc(b1_ready, 1)
            pool.wait_ge(b1_ready, 1)

            def low_parts(i):
                for hs in range(POOL_SLOT, HALVES, SLOTS):
                    pool.wait_ge(hi_ready, i * HALVES + (hs + 1))
                    pool.tensor_tensor(w_lo[:, POOL_SLOT, :], w_raw[:, POOL_SLOT, :], w_hi[:, POOL_SLOT, :].bitcast(F32),
                                       ALU.subtract).then_inc(lo_ready[POOL_SLOT], 1)

            with pool.Fori(0, NE) as i:
                low_parts(i)
            pool.wait_ge(route_ready, 1)
            more = pool.value_load(flag[0:1, 0:1], min_val=0, max_val=1)
            with pool.If(more > 0):
                with pool.Fori(NE, 2 * NE) as i:
                    low_parts(i)
            for n in range(TT):
                pool.wait_ge(squares, 2 * TT + n + 1)
                root(n, EPS)

        @block.tensor
        def _(pe):
            def arrive(name):
                n = MIX.index(name)
                pe.wait_ge(slot_in[n % MIX_SLOTS], 16 * (n // MIX_SLOTS + 1))
                return n % MIX_SLOTS

            def free_bank(f):
                if f >= 2:
                    who, count = emptied(f - 2)
                    pe.wait_ge(emptied_sem[who], count)
                return bank[4 + f % 2]

            pe.wait_ge(const_in, 16)
            pe.wait_ge(vec_in, 80)
            pe.wait_ge(vrow_ready, 1)
            pe.transpose(bank[3][:, 0:60], vrow[0:60, :], ident[0:60, 0:60]).then_inc(vrow_turned, 1)
            pe.wait_ge(relb_ready, 16)
            pe.wait_ge(hot_in, 16)
            pe.matmul(bank[6][0:HEADS, 0:N_HOT], relb, hot,
                      start=True, stop=True).then_inc(bline_done, 1)

            def ada(n):
                before = [m for m in range(n) if ADA_BANK[m] == ADA_BANK[n]]
                if before:
                    pe.wait_ge(ada_emptied, before[-1] + 1)
                if n < SPLIT_ADA:
                    if n == 0:
                        pe.wait_ge(cond_ready, 1)
                    m = MIX.index(ADA[n])
                    pe.wait_ge(slot_in[m], 16)
                    w = slot(m, 8)
                    for k in range(KD // 2):
                        pe.matmul(bank[ADA_BANK[n]], cond_b[:, k, :], w[:, KD // 2 + k, :], start=k == 0, stop=False)
                pe.wait_ge(ada_summed, n + 1)
                pe.matmul(bank[ADA_BANK[n]], ones, ada_acc[:, n % 2, :], start=n >= SPLIT_ADA, stop=True).then_inc(ada_done, 1)

            def features(name, b, k_n, rhs, between=None):
                s = MIX.index(name) % MIX_SLOTS
                f = FILL[(name, b)]
                out_b = free_bank(f)
                w = slot(s, k_n)
                for m in range(2):
                    col = (2 * b + m) * P
                    for k in range(k_n):
                        mm = pe.matmul(out_b[:, m * T:(m + 1) * T], w[:, k, col:col + P], rhs[:, k, :],
                                       start=k == 0, stop=k == k_n - 1)
                    if m == 0 and between is not None:
                        between()
                mm.then_inc(fill_done, 1)

            def tokens(name, a, lhs):
                s = MIX.index(name) % MIX_SLOTS
                f = FILL[(name, a)]
                out_b = free_bank(f)
                w = slot(s, 8)
                for k in range(KD):
                    mm = pe.matmul(out_b[:, :], lhs[:, k, a * P:(a + 1) * P], w[:, k, :],
                                   start=k == 0, stop=k == KD - 1)
                mm.then_inc(fill_done, 1)

            pe.wait_ge(bc_padded, 1)
            for r in range(2):
                for j in range(4):
                    mm = pe.transpose(bank[r][:, j * P:(j + 1) * P],
                                      b_bar[:, r, 4 * j:4 * j + 4, :].rearrange("p s c -> p (s c)"), ident)
            mm.then_inc(bc_turned, 1)
            pe.wait_ge(bc_padded, 2)
            pe.wait_ge(vcol_ready, 1)
            for r in range(2):
                for j in range(4):
                    mm = pe.transpose(bank[2 + r][:, j * P:(j + 1) * P], c_pad[:, r, j, :], ident)
            mm.then_inc(bc_turned, 1)
            for n in range(SPLIT_ADA):
                ada(n)
            for g in range(4):
                if g == 0:
                    pe.wait_ge(normed, 1)
                    pe.wait_ge(bline_ready, 1)
                if g == 2:
                    pe.wait_ge(normed, 2)
                if g >= 2:
                    pe.wait_ge(hT_ready, g - 1)
                for kk in range(2):
                    for a in range(TT):
                        k = 2 * g + kk
                        mm = pe.transpose(bank[6 + g % 2][:, kk * T + a * P:kk * T + (a + 1) * P],
                                          xs[:, a, k * P:(k + 1) * P], ident)
                mm.then_inc(h_turned, 1)
            pe.wait_ge(hT_ready, 4)
            arrive("u")
            for b in range(2):
                features("u", b, 8, hT)

            def inputs_to_states(n):
                if n == 0:
                    pe.wait_ge(bc_ready, 2)
                    pe.wait_ge(act_emptied, emptied(FILL[("u", 1)])[1])
                else:
                    pe.wait_ge(bu_read, n)
                for m in range(2):
                    st = 2 * n + m
                    j, q = st // 4, st % 4
                    for r in range(2):
                        mm = pe.matmul(bank[m][:, r * T:(r + 1) * T], BT[32 * q:32 * q + 32, r, j, :],
                                       uT[32 * q:32 * q + 32, j, :], start=True, stop=True,
                                       tile_position=(32 * q, 0))
                mm.then_inc(bu_done, 1)

            def states_to_outputs(n):
                pe.wait_ge(x_ready, n + 1)
                j = n // 2
                if n % 2 == 0 and j >= 1:
                    pe.wait_ge(y_read, j)
                for m in range(2):
                    st = 2 * n + m
                    q = st % 4
                    o = bank[2][32 * q:32 * q + 32, 0:T]
                    pe.matmul(o, CT[:, 0, j, 32 * q:32 * q + 32], xre[n % 2][:, m * T:(m + 1) * T],
                              start=True, stop=False, tile_position=(0, 32 * q))
                    mm = pe.matmul(o, CT[:, 1, j, 32 * q:32 * q + 32], xim[n % 2][:, m * T:(m + 1) * T],
                                   start=False, stop=True, tile_position=(0, 32 * q))
                mm.then_inc(y_done, 1)

            seq = [("q", 0), ("q", 1), ("k", 0), ("k", 1), ("v", 0), ("v", 1), ("ga0", 0), ("ga0", 1)]
            for n, (name, b) in enumerate(seq):
                inputs_to_states(n)
                if b == 0:
                    arrive(name)
                if name == "v":
                    tokens(name, b, hT)
                else:
                    features(name, b, 8, hT)
                if n >= 1:
                    states_to_outputs(n - 1)
                if n % 2:
                    ada(4 + n // 2)

            def scores(h):
                if h >= 2:
                    pe.wait_ge(pT_ready, h - 1)
                if h == 0:
                    pe.wait_ge(act_emptied, emptied(FILL[("v", 1)])[1])
                r = 64 * (h % 2)
                o = bank[6 + h % 2]
                for a in range(TT):
                    mm = pe.matmul(o[:, a * P:a * P + (a + 1) * P], qT[r:r + 64, h // 2, a * P:(a + 1) * P],
                                   kT[r:r + 64, h // 2, 0:(a + 1) * P], start=True, stop=True,
                                   tile_position=(r, 0))
                mm.then_inc(s_done, 1)

            scores(0)
            scores(1)
            def values(h):
                pe.wait_ge(pT_ready, h + 1)
                if h % 2 == 0 and h >= 2:
                    pe.wait_ge(att_ready, h // 2)
                if h == 0:
                    pe.wait_ge(ada_emptied, 8)
                r = 64 * (h % 2)
                o = bank[3][r:r + 64, 0:T]
                pe.matmul(o, vv[:, 0, h * HD:(h + 1) * HD], pt_m[h % 2][:, 0:T], start=True, stop=False,
                          tile_position=(0, r))
                pe.matmul(o[:, P:T], vv[:, 1, h * HD:(h + 1) * HD], pt_m[h % 2][:, T:3 * P],
                          start=False, stop=True, tile_position=(0, r)).then_inc(pv_done, 1)

            for h in range(HEADS):
                if 0 < h < HEADS - 1:
                    scores(h + 1)
                before = (lambda h=h: values(h - 1)) if h else None
                if h < 6:
                    name = ("ga1", "gs0", "gs1")[h // 2]
                    if h % 2 == 0:
                        arrive(name)
                    features(name, h % 2, 8, hT, before)
                    if h == 0:
                        states_to_outputs(7)
                else:
                    if h == 6:
                        arrive("glu")
                        pe.wait_ge(gelu_out, 1)
                    for b in range(2):
                        features("glu", 2 * (h - 6) + b, 4, uT, None if b else before)
                if h - 1 in ADA_HEAD:
                    if h == 2:
                        pe.wait_ge(bu_read, 8)
                    ada(ADA_HEAD[h - 1])
                pe.wait_ge(probs_ready, h + 1)
                for b in range(3):
                    mm = pe.transpose(bank[6 + h % 2][:, b * P:(b + 1) * P], lg_m[h % 2][:, b * P:(b + 1) * P], ident)
                mm.then_inc(p_turned, 1)
            values(HEADS - 1)
            pe.wait_ge(att_ready, 4)
            arrive("ao")
            for b in range(4):
                features("ao", b, 4, attT)
            pe.wait_ge(glu_ready, 1)
            arrive("so")
            for b in range(4):
                features("so", b, 4, gluT)
            pe.wait_ge(merged_ready, 4)
            arrive("wo0")
            arrive("wo1")
            for a in range(TT):
                for name in ("wo0", "wo1"):
                    tokens(name, a, aoT)

            def turn_h2(a):
                pe.wait_ge(normed, TT + a + 1)
                for n in range(2):
                    if a:
                        pe.wait_ge(rT_ready, n + 1)
                    for k in range(4):
                        mm = pe.transpose(bank[6 + n][:, k * P:(k + 1) * P],
                                          h2[:, a, (4 * n + k) * P:(4 * n + k + 1) * P], ident)
                    mm.then_inc(h_turned, 1)

            def logits(a):
                pe.wait_ge(rT_ready, 2 * a + 2)
                for k in range(KD):
                    pe.matmul(bank[a][:, 0:NE], rT[:, k, a * P:(a + 1) * P], wr[:, k, :], start=k == 0, stop=False)
                pe.matmul(bank[a][:, 0:NE], ones[0:1, :], br[:, :], start=False, stop=True).then_inc(logit_done, 1)

            pe.wait_ge(ada_emptied, len(ADA))
            pe.wait_ge(moe_in, 80)
            turn_h2(0)
            logits(0)
            turn_h2(1)
            logits(1)
            pe.wait_ge(mask_ready, 1)
            pe.matmul(bank[3][:, 0:NE], tri, msk[:, 0, :], start=True, stop=True)
            pe.matmul(bank[3][:, NE:2 * NE], ones, msk[:, 0, :], start=True, stop=False)
            pe.matmul(bank[3][:, NE:2 * NE], tri, msk[:, 1, :], start=False, stop=True)
            pe.matmul(bank[3][:, 2 * NE:3 * NE], ones, msk[:, 0, :], start=True, stop=False)
            pe.matmul(bank[3][:, 2 * NE:3 * NE], ones, msk[:, 1, :], start=False, stop=True).then_inc(rank_done, 1)
            pe.wait_ge(gates_ready, 1)
            for a in range(TT):
                mm = pe.transpose(bank[2][0:NE, a * P:(a + 1) * P], gat[:, a, :], ident)
            mm.then_inc(gates_turned, 1)
            def gather(j, r):
                if r == 0:
                    pe.wait_ge(pick_ready, j + 1)
                else:
                    pe.wait_ge(xe_in, 4 * j + r)
                part = h2_hi if r < 2 else h2_lo
                for m in range(4):
                    k = 4 * (r % 2) + m
                    for a in range(TT):
                        mm = pe.matmul(bank[6 + m // 2][:, (m % 2) * T:(m % 2 + 1) * T],
                                       part[:, a, k * P:(k + 1) * P], pick[:, a, :], start=a == 0, stop=a == TT - 1)
                mm.then_inc(gathered, 1)

            def products(i, hs, k_n, n_n, x_hi, x_lo, k0, outs, start, low_in=None):
                pe.wait_ge(lo_ready[hs % SLOTS], i * USES + (hs // SLOTS + 1))
                hi = w_hi[:, hs % SLOTS, :].rearrange("p (k n) -> p k n", k=k_n)
                lo = w_lo[:, hs % SLOTS, :].rearrange("p (k n) -> p k n", k=k_n)
                for k in range(k_n):
                    for w in (hi, lo):
                        for n in range(n_n):
                            pe.matmul(outs[n], x_hi[:, k0 + k, :], w[:, k, 512 * n:512 * n + 512],
                                      start=start and k == 0 and w is hi, stop=False)
                if low_in is not None:
                    pe.wait_ge(xe_in, low_in)
                for k in range(k_n):
                    for n in range(n_n):
                        mm = pe.matmul(outs[n], x_lo[:, k0 + k, :], hi[:, k, 512 * n:512 * n + 512],
                                       start=False, stop=hs == HALVES - 1 and k == k_n - 1)
                mm.then_inc(w_used, 1)

            def up(i, m, hs, low_in=None):
                s = hs // 2
                rows = slice(m * P, (m + 1) * P)
                products(i, hs, 4, 1, xe_hi[:, :, rows], xe_lo[:, :, rows], 4 * (hs % 2), [bank[s]], hs % 2 == 0, low_in)
                if hs % 2:
                    col = 512 * (s // 2) + FF * (s % 2)
                    pe.matmul(bank[s], sel[:, :], b1_hl[:, col:col + 512], start=False, stop=True).then_inc(up_done, 1)

            def turn_act(i, half):
                pe.wait_ge(act_ready, 2 * i + (half + 1))
                for k in range(4):
                    mm = pe.transpose(bank[half][:, k * P:(k + 1) * P],
                                      act_t[:, half * 512 + k * P:half * 512 + (k + 1) * P], ident)
                mm.then_inc(act_turned, 1)

            def down(i, hs):
                if hs % 2 == 0:
                    pe.wait_ge(aT_ready, 2 * i + (hs // 2 - 3))
                products(i, hs, 2, 2, aT_hi, aT_lo, 2 * (hs - 8), [bank[4], bank[5]], hs == 8)

            def turn_picks(i, e):
                pe.wait_ge(pick_t_ready, i + 2)
                for a in range(TT):
                    pe.matmul(bank[2][:, a * P:(a + 1) * P], pick_t[:, a, :], ident_r[:, :], start=True, stop=True)
                for a in range(TT):
                    mm = pe.matmul(bank[2][:, T:T + 2], pick_t[:, a, :],
                                   gate_hl[:, a, bass.ds(e, 1), :].rearrange("p o g -> p (o g)"),
                                   start=a == 0, stop=a == TT - 1)
                mm.then_inc(pick_turned, 1)

            def combine(i):
                pe.wait_ge(pickT_ready, i + 2)
                pe.wait_ge(ye_ready, i + 2)
                for q in range(4):
                    a, n = q // 2, q % 2
                    for y in (y_hi, y_lo):
                        mm = pe.matmul(bank[(2, 3, 6, 7)[q]], pickT[:, a * P:(a + 1) * P],
                                       y[:, 512 * n:512 * n + 512], start=y is y_hi, stop=y is y_lo)
                    mm.then_inc(comb_done, 1)

            def expert(j, m, before):
                i = j * 2 + m
                if m == 0:
                    pe.wait_ge(xe_in, 4 * j + 2)
                pe.wait_ge(sel_ready, i + 1)
                up(i, m, 0, 4 * j + 4 if m == 0 else None)
                up(i, m, 1)
                up(i, m, 2)
                if before:
                    combine(i - 1)
                up(i, m, 3)
                pe.wait_ge(acc_done, 4 * i + 1)
                up(i, m, 4)
                up(i, m, 5)
                turn_act(i, 0)
                pe.wait_ge(acc_done, 4 * i + 2)
                up(i, m, 6)
                up(i, m, 7)
                pe.wait_ge(acc_done, 4 * i + 4)
                if m == 1:
                    gather(j + 1, 0)
                pe.wait_ge(ye_ready, i + 1)
                down(i, 8)
                if m == 1:
                    gather(j + 1, 1)
                turn_act(i, 1)
                down(i, 9)
                if m == 1:
                    gather(j + 1, 2)
                down(i, 10)
                if m == 1:
                    gather(j + 1, 3)
                turn_picks(i, i)
                down(i, 11)

            def combine_last(j, m):
                pe.wait_ge(xe_in, 4 * j + 4 + 4 * m)
                combine(j * 2 + m)

            pe.wait_ge(rT_ready, 4)
            pe.wait_ge(h2_hi_ready, TT)
            for r in range(4):
                if r == 2:
                    pe.wait_ge(h2_ready, TT)
                gather(0, r)
                if r == 0:
                    pe.wait_ge(gT_ready, 1)
                for q in ((2,), (3,), (0, 1), ())[r]:
                    a, n = q // 2, q % 2
                    pe.matmul(bank[(4, 5, 0, 1)[q]], gT[:, a * P:(a + 1) * P], b2all[:, 512 * n:512 * n + 512],
                              start=True, stop=True).then_inc(b2_done, 1)
            pe.wait_ge(route_ready, 1)
            turn_picks(-1, 0)
            pe.wait_ge(b1_ready, 1)
            pe.wait_ge(acc_init, 2)
            with pe.Fori(0, NE // 2) as j:
                expert(j, 0, True)
                expert(j, 1, True)
            combine_last(NE // 2 - 1, 1)
            pe.wait_ge(route_ready, 1)
            more = pe.value_load(flag[0:1, 0:1], min_val=0, max_val=1)
            with pe.If(more > 0):
                with pe.Fori(NE // 2, NE) as j:
                    for m in range(2):
                        expert(j, m, False)
                        combine_last(j, m)

        @block.scalar
        def _(act):
            for r, b in enumerate((ssm_b_re, ssm_b_im)):
                act.dma_start(b_in[:, r, :, :], b[0].rearrange("(s a) p c -> (a p) s c", a=2)).then_inc(param_in, 16)
            act.dma_start(hot, const[0:BUCKETS + 1, C_HOT:C_N]).then_inc(hot_in, 16)
            for r, cc in enumerate((ssm_c_re, ssm_c_im)):
                act.dma_start(c_in[:, r, :, :], cc[0].rearrange("(j g) c p -> (g c) j p", j=4)).then_inc(param_in, 16)
            act.dma_start(b_rows, b_ada.rearrange("o (r n) -> (o r) n", n=512)).then_inc(b_rows_in, 16)
            act.dma_start(row_a[:, :], broadcast(g_pre_mix, 0, D)).then_inc(g_pre_in, 16)
            act.wait_ge(vcol_ready, 1)
            act.activation(m4[:, 0:8], cond_c, ACT.Tanh, scale=0.5).then_inc(dt_ready, 1)
            act.activation(ldt, ldt, ACT.Exp).then_inc(dt_ready, 1)
            act.wait_ge(theta_ready, 1)
            act.activation(rho, rho, ACT.Exp).then_inc(sine_ready, 1)
            act.wait_ge(theta_ready, 2)
            act.activation(es, theta, ACT.Sin).then_inc(sine_ready, 1)
            act.activation(ec, theta, ACT.Sin, scale=0.5).then_inc(sine_ready, 1)
            act.wait_ge(bline_done, 1)
            act.wait_ge(vrow_turned, 1)
            act.activation(bline, bank[6][0:HEADS, 0:N_HOT], ACT.Copy).then_inc(bline_ready, 1)

            act.wait_ge(x_in, 16 * TT)
            for n in range(TT):
                act.activation(junk, xs[:, n, :], ACT.Square, accum_out=ss[:, n:n + 1]).then_inc(squares, 1)
                act.wait_ge(squares, n + 1)
            for m, dst in enumerate((BT, CT)):
                act.wait_ge(bc_turned, m + 1)
                for r in range(2):
                    last = act.activation(dst[:, r, :, :].rearrange("p j s -> p (j s)"), bank[2 * m + r], ACT.Copy)
                last.then_inc(bc_ready, 1)

            for g in range(4):
                act.wait_ge(h_turned, g + 1)
                act.activation(hT[:, 2 * g:2 * g + 2, :].rearrange("p k t -> p (k t)"), bank[6 + g % 2][:, :],
                               ACT.Copy).then_inc(hT_ready, 1)

            def empty(name, b, dst, func=ACT.Copy, scale=1.0):
                f = FILL[(name, b)]
                act.wait_ge(fill_done, f + 1)
                act.activation(dst, bank[4 + f % 2][:, :], func, scale=scale).then_inc(act_emptied, 1)

            def two(view, b):
                return view[:, 2 * b:2 * b + 2, :].rearrange("p k t -> p (k t)")

            for b in range(2):
                empty("u", b, two(uT, b))
            for b in range(2):
                empty("q", b, two(qT, b))
            for b in range(2):
                empty("k", b, two(kT, b))
            for b in range(2):
                empty("v", b, vv[:, b, :])
            for b in range(2):
                empty("ga0", b, two(ga_t, b), ACT.Tanh, 0.5)

            def pair_out(j):
                act.wait_ge(pv_done, 2 * j + 2)
                act.activation(attT[:, j, :], bank[3][:, 0:T], ACT.Copy).then_inc(att_ready, 1)

            for h in range(HEADS):
                act.wait_ge(max_ready, h + 1)
                lo = lg_m[h % 2]
                act.activation(lo[:, 0:P], lo[:, 0:P], ACT.Exp, bias=mx[:, 0:1], accum_out=sums[:, 0:1]).then_inc(exp_done, 1)
                act.activation(lo[:, P:3 * P], lo[:, P:3 * P], ACT.Exp, bias=mx[:, 1:2], accum_out=sums[:, 1:2]).then_inc(exp_done, 1)
                if h < 6:
                    name = ("ga1", "gs0", "gs1")[h // 2]
                    dst = two(ga_t, 2 + h) if h < 2 else two(gs_t, h - 2)
                    empty(name, h % 2, dst, ACT.Tanh, 0.5)
                else:
                    if h == 6:
                        act.wait_ge(gelu_out, 1)
                    for b in range(2):
                        if h == 6:
                            empty("glu", b, gv[:, 512 * b:512 * b + 512])
                        else:
                            empty("glu", 2 + b, gt_[:, 512 * b:512 * b + 512], ACT.Tanh, 0.25)
                if h % 2 == 0 and h:
                    pair_out(h // 2 - 1)
                act.wait_ge(p_turned, h + 1)
                act.activation(pt_m[h % 2], bank[6 + h % 2][:, 0:3 * P], ACT.Copy).then_inc(pT_ready, 1)
                if h == 0:
                    act.wait_ge(gelu_in, 1)
                    act.activation(gt_, gt_, ACT.Tanh, scale=GELU_C).then_inc(gelu_th, 1)
            pair_out(HEADS // 2 - 1)
            for b in range(4):
                empty("ao", b, two(aoT, b))
            def square_x1(n):
                act.wait_ge(x1_ready, n + 1)
                act.activation(junk, xs[:, n, :], ACT.Square, accum_out=ss[:, n:n + 1]).then_inc(x1_squares, 1)
                act.wait_ge(x1_squares, n + 1)

            for a in range(TT):
                for n in range(2):
                    f = FILL[(f"wo{n}", a)]
                    act.wait_ge(fill_done, f + 1)
                    sq = act.activation(junk[:, 512 * n:512 * n + 512], bank[4 + f % 2], ACT.Square,
                                        accum_out=ss_y[:, 2 * a + n:2 * a + n + 1])
                    if n:
                        sq.then_inc(squares, 1)
                    empty(f"wo{n}", a, y_sb[:, a, 512 * n:512 * n + 512])
                    if a == 1 and n == 0:
                        act.wait_ge(act_emptied, emptied(f)[1])
                        square_x1(0)
            def turned(a):
                for n in range(2):
                    act.wait_ge(h_turned, 4 + 2 * a + n + 1)
                    act.activation(rT[:, 4 * n:4 * n + 4, a * P:(a + 1) * P],
                                   bank[6 + n].rearrange("p (k t) -> p k t", k=4), ACT.Copy).then_inc(rT_ready, 1)

            def rows_high(a):
                act.activation(h2_hi[:, a, :], h2[:, a, :], ACT.Copy).then_inc(h2_hi_ready, 1)

            turned(0)
            act.wait_ge(act_emptied, emptied(FILL[("wo1", 1)])[1])
            square_x1(1)
            act.wait_ge(x1_ready, TT)
            rows_high(0)
            turned(1)
            rows_high(1)
            act.wait_ge(moe_in, 80)
            act.wait_ge(logit_done, 2)
            act.activation(b1_hl[:, :], b1_raw, ACT.Copy).then_inc(b1_hi_ready, 1)
            for a in range(TT):
                act.wait_ge(top_ready, a + 1)
                act.activation(topx[:, a, 0:TOPK], top[:, a, 0:TOPK], ACT.Exp, bias=ms2[:, a:a + 1],
                               accum_out=sums[:, a:a + 1]).then_inc(topexp, 1)
            act.wait_ge(gates_turned, 1)
            act.activation(gT[:, :], bank[2][0:NE, 0:T], ACT.Copy).then_inc(gT_ready, 1)
            def high(i, hs):
                act.wait_ge(raw_in[hs % SLOTS], i * (16 * USES) + (16 * (hs // SLOTS) + 16))
                act.wait_ge(w_used, i * HALVES + (hs + 1))
                act.activation(w_hi[:, hs % SLOTS, :], w_raw[:, hs % SLOTS, :], ACT.Copy).then_inc(hi_ready, 1)

            def rows_in(j, r):
                act.wait_ge(gathered, 4 * j + (r + 1))
                part = xe_hi if r < 2 else xe_lo
                for n in range(2):
                    k = 4 * (r % 2) + 2 * n
                    last = act.activation(part[:, k:k + 2, :].rearrange("p k s -> p (k s)"), bank[6 + n], ACT.Copy)
                last.then_inc(xe_in, 1)

            def gate_tanh(i, half):
                act.wait_ge(g_ready, 2 * i + (half + 1))
                act.activation(th_c, g_c, ACT.Tanh, scale=ALPHA / 2).then_inc(gate_th, 1)

            def act_high(i, half):
                act.wait_ge(act_turned, 2 * i + (half + 1))
                act.activation(aT_hi[:, 4 * half:4 * half + 4, :].rearrange("p k s -> p (k s)"), bank[half], ACT.Copy
                               ).then_inc(aT_hi_ready, 1)

            def picks_in(i):
                act.wait_ge(pick_turned, i + 2)
                act.activation(two_gates, bank[2][:, T:T + 2], ACT.Copy, accum_out=gate_s)
                act.activation(pickT[:, :], bank[2][:, 0:T], ACT.Copy).then_inc(pickT_ready, 1)

            def out_high(i):
                act.wait_ge(w_used, i * HALVES + (HALVES + SLOTS))
                act.wait_ge(pickT_ready, i + 2)
                for n in range(2):
                    act.activation(y_hi[:, 512 * n:512 * n + 512], bank[4 + n], ACT.Copy, scale=gate_s
                                   ).then_inc(y_hi_ready, 1)

            def expert(j, m, before):
                i = j * 2 + m
                high(i, 0)
                if before and m == 0:
                    rows_in(j, 2)
                high(i, 1)
                if before:
                    if m == 0:
                        rows_in(j, 3)
                    picks_in(i - 1)
                high(i, 2)
                if before:
                    out_high(i - 1)
                for hs in range(3, 8):
                    high(i, hs)
                gate_tanh(i, 0)
                high(i, 8)
                high(i, 9)
                act_high(i, 0)
                high(i, 10)
                gate_tanh(i, 1)
                if m == 1:
                    rows_in(j + 1, 0)
                high(i, 11)
                if m == 1:
                    rows_in(j + 1, 1)
                act_high(i, 1)

            def expert_last(j, m):
                if m == 1:
                    rows_in(j + 1, 2)
                    rows_in(j + 1, 3)
                picks_in(j * 2 + m)
                out_high(j * 2 + m)

            act.sem_inc(w_used, SLOTS)
            act.wait_ge(h2_ready, TT)
            for m, q in enumerate((2, 3, 0, 1)):
                if m < 2:
                    rows_in(0, m)
                act.wait_ge(b2_done, m + 1)
                act.activation(acc[:, q // 2, 512 * (q % 2):512 * (q % 2) + 512], bank[(4, 5, 0, 1)[q]], ACT.Copy
                               ).then_inc(acc_init, 1)
            act.wait_ge(b1_ready, 1)
            with act.Fori(0, NE // 2) as j:
                expert(j, 0, True)
                expert(j, 1, True)
            expert_last(NE // 2 - 1, 1)
            act.wait_ge(route_ready, 1)
            more = act.value_load(flag[0:1, 0:1], min_val=0, max_val=1)
            with act.If(more > 0):
                with act.Fori(NE // 2, NE) as j:
                    for m in range(2):
                        expert(j, m, False)
                        expert_last(j, m)
            act.wait_ge(normed, 3 * TT)
            for n in range(TT):
                act.activation(act_t, acc[:, n, :], ACT.Square, accum_out=ss[:, n:n + 1]).then_inc(squares, 1)
                act.wait_ge(squares, 2 * TT + n + 1)

        @block.vector
        def _(dve):
            V = Steps(dve, v_step)
            tt, ts, stt = dve.tensor_tensor, dve.tensor_scalar, dve.scalar_tensor_tensor

            def chain(ins):
                V.do(ins)
                V.settle()

            dve.wait_ge(vec_in, 80)
            dve.tensor_copy(vrow[0:ST, :].rearrange("s (a p) -> s a p", a=2),
                            ldt_in.rearrange("s (a o) -> s a o", o=1).broadcast_to([ST, 2, GP])).then_inc(vrow_ready, 1)
            dve.wait_ge(vrow_turned, 1)
            dve.tensor_copy(vcol, bank[3][:, 0:60]).then_inc(vcol_ready, 1)
            dve.wait_ge(vcol_ready, 1)
            dve.wait_ge(dt_ready, 2)
            chain(stt(cond_c, m4[:, 0:8], 1.0, cond_c, ALU.add, ALU.mult))
            chain(ts(cond_c, cond_c, 0.5, None, ALU.mult))
            for k in range(KD // 2):
                last = ts(cond_b[:, k, :], ones, cond_c[:, KD // 2 + k:KD // 2 + k + 1], None, ALU.mult)
            last.then_inc(cond_ready, 1)
            V.do(ts(lam, are, -1e-4, None, ALU.min))
            chain(tt(theta, aim, ldt, ALU.mult))
            tt(rho, lam, ldt, ALU.mult).then_inc(theta_ready, 1)
            chain(ts(m1, theta, 1.0 / (2 * math.pi), ROUND, ALU.mult, ALU.add))
            chain(ts(m1, m1, -ROUND, None, ALU.add))
            rest = 2 * math.pi - 6.28125
            c2 = float(np.float32(np.round(rest * 2 ** 22) / 2 ** 22))
            for cc in (6.28125, c2, rest - c2):
                chain(stt(theta, m1, -cc, theta, ALU.mult, ALU.add))
            ts(theta, theta, 3.1415925, -3.1415925, ALU.min, ALU.max).then_inc(theta_ready, 1)
            dve.wait_ge(sine_ready, 3)
            chain(tt(ec, ec, ec, ALU.mult))
            ts(ec, ec, -2.0, 1.0, ALU.mult, ALU.add).then_inc(trig_ready, 1)
            dve.wait_ge(trig_ready, 1)
            chain(tt(m1, rho, ec, ALU.mult))
            chain(tt(m2, rho, es, ALU.mult))
            chain(tt(m3, lam, lam, ALU.mult))
            chain(tt(m4, aim, aim, ALU.mult))
            chain(ts(m1, m1, -1.0, None, ALU.add))
            chain(tt(m3, m3, m4, ALU.add))
            chain(dve.reciprocal(m3, m3))
            chain(tt(zre, m1, lam, ALU.mult))
            chain(tt(m4, m2, aim, ALU.mult))
            chain(tt(zre, zre, m4, ALU.add))
            chain(tt(zim, m2, lam, ALU.mult))
            chain(tt(m4, m1, aim, ALU.mult))
            chain(tt(zim, zim, m4, ALU.subtract))
            chain(tt(zre, zre, m3, ALU.mult))
            chain(tt(zim, zim, m3, ALU.mult))
            dve.memset(b_bar, 0.0).then_inc(v_step, 1)
            V.n += 1
            dve.wait_ge(param_in, 64)
            V.settle()

            def over_c(v):
                return v.rearrange("p (s o) -> p s o", o=1).broadcast_to([P, ST, GC])

            for r, (a, b, op) in enumerate(((0, 1, ALU.subtract), (1, 0, ALU.add))):
                V.do(tt(b_tmp, b_in[:, a, :, :], over_c(zre), ALU.mult))
                chain(tt(b_tmp2, b_in[:, b, :, :], over_c(zim), ALU.mult))
                for g in range(2):
                    rows = slice(64 * g, 64 * g + 64)
                    last = tt(b_bar[rows, r, :, GC * g:GC * g + GC], b_tmp[rows], b_tmp2[rows], op)
                    if r == 0 or g == 0:
                        chain(last)
            last.then_inc(bc_padded, 1)
            for r in range(2):
                for g in range(2):
                    last = ts(c_pad[:, r, :, 64 * g:64 * g + 64], c_in[:, r, :, :], cst[:, C_EVEN + g:C_EVEN + g + 1],
                              1.0 if r == 0 else -1.0, ALU.mult, ALU.mult)
            last.then_inc(bc_padded, 1)

            def sum_ada(n):
                name = ADA[n]
                m = MIX.index(name)
                acc_n = ada_acc[:, n % 2, :]
                w = slot(m % MIX_SLOTS, 8)
                dve.wait_ge(slot_in[m % MIX_SLOTS], 16 * (m // MIX_SLOTS + 1))
                if n >= 2:
                    dve.wait_ge(ada_done, n - 1)
                chain(ts(acc_n, w[:, 0, :], cond_c[:, 0:1], None, ALU.mult))
                for k in range(1, KD // 2 if n < SPLIT_ADA else KD):
                    chain(stt(acc_n, w[:, k, :], cond_c[:, k:k + 1], acc_n, ALU.mult, ALU.add))
                if n == 0:
                    dve.wait_ge(b_rows_in, 16)
                rows, r = len(ADA), ADA_ROW[name]
                stt(acc_n[0:rows], b_rows, ident[0:rows, r:r + 1], acc_n[0:rows], ALU.mult, ALU.add).then_inc(ada_summed, 1)

            def empty_ada(n):
                name = ADA[n]
                src = bank[ADA_BANK[n]]
                dve.wait_ge(ada_done, n + 1)
                v = slice(512 * (name[3] == "b"), 512 * (name[3] == "b") + 512)
                if name[:2] == "sh":
                    dve.tensor_copy(row_b[:, v], src).then_inc(ada_emptied, 1)
                    return
                row, g_in = {"sc1": (row_a, g_pre_in), "gt1": (row_g, g_mix_in), "sc2": (row_a, g_ffn_in),
                             "gt2": (row_g2, g_post_in)}[name[:3]]
                dve.wait_ge(g_in, 16)
                stt(row[:, v], src, 1.0 if name[:2] == "sc" else 0.0, row[:, v], ALU.add, ALU.mult).then_inc(ada_emptied, 1)

            sum_ada(0)
            sum_ada(1)
            empty_ada(0)
            sum_ada(2)
            empty_ada(1)
            dve.wait_ge(rstd_ready, 2)
            dve.wait_ge(ada_emptied, 2)
            for a in range(TT):
                last = stt(xs[:, a, :], xs[:, a, :], rstd[:, a:a + 1], row_a[:, :], ALU.mult, ALU.mult)
            last.then_inc(scaled, 1)
            dve.wait_ge(scaled, 1)

            def shift(half):
                dve.wait_ge(ada_done, 3 + half)
                v = slice(512 * half, 512 * half + 512)
                V.do(tt(xs[:, 0, v], xs[:, 0, v], bank[4 + half], ALU.add))
                tt(xs[:, 1, v], xs[:, 1, v], bank[4 + half], ALU.add).then_inc(normed, 1)

            shift(0)
            sum_ada(3)
            shift(1)
            dve.wait_ge(normed, 2)
            dve.sem_inc(ada_emptied, 2)
            dve.wait_ge(tables_begun, 1)
            for n in (5, 6):
                level(dve, V, 1 << n)
            unit(dve, V)
            dve.sem_inc(angle_ready, 1)
            double(dve, V, T // 2, slice(0, ST // 2))
            V.settle()
            dve.sem_inc(tables_ready, 1)

            def skip(j):
                dve.wait_ge(y_done, 2 * j + 2)
                stt(uT[:, j, :], uT[:, j, :], dcol[:, j:j + 1], bank[2][:, 0:T],
                    ALU.mult, ALU.add).then_inc(y_read, 1)

            tp3 = by_tile(tp)
            for n in range(8):
                tc = tab_c[:, 2 * n:2 * n + 2, :]
                tsn = tab_s[:, 2 * n:2 * n + 2, :]
                zr, zi = z_re[n % 2], z_im[n % 2]
                zr3, zi3 = by_tile(zr), by_tile(zi)
                dve.wait_ge(bu_done, n + 1)
                if n == 4:
                    dve.wait_ge(tables_shared, 1)
                if n >= 2:
                    dve.wait_ge(x_ready, n - 1)
                V.do(tt(zr3, bu_re, tc, ALU.mult))
                V.do(tt(zi3, bu_im, tc, ALU.mult))
                chain(tt(tp3, bu_im, tsn, ALU.mult))
                chain(tt(zr3, zr3, tp3, ALU.add))
                tt(tp3, bu_re, tsn, ALU.mult).then_inc(bu_read, 1)
                dve.wait_ge(bu_read, n + 1)
                chain(tt(zi3, zi3, tp3, ALU.subtract))
                if n >= 3 and n % 2:
                    skip((n - 3) // 2)
                for m in range(2):
                    decay = rho[:, 2 * n + m:2 * n + m + 1].broadcast_to([P, T])
                    for z in (zr, zi):
                        v = z[:, m * T:(m + 1) * T]
                        last = dve.tensor_tensor_scan(v, decay, v, 0.0, ALU.mult, ALU.add)
                        if m == 0 or z is zr:
                            V.do(last)
                last.then_inc(z_ready, 1)
                dve.wait_ge(z_ready, n + 1)
                if n % 2 == 0:
                    sum_ada(4 + n // 2)
                elif n < 7:
                    empty_ada(4 + n // 2)

            yv = uT.rearrange("p j t -> p (j t)")

            def gelu():
                skip(3)
                dve.wait_ge(y_read, 4)
                chain(tt(gt_, yv, yv, ALU.mult))
                chain(ts(gt_, gt_, 0.044715, 1.0, ALU.mult, ALU.add))
                tt(gt_, gt_, yv, ALU.mult).then_inc(gelu_in, 1)

            def head(h):
                dve.wait_ge(s_done, h + 1)
                dve.wait_ge(bias_in[h % 2], 32 * (h // 2 + 1))
                if h >= 2:
                    dve.wait_ge(p_turned, h - 1)
                lo = lg_m[h % 2]
                stt(lo, bank[6 + h % 2][:, 0:3 * P], HD ** -0.5, bias_m[h % 2], ALU.mult, ALU.add).then_inc(logits_ready, 1)
                dve.wait_ge(logits_ready, h + 1)
                V.do(dve.reduce_max(m1[:, 0:1], lo[:, 0:P], AX))
                chain(dve.reduce_max(m1[:, 1:2], lo[:, P:3 * P], AX))
                ts(mx, m1[:, 0:2], -1.0, None, ALU.mult).then_inc(max_ready, 1)
                dve.wait_ge(exp_done, 2 * h + 2)
                chain(dve.reciprocal(m2[:, 0:2], sums))
                V.do(ts(lo[:, 0:P], lo[:, 0:P], m2[:, 0:1], None, ALU.mult))
                ts(lo[:, P:3 * P], lo[:, P:3 * P], m2[:, 1:2], None, ALU.mult).then_inc(probs_ready, 1)
                V.settle()

            for h in range(HEADS):
                head(h)
                if h == 0:
                    empty_ada(7)
                    gelu()
                if h in ADA_HEAD:
                    sum_ada(ADA_HEAD[h])
                if h == 1:
                    dve.wait_ge(gelu_th, 1)
                    stt(yv, gt_, 1.0, yv, ALU.add, ALU.mult).then_inc(gelu_out, 1)
                if h - 1 in ADA_HEAD:
                    empty_ada(ADA_HEAD[h - 1])

            dve.wait_ge(act_emptied, emptied(FILL[("glu", 3)])[1])
            stt(gv, gt_, 1.0, gv, ALU.add, ALU.mult).then_inc(glu_ready, 1)
            dve.wait_ge(act_emptied, emptied(FILL[("ao", 3)])[1])
            chain(stt(ao_flat, ta_flat, 1.0, ao_flat, ALU.add, ALU.mult))
            for b in range(4):
                f = FILL[("so", b)]
                v = slice(512 * b, 512 * b + 512)
                dve.wait_ge(fill_done, f + 1)
                stt(gs_flat[:, v], gs_flat[:, v], 1.0, bank[4 + f % 2][:, :], ALU.add, ALU.mult).then_inc(dve_emptied, 1)
                dve.wait_ge(dve_emptied, emptied(f)[1])
                stt(ao_flat[:, v], gs_flat[:, v], 0.25, ao_flat[:, v], ALU.mult, ALU.add).then_inc(merged_ready, 1)

            dve.wait_ge(x_again, 16 * TT)
            dve.wait_ge(ada_emptied, len(ADA))
            for a in range(TT):
                dve.wait_ge(rstd_ready, TT + 2 * a + 1)
                dve.wait_ge(act_emptied, emptied(FILL[("wo1", a)])[1])
                chain(stt(y_sb[:, a, :], y_sb[:, a, :], rstd[:, a:a + 1], row_g[:, :], ALU.mult, ALU.mult))
                tt(xs[:, a, :], xs[:, a, :], y_sb[:, a, :], ALU.add).then_inc(x1_ready, 1)
                dve.wait_ge(rstd_ready, TT + 2 * a + 2)
                chain(stt(h2[:, a, :], xs[:, a, :], rstd[:, a:a + 1], row_a[:, :], ALU.mult, ALU.mult))
                tt(h2[:, a, :], h2[:, a, :], row_b[:, :], ALU.add).then_inc(normed, 1)
            def pair_rows(j):
                for m in range(2):
                    for a in range(TT):
                        last = ts(pick[:, a, m * P:(m + 1) * P], iota, row_of[:, a, bass.ds(j * 2 + m, 1)], None,
                                  ALU.is_equal)
                last.then_inc(pick_ready, 1)

            def largest(a):
                dve.wait_ge(logit_done, a + 1)
                chain(dve.tensor_copy(lgr[:, a, :], bank[a][:, 0:NE]))
                chain(dve.max(top[:, a, :], lgr[:, a, :]))
                V.do(dve.max_index(idx[:, a, :], top[:, a, :], lgr[:, a, :]))
                ts(ms2[:, a:a + 1], top[:, a, 0:1], -1.0, None, ALU.mult).then_inc(top_ready, 1)

            def rows_low(a):
                dve.wait_ge(h2_hi_ready, a + 1)
                tt(h2_lo[:, a, :], h2[:, a, :], h2_hi[:, a, :].bitcast(F32), ALU.subtract).then_inc(h2_ready, 1)

            largest(0)
            rows_low(0)
            rows_low(1)
            V.do(dve.memset(row_of, NOWHERE))
            for a in range(TT):
                V.do(ts(pick_t[:, a, :], ones, 0.0, None, ALU.mult))
            V.do(dve.tensor_copy(ident_r[:, :], ident))
            V.do(tt(sel_table, ident[0:2 * NE, 0:NE + 1], ident[0:2 * NE, NE:2 * NE + 1], ALU.add))
            V.settle()
            dve.sem_inc(pick_t_ready, 1)
            largest(1)
            dve.wait_ge(top_ready, 2)
            V.settle()
            chain(dve.tensor_copy(idf.rearrange("p a e -> p (a e)"), idx[:, :, :].rearrange("p a e -> p (a e)")))

            def by_choice(v):
                return v[:, :, 0:TOPK].rearrange("p a (j o) -> p a j o", o=1).broadcast_to([P, TT, TOPK, NE])

            for a in range(TT):
                V.do(tt(chosen[:, a], iota[:, 0:NE].rearrange("p (o e) -> p o e", o=1).broadcast_to([P, TOPK, NE]),
                        by_choice(idf)[:, a], ALU.is_equal))
            V.settle()
            dve.tensor_reduce(msk, chosen.rearrange("p a j e -> p a e j"), AX, ALU.add).then_inc(mask_ready, 1)
            dve.wait_ge(mask_ready, 1)
            for a in range(TT):
                V.do(ts(row_of[:, a, 0:NE], msk[:, a, :], -NOWHERE, NOWHERE, ALU.mult, ALU.add))
            dve.wait_ge(topexp, 2)
            chain(dve.reciprocal(m2[:, 0:2], sums))
            for a in range(TT):
                V.do(ts(topx[:, a, 0:TOPK], topx[:, a, 0:TOPK], m2[:, a:a + 1], None, ALU.mult))
            V.settle()
            for a in range(TT):
                V.do(tt(weighed[:, a], chosen[:, a], by_choice(topx)[:, a], ALU.mult))
            V.settle()
            dve.tensor_reduce(gat, weighed.rearrange("p a j e -> p a e j"), AX, ALU.add).then_inc(gates_ready, 1)
            dve.wait_ge(gates_ready, 1)
            dve.wait_ge(rank_done, 1)
            for a in range(TT):
                V.do(tt(row_of[:, a, 0:NE], row_of[:, a, 0:NE], bank[3][:, a * NE:(a + 1) * NE], ALU.add))
            V.settle()
            pair_rows(0)
            dve.wait_ge(gates_turned, 1)
            for a in range(TT):
                V.do(ts(gat[:, a, :], gat[:, a, :], 0.5, None, ALU.mult))
            V.settle()
            for a in range(TT):
                for h in range(2):
                    V.do(dve.tensor_copy(gate_hl[:, a, h * NE:(h + 1) * NE, 0], gat[:, a, :]))
            V.settle()
            for a in range(TT):
                for h in range(2):
                    V.do(tt(gate_hl[:, a, h * NE:(h + 1) * NE, 1], gat[:, a, :],
                            gate_hl[:, a, h * NE:(h + 1) * NE, 0].bitcast(F32), ALU.subtract))
                V.do(ts(row_of[:, a, NE:2 * NE], row_of[:, a, 0:NE], -float(CAP), None, ALU.add))
            chain(dve.reduce_max(m1[:, 0:1], bank[3][:, 2 * NE:3 * NE], AX))
            ts(flag[:, 0:1], m1[:, 0:1], float(CAP), None, ALU.is_gt).then_inc(route_ready, 1)

            def low_part(i, hs):
                dve.wait_ge(hi_ready, i * HALVES + (hs + 1))
                tt(w_lo[:, hs % SLOTS, :], w_raw[:, hs % SLOTS, :], w_hi[:, hs % SLOTS, :].bitcast(F32), ALU.subtract
                   ).then_inc(lo_ready[hs % SLOTS], 1)

            def expert_rows(i):
                for a in range(TT):
                    last = ts(pick_t[:, a, :], iota, row_of[:, a, bass.ds(i, 1)], None, ALU.is_equal)
                last.then_inc(pick_t_ready, 1)

            def clamp(i, half):
                dve.wait_ge(up_done, 4 * i + (2 * half + 2))
                ts(g_c, bank[2 * half][:, :], LIMIT, None, ALU.min).then_inc(g_ready, 1)
                V.do(ts(u_c, bank[2 * half + 1][:, :], LIMIT, -LIMIT, ALU.min, ALU.max))

            def times_gate(i, half):
                dve.wait_ge(g_ready, 2 * i + (half + 1))
                V.settle()
                V.do(stt(u_c, u_c, 1.0, g_c, ALU.add, ALU.mult))

            def swish(i, half):
                dve.wait_ge(gate_th, 2 * i + (half + 1))
                V.settle()
                stt(act_t[:, 512 * half:512 * half + 512], th_c, 1.0, u_c, ALU.add, ALU.mult).then_inc(act_ready, 1)

            def act_low(i, half):
                dve.wait_ge(aT_hi_ready, 2 * i + (half + 1))
                v = aT_lo[:, 4 * half:4 * half + 4, :].rearrange("p k s -> p (k s)")
                hi = aT_hi[:, 4 * half:4 * half + 4, :].rearrange("p k s -> p (k s)")
                tt(v, bank[half], hi.bitcast(F32), ALU.subtract).then_inc(aT_ready, 1)

            def out_low(i):
                for n in range(2):
                    v = slice(512 * n, 512 * n + 512)
                    dve.wait_ge(y_hi_ready, 2 * i + (n + 3))
                    last = stt(y_lo[:, v], bank[4 + n], gate_s, y_hi[:, v].bitcast(F32), ALU.mult, ALU.subtract)
                last.then_inc(ye_ready, 1)

            def add_up(i, q):
                v = acc[:, q // 2, 512 * (q % 2):512 * (q % 2) + 512]
                dve.wait_ge(comb_done, 4 * i + (q + 5))
                tt(v, v, bank[(2, 3, 6, 7)[q]][:, :], ALU.add).then_inc(acc_done, 1)

            PER = 4

            def expert(j, j0, m, before):
                i = j * 2 + m
                e = (j - j0) * 2 + m if j0 else i
                V.at = start + i * PER
                V.n = 0
                dve.tensor_copy(sel[:, :], sel_table[:, bass.ds(e, 1)].broadcast_to([2 * NE, P])).then_inc(sel_ready, 1)
                low_part(i, 0)
                low_part(i, 1)
                if m == 0:
                    dve.wait_ge(gathered, 4 * j + 4)
                    pair_rows(j + 1)
                low_part(i, 2)
                if before:
                    out_low(i - 1)
                dve.wait_ge(pickT_ready, i + 1)
                expert_rows(i)
                low_part(i, 4)
                if before:
                    add_up(i - 1, 0)
                    add_up(i - 1, 1)
                low_part(i, 5)
                if before:
                    add_up(i - 1, 2)
                    add_up(i - 1, 3)
                clamp(i, 0)
                low_part(i, 6)
                times_gate(i, 0)
                swish(i, 0)
                low_part(i, 8)
                act_low(i, 0)
                low_part(i, 9)
                dve.wait_ge(act_ready, 2 * i + 1)
                clamp(i, 1)
                times_gate(i, 1)
                swish(i, 1)
                low_part(i, 10)
                act_low(i, 1)
                dve.wait_ge(act_ready, 2 * i + 2)
                assert V.n == PER, V.n

            def expert_last(i):
                out_low(i)
                for q in range(4):
                    add_up(i, q)

            dve.wait_ge(acc_init, 4)
            start = V.n
            with dve.Fori(0, NE // 2) as j:
                expert(j, 0, 0, True)
                expert(j, 0, 1, True)
            expert_last(NE - 1)
            dve.wait_ge(route_ready, 1)
            more = dve.value_load(flag[0:1, 0:1], min_val=0, max_val=1)
            with dve.If(more > 0):
                with dve.Fori(NE // 2, NE) as j:
                    for m in range(2):
                        expert(j, NE // 2, m, False)
                        expert_last(j * 2 + m)
            dve.drain()
            dve.sem_inc(normed, TT)
            for a in range(TT):
                dve.wait_ge(rstd_ready, 3 * TT + a + 1)
                stt(acc[:, a, :], acc[:, a, :], rstd[:, a:a + 1], row_g2, ALU.mult, ALU.mult).then_inc(scaled, 1)
                dve.wait_ge(scaled, 2 + a)
                tt(xs[:, a, :], xs[:, a, :], acc[:, a, :], ALU.add).then_inc(out_ready, 1)


_INS = ["x", "c", "rel_bias", "w_ada", "b_ada", "g_pre_mix", "g_post_mix", "g_pre_ffn", "g_post_ffn", "w_in",
        "ssm_a_re", "ssm_a_im", "ssm_log_dt", "ssm_b_re", "ssm_b_im", "ssm_c_re", "ssm_c_im", "ssm_d", "w_glu",
        "w_ssm_out", "w_att_out", "w_out", "w_router", "b_router", "w_exp_in", "b_exp_in", "w_exp_out", "b_exp_out"]


def kernel(**inputs):
    import concourse.bacc as _bacc
    from concourse.bass_utils import run_bass_kernel_spmd as _run

    nc = _bacc.Bacc("TRN2", target_bir_lowering=False, num_devices=1)
    arrays, args = {}, []
    for name in _INS:
        a = np.ascontiguousarray(inputs[name])
        arrays[f"in_{name}"] = a
        args.append(nc.dram_tensor(f"in_{name}", a.shape, mybir.dt.from_np(a.dtype), kind="ExternalInput").ap())
    arrays["in_const"] = constants()
    args.append(nc.dram_tensor("in_const", (P, C_N), F32, kind="ExternalInput").ap())
    args.append(nc.dram_tensor("bias_line", (HEADS, N_HOT), F32, kind="Internal").ap())
    args.append(nc.dram_tensor("bias_rows", (HEADS, P, 512), F32, kind="Internal").ap())
    args.append(nc.dram_tensor("out_0", (1, T, D), F32, kind="ExternalOutput").ap())
    build(nc, *args)
    r = _run(nc, [arrays], core_ids=[0])
    return r.results[0]["out_0"]
```
